# Optimizing a Trainium2 kernel written in Bass

```python
import jax, jax.numpy as jnp
from jax import lax
import numpy as np

D_MODEL = 1024
BATCH = 1
SEQ = 1024
DEPTH = 1
DEC_BATCH = 1
DEC_SEQ = 256
PAST_LEN = 128

CHUNK = 128
A_WIDTH = 1024
A_GROUPS = 8
A_GROUP_DIM = A_WIDTH // A_GROUPS
N_HEADS = 8
QK_NOPE_DIM = 128
QK_ROPE_DIM = 64
QK_HEAD_DIM = QK_NOPE_DIM + QK_ROPE_DIM
V_HEAD_DIM = 128
Q_LORA_RANK = 256
KV_LORA_RANK = 128
ROPE_THETA = 10000.0
Q_BLOCK = 128
N_EXPERTS = 16
EXPERT_FF = 1024
CAPACITY_FACTOR = 2
NORM_EPS = 1e-6

OFF_UV = 0
OFF_CQ = OFF_UV + 2 * A_WIDTH
OFF_CKV = OFF_CQ + Q_LORA_RANK
OFF_KR = OFF_CKV + KV_LORA_RANK
OFF_GA = OFF_KR + QK_ROPE_DIM
OFF_GB = OFF_GA + D_MODEL
IN_COLS = OFF_GB + D_MODEL

kernel_name = "hybrid_gmlp_mla_ec_encoder"

def _rmsnorm(x, g):
    xf = x.astype(jnp.float32)
    y = xf * lax.rsqrt(jnp.mean(xf * xf, axis=-1, keepdims=True) + NORM_EPS)
    return (y * g.astype(jnp.float32)).astype(x.dtype)

def _rope_tables(seq):
    half = QK_ROPE_DIM // 2
    inv_freq = ROPE_THETA ** (-jnp.arange(half, dtype=jnp.float32) / half)
    freqs = jnp.arange(seq, dtype=jnp.float32)[:, None] * inv_freq[None, :]
    return jnp.cos(freqs)[:, None, :], jnp.sin(freqs)[:, None, :]

def _rope(x, cos, sin):
    half = QK_ROPE_DIM // 2
    xf = x.astype(jnp.float32)
    x1, x2 = xf[..., :half], xf[..., half:]
    return jnp.concatenate([x1 * cos - x2 * sin, x1 * sin + x2 * cos], axis=-1).astype(x.dtype)

def _chunk_gmlp(uv, v_norm_g, w_spatial, b_spatial, w_a_out):
    B, S, _ = uv.shape
    uv = jax.nn.gelu(uv, approximate=False)
    u, v = uv[..., :A_WIDTH], uv[..., A_WIDTH:]
    v = _rmsnorm(v, v_norm_g)
    v = v.reshape(B, S // CHUNK, CHUNK, A_GROUPS, A_GROUP_DIM)
    sv = jnp.einsum('gpq,bnqgc->bnpgc', w_spatial, v) + b_spatial.T[None, None, :, :, None]
    sv = sv.reshape(B, S, A_WIDTH)
    return (u * sv) @ w_a_out

def _mla(c_q, c_kv, k_rope, q_norm_g, w_uq, kv_norm_g, w_ukv, q_head_g, k_head_g, w_b_out):
    B, S, _ = c_q.shape
    cos, sin = _rope_tables(S)
    q = (_rmsnorm(c_q, q_norm_g) @ w_uq).reshape(B, S, N_HEADS, QK_HEAD_DIM)
    kv = (_rmsnorm(c_kv, kv_norm_g) @ w_ukv).reshape(B, S, N_HEADS, QK_NOPE_DIM + V_HEAD_DIM)
    k_nope, v = kv[..., :QK_NOPE_DIM], kv[..., QK_NOPE_DIM:]
    k_r = jnp.broadcast_to(k_rope[:, :, None, :], (B, S, N_HEADS, QK_ROPE_DIM))
    k = jnp.concatenate([k_nope, k_r], axis=-1)
    q = _rmsnorm(q, q_head_g)
    k = _rmsnorm(k, k_head_g)
    q = jnp.concatenate([q[..., :QK_NOPE_DIM], _rope(q[..., QK_NOPE_DIM:], cos, sin)], axis=-1)
    k = jnp.concatenate([k[..., :QK_NOPE_DIM], _rope(k[..., QK_NOPE_DIM:], cos, sin)], axis=-1)
    scale = QK_HEAD_DIM ** -0.5
    n_blk = S // Q_BLOCK
    q_blocks = q.reshape(B, n_blk, Q_BLOCK, N_HEADS, QK_HEAD_DIM).transpose(1, 0, 2, 3, 4)

    def attend(qb):
        s = jnp.einsum('bqhd,bkhd->bhqk', qb, k, preferred_element_type=jnp.float32) * scale
        p = jax.nn.softmax(s, axis=-1).astype(v.dtype)
        return jnp.einsum('bhqk,bkhd->bqhd', p, v)

    o = lax.map(attend, q_blocks)
    o = o.transpose(1, 0, 2, 3, 4).reshape(B, S, N_HEADS * V_HEAD_DIM)
    return o @ w_b_out

def _expert_choice_ffn(h, w_router, w_gate, w_up, w_down):
    B, S, D = h.shape
    n_tok = B * S
    t = h.reshape(n_tok, D)
    cap = max(1, min(n_tok, CAPACITY_FACTOR * n_tok // N_EXPERTS))
    aff = jax.nn.softmax((t @ w_router).astype(jnp.float32), axis=-1)
    gates, idx = lax.top_k(aff.T, cap)
    xs = t[idx]
    hid = jax.nn.silu(jnp.einsum('ecd,edf->ecf', xs, w_gate)) * jnp.einsum('ecd,edf->ecf', xs, w_up)
    out = jnp.einsum('ecf,efd->ecd', hid, w_down) * gates[..., None].astype(t.dtype)
    y = jnp.zeros_like(t).at[idx.reshape(-1)].add(out.reshape(-1, D))
    return y.reshape(B, S, D)

def _layer(x, norm1_g, w_in, v_norm_g, w_spatial, b_spatial, w_a_out, q_norm_g, w_uq,
           kv_norm_g, w_ukv, q_head_g, k_head_g, w_b_out, w_out, norm2_g,
           w_router, w_gate, w_up, w_down):
    h = _rmsnorm(x, norm1_g)
    p = h @ w_in
    uv = p[..., OFF_UV:OFF_CQ]
    c_q = p[..., OFF_CQ:OFF_CKV]
    c_kv = p[..., OFF_CKV:OFF_KR]
    k_rope = p[..., OFF_KR:OFF_GA]
    g_a = jax.nn.sigmoid(p[..., OFF_GA:OFF_GB])
    g_b = jax.nn.sigmoid(p[..., OFF_GB:IN_COLS])
    a_out = _chunk_gmlp(uv, v_norm_g, w_spatial, b_spatial, w_a_out)
    b_out = _mla(c_q, c_kv, k_rope, q_norm_g, w_uq, kv_norm_g, w_ukv, q_head_g, k_head_g, w_b_out)
    x = x + (g_a * a_out + g_b * b_out) @ w_out
    x = x + _expert_choice_ffn(_rmsnorm(x, norm2_g), w_router, w_gate, w_up, w_down)
    return x

def setup_inputs(seed: int = 0) -> dict:
    key = jax.random.key(seed)
    ks = jax.random.split(key, 24)

    def nrm(k, shape, fan_in):
        return jax.random.normal(k, shape, jnp.float32) * (fan_in ** -0.5)

    def gain(k, shape):
        return 1.0 + 0.02 * jax.random.normal(k, shape, jnp.float32)

    L = DEPTH
    return {
        "x_prompt": jax.random.normal(ks[0], (BATCH, SEQ, D_MODEL), jnp.float32),
        "x_sample": jax.random.normal(ks[1], (DEC_BATCH, DEC_SEQ, D_MODEL), jnp.float32),
        "norm1_g": gain(ks[2], (L, D_MODEL)),
        "w_in": nrm(ks[3], (L, D_MODEL, IN_COLS), D_MODEL),
        "v_norm_g": gain(ks[4], (L, A_WIDTH)),
        "w_spatial": nrm(ks[5], (L, A_GROUPS, CHUNK, CHUNK), CHUNK),
        "b_spatial": gain(ks[6], (L, A_GROUPS, CHUNK)),
        "w_a_out": nrm(ks[7], (L, A_WIDTH, D_MODEL), A_WIDTH),
        "q_norm_g": gain(ks[8], (L, Q_LORA_RANK)),
        "w_uq": nrm(ks[9], (L, Q_LORA_RANK, N_HEADS * QK_HEAD_DIM), Q_LORA_RANK),
        "kv_norm_g": gain(ks[10], (L, KV_LORA_RANK)),
        "w_ukv": nrm(ks[11], (L, KV_LORA_RANK, N_HEADS * (QK_NOPE_DIM + V_HEAD_DIM)), KV_LORA_RANK),
        "q_head_g": gain(ks[12], (L, QK_HEAD_DIM)),
        "k_head_g": gain(ks[13], (L, QK_HEAD_DIM)),
        "w_b_out": nrm(ks[14], (L, N_HEADS * V_HEAD_DIM, D_MODEL), N_HEADS * V_HEAD_DIM),
        "w_out": nrm(ks[15], (L, D_MODEL, D_MODEL), D_MODEL),
        "norm2_g": gain(ks[16], (L, D_MODEL)),
        "w_router": nrm(ks[17], (L, D_MODEL, N_EXPERTS), D_MODEL),
        "w_gate": nrm(ks[18], (L, N_EXPERTS, D_MODEL, EXPERT_FF), D_MODEL),
        "w_up": nrm(ks[19], (L, N_EXPERTS, D_MODEL, EXPERT_FF), D_MODEL),
        "w_down": nrm(ks[20], (L, N_EXPERTS, EXPERT_FF, D_MODEL), EXPERT_FF),
    }

def reference(x_prompt, x_sample, norm1_g, w_in, v_norm_g, w_spatial, b_spatial, w_a_out,
              q_norm_g, w_uq, kv_norm_g, w_ukv, q_head_g, k_head_g, w_b_out, w_out,
              norm2_g, w_router, w_gate, w_up, w_down):
    params = (norm1_g, w_in, v_norm_g, w_spatial, b_spatial, w_a_out, q_norm_g, w_uq,
              kv_norm_g, w_ukv, q_head_g, k_head_g, w_b_out, w_out, norm2_g,
              w_router, w_gate, w_up, w_down)

    def run(x):
        for l in range(DEPTH):
            x = _layer(x, *[prm[l] for prm in params])
        return x

    y_prompt = run(x_prompt)
    y_sample = run(x_sample)
    return (y_prompt, y_sample)


_drawn_inputs = setup_inputs


def setup_inputs(seed=0):
    import zlib

    import numpy as np

    out = dict(_drawn_inputs(seed))
    spreads = {}
    factors = {'norm1_g': 2.998,
     'v_norm_g': 5.293,
     'b_spatial': 5.695,
     'q_norm_g': 8.0,
     'kv_norm_g': 8.0,
     'q_head_g': 8.0,
     'k_head_g': 8.0,
     'norm2_g': 3.229}
    for name, (base, spread) in spreads.items():
        noise = np.random.default_rng([zlib.crc32(name.encode()), seed]).standard_normal(out[name].shape)
        drawn = base * np.exp(spread * noise) if base else spread * noise
        out[name] = __import__('jax').numpy.asarray(drawn.astype(out[name].dtype))
    for name, factor in factors.items():
        out[name] = (out[name] * factor).astype(out[name].dtype)
    return out
```

```python
from contextlib import ExitStack

import concourse.bass as bass
from concourse import mybir

F32 = mybir.dt.float32
F32R = mybir.dt.float32r
U32 = mybir.dt.uint32
ALU = mybir.AluOpType
ACT = mybir.ActivationFunctionType
AX_X = mybir.AxisListType.X

P = 128
D = 1024
KD = D // P
TP, TS = 1024, 256
T = TP + TS
NCH = T // P
NCH_P = TP // P
BLOCKS = [(0, 512), (512, 512), (1024, 256)]
BANK = 512
H = 8
NOPE, ROPE = 128, 64
HEAD = NOPE + ROPE
QR, KVR = 256, 128
OFF_CQ = 2 * D
OFF_KR = OFF_CQ + QR + KVR
OFF_GA = OFF_KR + ROPE
EPS = 1e-6
SCALE = float(HEAD) ** -0.5
E = 16
CAP_P, CAP_S = 2 * TP // E, 2 * TS // E
GRP = P // CAP_S
GN = D // GRP

G_C, G_V, G_U, G_GATE, G_A, G_B, G_OUT = 0, 4, 12, 20, 36, 44, 52


def build(nc, x_p, x_s, norm1_g, w_in, v_norm_g, w_spatial, b_spatial, w_a_out, q_norm_g, w_uq,
          kv_norm_g, w_ukv, q_head_g, k_head_g, w_b_out, w_out, norm2_g, w_router, w_gate, w_up,
          w_down, rope_cs, y_p, y_s):
    ctx = ExitStack()
    with ctx:
        def sem(name):
            return ctx.enter_context(nc.semaphore(name))

        def sb(stack, name, shape, dt=F32):
            return stack.enter_context(nc.sbuf_tensor(name, shape, dt))

        def f32(ap):
            return ap.bitcast(F32)

        v_d = nc.dram_tensor("v_d", [KD, P, T], F32).ap()
        u_d = nc.dram_tensor("u_d", [KD, P, T], F32).ap()
        g_d = nc.dram_tensor("g_d", [2 * KD, P, T], F32).ap()
        y_d = nc.dram_tensor("ya_d", [KD, P, T], F32).ap()
        za_d = nc.dram_tensor("za_d", [KD, P, T], F32).ap()
        z_d = nc.dram_tensor("z_d", [KD, P, T], F32).ap()
        o_d = nc.dram_tensor("o_d", [H, P, T], F32).ap()
        h_d = nc.dram_tensor("h_d", [T, D], F32).ap()

        PS = ctx.enter_context(nc.psum_tensor("PS", [P, 8 * BANK], F32))

        def bank(b, n=BANK, w=1):
            return PS[:, b * BANK:b * BANK + n * w]

        def lin_set(j, b):
            o = 3 * BANK * j + BLOCKS[b][0]
            return PS[:, o:o + BLOCKS[b][1]]

        def lin_all(j):
            return PS[:, 3 * BANK * j:3 * BANK * j + T]

        ident = sb(ctx, "ident", [P, P])
        ones = sb(ctx, "ones", [P, P])
        small = sb(ctx, "small", [P, 256])
        g1c = small[:, 0:8]
        gqn = small[:, 8:10]
        gkvn = small[:, 10:11]
        gq = small[:, 11:12]
        gqr = small[:, 12:13]
        gk = small[:, 13:14]
        gkr = small[:, 14:15]
        ssq1 = small[:, 16:26]
        var1 = small[:, 26:36]
        rstd1 = small[:, 36:46]
        std1 = small[:, 46:56]
        ssq2 = small[:, 56:66]
        var2 = small[:, 66:76]
        rstd2 = small[:, 76:86]
        std2 = small[:, 86:96]
        rq_v = small[:, 96:106]
        rq_s = small[:, 106:116]
        rq_r = small[:, 116:126]
        rq = small[:, 126:136]
        mx = small[:, 136:146]
        nmx = small[:, 146:156]
        psumr = small[:, 156:166]
        prec = small[:, 166:176]
        lmx = small[:, 176:186]
        lsum = small[:, 186:196]
        lrec = small[:, 196:206]
        vg = small[:, 206:207]
        gcol_p = small[:, 207:208]
        gcol_s = small[:, 208:209]
        epsc = small[:, 209:210]
        rk_v = small[:, 210:220]
        rk_s = small[:, 220:230]
        rk_r = small[:, 230:240]
        spare = small[:, 240:241]


        w_raw = sb(ctx, "w_raw", [P, 2, KD, P])
        w_hi = sb(ctx, "w_hi", [P, 2, KD, P], F32R)
        w_lo = sb(ctx, "w_lo", [P, 2, KD, P], F32R)
        stg = sb(ctx, "stg", [P, 2, T])
        gt = sb(ctx, "gt", [P, 2, T])

        region_a = 2 * KD * T * 4
        with ExitStack() as s:
            act_hi = sb(s, "act_hi", [P, KD, T], F32R)
            act_lo = sb(s, "act_lo", [P, KD, T], F32R)
            with ExitStack() as s2:
                x_in = sb(s2, "x_in", [P, NCH, D])
                xn = sb(s2, "xn", [P, 2, D])
                htmp = sb(s2, "htmp", [P, 2, KD, P])
            with ExitStack() as s2:
                tab_q = sb(s2, "tab_q", [P, T])
                cq_hi = sb(s2, "cq_hi", [P, 2, T], F32R)
                cq_lo = sb(s2, "cq_lo", [P, 2, T], F32R)
                ckv = sb(s2, "ckv", [P, T])
                krf = sb(s2, "krf", [P, T])
                sq_kr = sb(s2, "sq_kr", [P, T])
                ckv_hi = sb(s2, "ckv_hi", [P, T], F32R)
                ckv_lo = sb(s2, "ckv_lo", [P, T], F32R)
                with ExitStack() as s3:
                    rs_v = sb(s3, "rs_v", [P, T])
                    with ExitStack() as s4:
                        acc_v = sb(s4, "acc_v", [P, T])
                        ct = sb(s4, "ct", [P, 3, T])
                    with ExitStack() as s4:
                        vt = sb(s4, "vt", [P, T])
                        vtok = sb(s4, "vtok", [P, T])
                        yt = sb(s4, "yt", [P, T])
                        ws = sb(s4, "ws", [P, P])
                        wsT = sb(s4, "wsT", [P, P])
                        bb = sb(s4, "bb", [P, P])
                with ExitStack() as s3:
                    aq_raw = sb(s3, "aq_raw", [P, 2, 256])
                    aq_hi = sb(s3, "aq_hi", [P, 2, 256], F32R)
                    aq_lo = sb(s3, "aq_lo", [P, 2, 256], F32R)
                    akv_raw = sb(s3, "akv_raw", [P, 256])
                    ak_hi = sb(s3, "ak_hi", [P, P], F32R)
                    ak_lo = sb(s3, "ak_lo", [P, P], F32R)
                    kf = sb(s3, "kf", [P, T])
                    diag = sb(s3, "diag", [P, T])
                    prob = sb(s3, "prob", [P, 2, TP])
                    ostg = sb(s3, "ostg", [P, 2, BANK])
            with ExitStack() as s2:
                zt = sb(s2, "zt", [P, 2, T])
            with ExitStack() as s2:
                with ExitStack() as s3:
                    x2 = sb(s3, "x2", [P, NCH, D])
                with ExitStack() as s3:
                    xs_p = sb(s3, "xs_p", [P, D])
                    xs_s = sb(s3, "xs_s", [CAP_S, D])
                    xT_hi = sb(s3, "xT_hi", [P, KD, P], F32R)
                    xT_lo = sb(s3, "xT_lo", [P, KD, P], F32R)
                    hT_hi = sb(s3, "hT_hi", [P, KD, P], F32R)
                    hT_lo = sb(s3, "hT_lo", [P, KD, P], F32R)
                    hid = sb(s3, "hid", [P, D])
                    ob_p = sb(s3, "ob_p", [P, D])
                    ob_s = sb(s3, "ob_s", [CAP_S, D])
                    xT_s = sb(s3, "xT_s", [P, KD, CAP_S])
                    hid_s = sb(s3, "hid_s", [P, GN])
                    hT_s = sb(s3, "hT_s", [P, GN])
                    ixg_p = sb(s3, "ixg_p", [P, 1], U32)
                    ixg_s = sb(s3, "ixg_s", [CAP_S, 1], U32)
                    ixs_p = sb(s3, "ixs_p", [P, 1], U32)
                    ixs_s = sb(s3, "ixs_s", [CAP_S, 1], U32)
                x2_end = sb(s2, "x2_room", [P, NCH, D])
                g2b = sb(s2, "g2b", [P, D])
                wr = sb(s2, "wr", [P, KD, E])
                lg = sb(s2, "lg", [P, NCH, E])
                aff = sb(s2, "aff", [P, NCH, E])
                affT = sb(s2, "affT", [E, T])
                topv = sb(s2, "topv", [E, 2, P])
                topi = sb(s2, "topi", [E, 2, P], U32)
                topf = sb(s2, "topf", [E, 2, P])
                gates = sb(s2, "gates", [P, 2, E])
                rows = sb(s2, "rows", [P, 3, E], U32)
        with ExitStack() as s:
            q_hi = sb(s, "q_hi", [P, T], F32R)
            q_lo = sb(s, "q_lo", [P, T], F32R)
            qr2 = sb(s, "qr2", [P, T], F32R)
            k_hi = sb(s, "k_hi", [P, T], F32R)
            k_lo = sb(s, "k_lo", [P, T], F32R)
            kr2 = sb(s, "kr2", [P, T], F32R)
            krl = sb(s, "krl", [P, T], F32R)
            v_hi = sb(s, "v_hi", [P, T], F32R)
            v_lo = sb(s, "v_lo", [P, T], F32R)
            pt_hi = sb(s, "pt_hi", [P, NCH_P, BANK], F32R)
            pt_lo = sb(s, "pt_lo", [P, NCH_P, BANK], F32R)
        with ExitStack() as s:
            raw = sb(s, "raw", [P, 4, 2, D])
            ehi = sb(s, "ehi", [P, 3, 2, D], F32R)
            elo = sb(s, "elo", [P, 3, 2, D], F32R)
        h2, h2T = w_raw[:, :, :, :], gt[:, :, 0:D]
        tab_k, sq_v = gt[:, 0, :], gt[:, 1, :]
        ut = gt[:, 0, :]
        sq_q, sq_qr, sq_k = stg[:, 0, :], gt[:, 0, :], gt[:, 1, :]
        rt1, rt2 = stg[0:ROPE, 1, :], prob[:, :, :].rearrange("p a n -> p (a n)")[0:ROPE, 0:T]
        rt3 = diag[0:ROPE, :]

        names = """consts params n1_ssq n1_small n1_xn n1_tr n1_h n1_hi n1_lo
            w_in0 w_in1 w_hi_s w_lo_s blk evac stored0 stored1 v_sq v_acc
            c_dve c_act c_sta c_stev
            sp_vin sp_wsin sp_uin sp_bin sp_vn sp_t sp_tok sp_m sp_act sp_y sp_stored
            ld_in0 ld_in1 ld_hi ld_lo gt_in0 gt_in1 zt_in0 zt_in1 z_mul
            aw_in aw_hi aw_lo ap_pe ap_act ap_dve
            qk_pe mx_dve nm_dve ex_act rc_dve pr_dve t_pe th_act tl_dve pv_pe ov_act o_st0 o_st1
            x2_in ot_pe x2_dve
            r_in rt_pe0 r_ssq r_small r_h r_t r_hT r_exp r_dve y_out h_out0 h_out1 a_t a_T tk rt_pe rows_s
            e_in0 e_in1 e_in2 e_in3 e_hi e_lo e_pe g_ap g_as u_ap u_as d_ap d_as
           ix_g ix_s gath tx_pe txs_pe xh_act xl_dve xs_dve silu_p silu_s mul_p mul_s th_pe ths_pe hh_act
            hl_dve hs_dve ob_act ob_dve scat passed_pool passed_pe""".split()
        S = {n: sem(n) for n in names}
        credit = {n: 2 for n in """sp_t sp_y sp_m sp_act sp_tok sp_vn aw_lo aw_hi ap_pe ap_act ap_dve
            qk_pe mx_dve nm_dve ex_act rc_dve pr_dve t_pe th_act tl_dve pv_pe ov_act ld_lo
            z_mul ot_pe x2_dve""".split()}
        credit.update(o_st0=32, o_st1=32, sp_stored=32)

        def at(name, n):
            return n + credit.get(name, 0)

        w_in_s = [S["w_in0"], S["w_in1"]]
        stored = [S["stored0"], S["stored1"]]
        x_in_s = [sem(f"x_loaded{n}") for n in range(5)]
        ld_in = [S["ld_in0"], S["ld_in1"]]
        gt_in = [S["gt_in0"], S["gt_in1"]]
        zt_in = [S["zt_in0"], S["zt_in1"]]

        def mm3(pe, out, lh, ll, rh, rl, first, last):
            pe.matmul(out, lh, rh, start=first, stop=False)
            pe.matmul(out, lh, rl, start=False, stop=False)
            return pe.matmul(out, ll, rh, start=False, stop=last)

        w_in_v = w_in.rearrange("(k p) n -> p k n", p=P)
        x_view = [x_p.rearrange("(c p) d -> p c d", p=P), x_s.rearrange("(c p) d -> p c d", p=P)]

        def w_tile(kind, m):
            if kind in "vug":
                first = {"v": D, "u": 0, "g": OFF_GA}[kind]
                return w_in_v[:, :, bass.ds(m * P + first, P)]
            w = {"a": w_a_out, "b": w_b_out, "o": w_out}[kind]
            return w.rearrange("(k p) n -> p k n", p=P)[:, :, bass.ds(m * P, P)]

        def pieces(e):
            first, last = isinstance(e, int) and e == 0, isinstance(e, int) and e == E
            q0 = 0 if first else 12 * e - 4
            out = []
            if not last:
                out += [("g", e, l, l) for l in range(4)] + [("u", e, l, l + 4) for l in range(4)]
            if not first:
                out += [("d", e - 1, l, (l if last else l + 8)) for l in range(4)]
            return [(kind, ee, kk, q0 + l, l % 4) for kind, ee, kk, l in out]

        def part(l, first):
            return l % 3 if first else (l + 2) % 3

        def loads_of(e, n):
            if isinstance(e, int):
                return 16 * ((0 if e == 0 else 12 * e - 4) + n + 4 >> 2)
            return 48 * e + (16 * (n // 4))

        def run_frames(eng, frame):
            frame(0)
            frame(1)
            with eng.Fori(2, E - 1) as e:
                frame(e)
            frame(E - 1)
            frame(E)

        PE_STEPS, ACT_STEPS, DVE_STEPS = 17, 11, 17

        block = ctx.enter_context(nc.Block())

        @block.sync
        def _(sp):
            def load_w(g, j, view):
                sp.wait_ge(S["w_lo_s"], g - 1)
                sp.dma_start(w_raw[:, j], view).then_inc(w_in_s[j], 16)

            def load_act(src, n0):
                for j in range(2):
                    sp.dma_start(stg[:, j, :], src[j]).then_inc(ld_in[j], 16)
                with sp.Fori(1, KD // 2) as i:
                    for j in range(2):
                        sp.wait_ge(S["ld_lo"], at("ld_lo", n0 + 2 * i + (j - 1)))
                        sp.dma_start(stg[:, j, :], src[2 * i + j]).then_inc(ld_in[j], 16)

            col = lambda a: a.rearrange("(p o) -> p o", o=1)
            for n in range(5):
                src = x_view[0][:, 2 * n:2 * n + 2] if n < 4 else x_view[1][:, 0:2]
                sp.dma_start(x_in[:, 2 * n:2 * n + 2], src).then_inc(x_in_s[n], 16)
            sp.dma_start(w_raw[:, 0], w_in_v[:, :, OFF_CQ:OFF_CQ + P]).then_inc(w_in_s[0], 16)
            sp.dma_start(w_raw[:, 1], w_in_v[:, :, OFF_CQ + P:OFF_CQ + 2 * P]).then_inc(w_in_s[1], 16)
            for dst, src in ((g1c, norm1_g.rearrange("(k p) -> p k", p=P)),
                             (gqn, q_norm_g.rearrange("(k p) -> p k", p=P)), (gkvn, col(kv_norm_g)),
                             (gq, col(q_head_g)[0:NOPE]), (gqr[0:64], col(q_head_g)[NOPE:HEAD]),
                             (gqr[64:96], col(q_head_g)[NOPE + 32:HEAD]),
                             (gqr[96:128], col(q_head_g)[NOPE:NOPE + 32]),
                             (gk, col(k_head_g)[0:NOPE]), (gkr[0:64], col(k_head_g)[NOPE:HEAD]),
                             (gkr[64:96], col(k_head_g)[NOPE + 32:HEAD]),
                             (gkr[96:128], col(k_head_g)[NOPE:NOPE + 32]), (tab_k, rope_cs)):
                sp.dma_start(dst, src, allow_slow_non_contiguous=True).then_inc(S["params"], 16)

            sp.wait_ge(S["w_lo_s"], 1)
            sp.dma_start(w_raw[:, 0], w_in_v[:, :, OFF_CQ + 2 * P:OFF_CQ + 3 * P]).then_inc(w_in_s[0], 16)
            sp.wait_ge(S["w_lo_s"], 2)
            for a, b, c in ((0, 64, 0), (64, 96, 32), (96, 128, 0)):
                sp.dma_start(w_raw[:, 1, :, a:b], w_in_v[:, :, OFF_KR + c:OFF_KR + c + b - a])\
                    .then_inc(w_in_s[1], 16)
            sp.wait_ge(S["n1_lo"], NCH)
            sp.dma_start(tab_q[:], rope_cs).then_inc(S["params"], 16)

            for kind, g0 in (("v", G_V), ("u", G_U)):
                with sp.Fori(0, KD // 2) as i:
                    for j in range(2):
                        load_w(g0 + 2 * i + j, j, w_tile(kind, 2 * i + j))

            for j in range(2):
                sp.wait_ge(stored[j], 16 * KD)
            sp.wait_ge(S["c_dve"], 21)
            with sp.Fori(0, KD) as i:
                load_w(G_GATE + 2 * i, 0, w_tile("g", 2 * i))
                sp.wait_ge(S["sp_t"], at("sp_t", 3 * i))
                sp.dma_start(vt[:], v_d[i]).then_inc(S["sp_vin"], 16)
                sp.dma_start(ws[:], w_spatial[i]).then_inc(S["sp_wsin"], 16)
                load_w(G_GATE + 2 * i + 1, 1, w_tile("g", 2 * i + 1))
                sp.wait_ge(S["sp_y"], at("sp_y", 3 * i))
                sp.dma_start(ut, u_d[i]).then_inc(S["sp_uin"], 16)
                sp.dma_start(bb[:], b_spatial[bass.ds(i, 1), :].to_broadcast([P, P])).then_inc(S["sp_bin"], 16)
                sp.dma_start(vg, v_norm_g.rearrange("(k p o) -> k p o", p=P, o=1)[i]).then_inc(S["sp_bin"], 16)

            sp.wait_ge(S["sp_stored"], at("sp_stored", 16 * KD))
            for j in range(2):
                sp.wait_ge(stored[j], 16 * 2 * KD)
            load_act(y_d, 0)
            for j in range(2):
                load_w(G_A + j, j, w_tile("a", j))
                sp.dma_start(gt[:, j, :], g_d[j]).then_inc(gt_in[j], 16)
            with sp.Fori(1, KD // 2) as i:
                for j in range(2):
                    load_w(G_A + 2 * i + j, j, w_tile("a", 2 * i + j))
                    sp.wait_ge(S["evac"], 3 * (G_A - 1) + 3 * (2 * i + j))
                    sp.dma_start(gt[:, j, :], g_d[2 * i + j]).then_inc(gt_in[j], 16)

            uq = w_uq.rearrange("(k p) n -> p k n", p=P)
            sp.wait_ge(S["evac"], 3 * G_A)
            with sp.Fori(0, H) as h:
                sp.wait_ge(S["ap_pe"], at("ap_pe", PE_STEPS * h))
                sp.dma_start(aq_raw[:, :, 0:HEAD], uq[:, :, bass.ds(h * HEAD, HEAD)]).then_inc(S["aw_in"], 16)
                sp.dma_start(aq_raw[:, :, 192:224], uq[:, :, bass.ds(h * HEAD + (NOPE + 32), 32)]).then_inc(S["aw_in"], 16)
                sp.dma_start(aq_raw[:, :, 224:256], uq[:, :, bass.ds(h * HEAD + NOPE, 32)]).then_inc(S["aw_in"], 16)
                sp.dma_start(akv_raw[:], w_ukv[:, bass.ds(h * 256, 256)]).then_inc(S["aw_in"], 16)

            for j in range(2):
                load_w(G_B + j, j, w_tile("b", j))
            sp.wait_ge(S["o_st0"], at("o_st0", 32 * H))
            sp.wait_ge(S["o_st1"], at("o_st1", 16 * H))
            for j in range(2):
                sp.wait_ge(stored[j], 16 * 20)
            sp.wait_ge(S["tl_dve"], at("tl_dve", NCH * H))
            load_act(o_d, KD)
            for j in range(2):
                sp.dma_start(gt[:, j, :], g_d[KD + j]).then_inc(gt_in[j], 16)
                sp.dma_start(zt[:, j, :], za_d[j]).then_inc(zt_in[j], 16)
            with sp.Fori(1, KD // 2) as i:
                for j in range(2):
                    load_w(G_B + 2 * i + j, j, w_tile("b", 2 * i + j))
                    sp.wait_ge(S["z_mul"], at("z_mul", 2 * i + (j - 1)))
                    sp.dma_start(gt[:, j, :], g_d[2 * i + (KD + j)]).then_inc(gt_in[j], 16)
                    sp.wait_ge(stored[j], 16 * 20 + 16 * i)
                    sp.dma_start(zt[:, j, :], za_d[2 * i + j]).then_inc(zt_in[j], 16)

            for j in range(2):
                sp.wait_ge(stored[j], 16 * 24)
            sp.dma_start(x2[:, 0:NCH_P], x_view[0]).then_inc(S["x2_in"], 16)
            sp.dma_start(x2[:, NCH_P:NCH], x_view[1]).then_inc(S["x2_in"], 16)
            load_act(z_d, 2 * KD)
            with sp.Fori(0, KD // 2) as i:
                for j in range(2):
                    load_w(G_OUT + 2 * i + j, j, w_tile("o", 2 * i + j))
            sp.dma_start(g2b[:], norm2_g.rearrange("(o d) -> o d", o=1).to_broadcast([P, D])).then_inc(S["r_in"], 16)
            sp.dma_start(wr[:], w_router.rearrange("(k p) e -> p k e", p=P)).then_inc(S["r_in"], 16)
            sp.wait_ge(S["x2_dve"], at("x2_dve", 3 * KD))
            sp.dma_start(y_p.rearrange("(c p) d -> p c d", p=P), x2[:, 0:NCH_P]).then_inc(S["y_out"], 16)
            sp.dma_start(y_s.rearrange("(c p) d -> p c d", p=P), x2[:, NCH_P:NCH]).then_inc(S["y_out"], 16)

            sp.wait_ge(S["blk"], 3 * (G_OUT + KD))
            mats = {"g": w_gate, "u": w_up, "d": w_down}

            def load_piece(kind, e, kk, q, slot):
                if not isinstance(q, int) or q >= 4:
                    sp.wait_ge(S["e_pe"], q - 3)
                sp.dma_start(raw[:, slot], mats[kind][e].rearrange("(k p) n -> p k n", p=P)[:, 2 * kk:2 * kk + 2])\
                    .then_inc(S[f"e_in{slot}"], 16)

            def frame(e):
                for kind, ee, kk, q, slot in pieces(e):
                    load_piece(kind, ee, kk, q, slot)
            run_frames(sp, frame)
            sp.wait_ge(S["scat"], 32 * E)

        @block.gpsimd
        def _(pool):
            def settled():
                pool.sem_inc(S["passed_pool"], 1)

            for n, c in credit.items():
                pool.sem_inc(S[n], c)
            pool.memset(ones[:], 1.0).then_inc(S["consts"], 1)
            pool.memset(ident[:], 1.0).then_inc(S["consts"], 1)
            pool.memset(epsc, EPS).then_inc(S["consts"], 1)
            pool.wait_ge(S["consts"], 3)
            pool.affine_select(out=ident[:], in_=ident[:], compare_op=ALU.is_equal, fill=0.0, base=0,
                               pattern=[[-1, P]], channel_multiplier=1).then_inc(S["consts"], 1)

            with pool.Fori(0, NCH // 2) as i:
                for j in range(2):
                    pool.wait_ge(S["n1_hi"], 2 * i + (j + 1))
                    pool.tensor_tensor(act_lo[:, :, bass.ds((2 * i + j) * P, P)], htmp[:, j],
                                       f32(act_hi[:, :, bass.ds((2 * i + j) * P, P)]),
                                       ALU.subtract).then_inc(S["n1_lo"], 1)

            def split(g, j, loads):
                pool.wait_ge(w_in_s[j], 16 * loads)
                pool.wait_ge(S["blk"], 3 * (g - 1)) if not isinstance(g, int) or g > 1 else None
                settled()
                pool.tensor_scalar(w_hi[:, j], w_raw[:, j], 1.0, 0.0, ALU.mult, ALU.add).then_inc(S["w_hi_s"], 1)
                pool.wait_ge(S["w_hi_s"], g + 1)
                pool.tensor_tensor(w_lo[:, j], w_raw[:, j], f32(w_hi[:, j]), ALU.subtract).then_inc(S["w_lo_s"], 1)

            for g in range(4):
                split(g, g % 2, [1, 1, 2, 4][g])

            def split_loop(g0):
                with pool.Fori(0, KD // 2) as i:
                    for j in range(2):
                        split(g0 + 2 * i + j, j, i + (g0 // 2 + 1 + 2 * j))

            split_loop(G_V)
            split_loop(G_U)
            with pool.Fori(0, KD) as i:
                split(G_GATE + 2 * i, 0, i + (G_GATE // 2 + 1))
                split(G_GATE + 2 * i + 1, 1, i + (G_GATE // 2 + 3))
            split_loop(G_A)

            with pool.Fori(0, H) as h:
                pool.wait_ge(S["aw_in"], 64 * h + 64)
                settled()
                pool.tensor_scalar(aq_hi[:], aq_raw[:], 1.0, 0.0, ALU.mult, ALU.add).then_inc(S["aw_hi"], 1)
                pool.tensor_scalar(ak_hi[:], akv_raw[:, 0:P], 1.0, 0.0, ALU.mult, ALU.add).then_inc(S["aw_hi"], 1)
                pool.wait_ge(S["aw_hi"], at("aw_hi", 2 * h + 2))
                pool.tensor_tensor(aq_lo[:], aq_raw[:], f32(aq_hi[:]), ALU.subtract).then_inc(S["aw_lo"], 1)
                pool.tensor_tensor(ak_lo[:], akv_raw[:, 0:P], f32(ak_hi[:]), ALU.subtract).then_inc(S["aw_lo"], 1)
            split_loop(G_B)
            split_loop(G_OUT)
            def gather(e):
                if not (isinstance(e, int) and e == 0):
                    pool.wait_ge(S["tx_pe"], e)
                    pool.wait_ge(S["txs_pe"], e)
                settled()
                for dst, k, n in ((ixg_p, 0, P), (ixg_s, 2, CAP_S)):
                    pool.tensor_copy(dst[:], rows[0:n, k, bass.ds(e, 1)]).then_inc(S["ix_g"], 1)
                pool.wait_ge(S["ix_g"], 2 * e + 2)
                settled()
                pool.indirect_dma_start(xs_p[:], None, h_d, bass.IndirectOffsetOnAxis(ap=ixg_p[:, 0:1], axis=0)).then_inc(S["gath"], 16)
                pool.indirect_dma_start(xs_s[:], None, h_d, bass.IndirectOffsetOnAxis(ap=ixg_s[:, 0:1], axis=0)).then_inc(S["gath"], 16)
                pool.wait_ge(S["gath"], 32 * e + 32)

            def scatter(e):
                settled()
                for dst, k, n in ((ixs_p, 0, P), (ixs_s, 1, CAP_S)):
                    pool.tensor_copy(dst[:], rows[0:n, k, bass.ds(e, 1)]).then_inc(S["ix_s"], 1)
                pool.wait_ge(S["ix_s"], 2 * e + 2)
                pool.wait_ge(S["ob_act"], e + 1)
                pool.wait_ge(S["ob_dve"], e + 1)
                settled()
                pool.indirect_dma_start(y_p, bass.IndirectOffsetOnAxis(ap=ixs_p[:, 0:1], axis=0), ob_p[:], None,
                                        compute_op=ALU.add).then_inc(S["scat"], 16)
                pool.indirect_dma_start(y_s, bass.IndirectOffsetOnAxis(ap=ixs_s[:, 0:1], axis=0), ob_s[:], None,
                                        compute_op=ALU.add).then_inc(S["scat"], 16)
                pool.wait_ge(S["scat"], 32 * e + 32)

            pool.wait_ge(S["rows_s"], 5)
            pool.wait_ge(S["h_out0"], 16 * NCH // 2)
            pool.wait_ge(S["h_out1"], 16 * NCH // 2)
            pool.wait_ge(S["y_out"], 32)
            gather(0)

            def frame(e):
                first, last = isinstance(e, int) and e == 0, isinstance(e, int) and e >= E - 1
                if not (first or (isinstance(e, int) and e == 1)):
                    scatter(e - 2)
                if not last:
                    gather(e + 1)
            run_frames(pool, frame)
            scatter(E - 1)

        @block.tensor
        def _(pe):
            pe.wait_ge(S["consts"], 4)
            with pe.Fori(0, NCH // 2) as i:
                for j in range(2):
                    pe.wait_ge(S["n1_xn"], 2 * i + (j + 1))
                    for k in range(KD):
                        last = pe.transpose(bank(2 * j, D)[:, k * P:(k + 1) * P], xn[:, j, k * P:(k + 1) * P], ident[:])
                    last.then_inc(S["n1_tr"], 1)

            def lin(g, j, between=None):
                pe.wait_ge(S["w_lo_s"], g + 1)
                if not isinstance(g, int) or g > 1:
                    pe.wait_ge(S["evac"], 3 * (g - 1))
                for b, (t0, tn) in enumerate(BLOCKS):
                    for k in range(KD):
                        last = mm3(pe, lin_set(j, b), w_hi[:, j, k], w_lo[:, j, k],
                                   act_hi[:, k, t0:t0 + tn], act_lo[:, k, t0:t0 + tn], k == 0, k == KD - 1)
                    last.then_inc(S["blk"], 1)
                    if between:
                        between(b)

            def lin_loop(g0, between=None):
                with pe.Fori(0, KD // 2) as i:
                    for j in range(2):
                        lin(g0 + 2 * i + j, j, (lambda b: between(i, j, b)) if between else None)

            pe.wait_ge(S["n1_lo"], NCH)
            for g in range(4):
                lin(g, g % 2)
            lin_loop(G_V)

            for n, (src, need, sem_) in enumerate(((rs_v, 4, "c_dve"), (krf, 5, "c_dve"), (acc_v, KD, "v_acc"))):
                pe.wait_ge(S[sem_], need)
                for b, (t0, tn) in enumerate(BLOCKS):
                    q = 3 * n + b
                    if q > 1:
                        pe.wait_ge(S["c_stev"], q - 1)
                    pe.matmul(bank(6 + q % 2, tn), ones[:], src[:, t0:t0 + tn], start=True,
                              stop=True).then_inc(S["c_sta"], 1)
            lin_loop(G_U)

            pe.wait_ge(S["c_stev"], 9)
            with pe.Fori(0, KD) as i:
                def gating(j, b):
                    t0, tn = BLOCKS[b]
                    if j == 0:
                        pe.wait_ge(S["sp_vn"], at("sp_vn", i + 1))
                        if b == 0:
                            pe.wait_ge(S["sp_act"], at("sp_act", 3 * i - 1))
                        elif b == 1:
                            pe.wait_ge(S["sp_act"], at("sp_act", 3 * i))
                        else:
                            pe.wait_ge(S["sp_tok"], at("sp_tok", 4 * i + 1))
                        o = bank(6 + b % 2)
                        for c in range(tn // P):
                            last = pe.transpose(o[:, c * P:(c + 1) * P], vt[:, t0 + c * P:t0 + (c + 1) * P], ident[:])
                        if b == 2:
                            pe.wait_ge(S["sp_wsin"], 16 * i + 16)
                            last = pe.transpose(o[:, 2 * P:3 * P], ws[:], ident[:])
                        last.then_inc(S["sp_t"], 1)
                    else:
                        if b == 0:
                            pe.wait_ge(S["sp_tok"], at("sp_tok", 4 * i + 4))
                        else:
                            pe.wait_ge(S["sp_act"], at("sp_act", 3 * i + (b - 1)))
                        o = bank(7 - b % 2)
                        for c in range(tn // P):
                            last = pe.matmul(o[:, c * P:(c + 1) * P], vtok[:, t0 + c * P:t0 + (c + 1) * P],
                                             wsT[:], start=True, stop=True)
                        last.then_inc(S["sp_m"], 1)
                lin(G_GATE + 2 * i, 0, lambda b: gating(0, b))
                lin(G_GATE + 2 * i + 1, 1, lambda b: gating(1, b))

            pe.wait_ge(S["ld_lo"], at("ld_lo", KD))
            lin_loop(G_A)

            pe.wait_ge(S["evac"], 3 * G_B)
            pe.wait_ge(S["c_dve"], 22)
            with pe.Fori(0, H) as h:
                def dve(n):
                    pe.wait_ge(S["ap_dve"], at("ap_dve", DVE_STEPS * h + n))

                def acts(n):
                    pe.wait_ge(S["ap_act"], at("ap_act", ACT_STEPS * h + n))

                def column_sums(out, parts):
                    for c in range(NCH):
                        for n, src in enumerate(parts):
                            last = pe.matmul(out[:, c:c + 1], src[:, c * P:(c + 1) * P], ones[0:src.shape[0], 0:1],
                                             start=(n == 0), stop=(n == len(parts) - 1))
                    last.then_inc(S["ap_pe"], 1)

                def project_q(half, j):
                    for b, (t0, tn) in enumerate(BLOCKS):
                        for k in range(2):
                            w = slice(half * P, half * P + P)
                            last = mm3(pe, lin_set(j, b), aq_hi[:, k, w], aq_lo[:, k, w],
                                       cq_hi[:, k, t0:t0 + tn], cq_lo[:, k, t0:t0 + tn], k == 0, k == 1)
                        last.then_inc(S["ap_pe"], 1)

                pe.wait_ge(S["aw_lo"], at("aw_lo", 2 * h + 2))
                pe.wait_ge(S["tl_dve"], at("tl_dve", NCH * h))
                for b, (t0, tn) in enumerate(BLOCKS):
                    mm3(pe, lin_set(1, b), ak_hi[:], ak_lo[:], ckv_hi[:, t0:t0 + tn],
                        ckv_lo[:, t0:t0 + tn], True, True).then_inc(S["ap_pe"], 1)
                project_q(0, 0)
                acts(1)
                pe.wait_ge(S["ov_act"], at("ov_act", 3 * h))
                column_sums(bank(6), (sq_k, sq_kr[0:ROPE]))
                dve(1)
                project_q(1, 1)
                dve(5)
                for b, (t0, tn) in enumerate(BLOCKS):
                    pe.matmul(lin_set(0, b), ones[:], diag[:, t0:t0 + tn], start=True,
                              stop=True).then_inc(S["ap_pe"], 1)
                dve(7)
                for b, (t0, tn) in enumerate(BLOCKS):
                    for c in range(t0, t0 + tn, P):
                        last = pe.matmul(lin_all(1)[:, c:c + P], ckv[:, c:c + P], akv_raw[:, P:2 * P],
                                         start=True, stop=True)
                    last.then_inc(S["ap_pe"], 1)
                column_sums(bank(7), (sq_q, sq_qr[0:ROPE]))
                acts(9)
                dve(13)

                def keys(c):
                    return (0, TP) if c < NCH_P else (TP, TS)

                def scores(c):
                    k0, kn = keys(c)
                    if c == 1:
                        dve(17)
                    pe.wait_ge(S["ex_act"], at("ex_act", NCH * h + (c - 1)))
                    q = slice(c * P, (c + 1) * P)
                    for o in range(0, kn, BANK):
                        n = min(BANK, kn - o)
                        k = slice(k0 + o, k0 + o + n)
                        out = bank(2 * (c % 2) + o // BANK, n)
                        pe.matmul(out, q_hi[:, q], k_hi[:, k], start=True, stop=False)
                        pe.matmul(out, q_hi[:, q], k_lo[:, k], start=False, stop=False)
                        pe.matmul(out, q_lo[:, q], k_hi[:, k], start=False, stop=False)
                        pe.matmul(out, qr2[:, q], kr2[:, k], start=False, stop=False)
                        last = pe.matmul(out, qr2[:, q], krl[:, k], start=False, stop=True)
                    last.then_inc(S["qk_pe"], 1)

                def turn(c):
                    kn = keys(c)[1]
                    pe.wait_ge(S["pr_dve"], at("pr_dve", NCH * h + (c + 1)))
                    pe.wait_ge(S["tl_dve"], at("tl_dve", NCH * h + c))
                    for k in range(kn // P):
                        last = pe.transpose(bank(4, TP)[:, k * P:(k + 1) * P],
                                            prob[:, c % 2, k * P:(k + 1) * P], ident[:])
                    last.then_inc(S["t_pe"], 1)

                def values(b):
                    t0, tn = BLOCKS[b]
                    k0, kn = keys(t0 // P)
                    pe.wait_ge(S["tl_dve"], at("tl_dve", NCH * h + (t0 + tn) // P))
                    pe.wait_ge(S["ov_act"], at("ov_act", 3 * h + max(b - 1, 0)))
                    for k in range(kn // P):
                        v = slice(k0 + k * P, k0 + (k + 1) * P)
                        last = mm3(pe, bank(6 + b % 2, tn), v_hi[:, v], v_lo[:, v], pt_hi[:, k, 0:tn],
                                   pt_lo[:, k, 0:tn], k == 0, k == kn // P - 1)
                    last.then_inc(S["pv_pe"], 1)

                for c in range(NCH + 2):
                    if c < NCH:
                        scores(c)
                    if c in (6, 10):
                        values(c // 4 - 1)
                    if c > 1:
                        turn(c - 2)
                values(2)

            pe.wait_ge(S["ld_lo"], at("ld_lo", 2 * KD))
            lin_loop(G_B)
            pe.wait_ge(S["ld_lo"], at("ld_lo", 3 * KD))

            def back(i, j, b):
                for d in {0: [], 1: [0], 2: [1, 2]}[b]:
                    t0, tn = BLOCKS[d]
                    pe.wait_ge(S["evac"], 3 * (2 * i + (G_OUT + j)) + (d + 1))
                    s = 3 * (2 * i + j) + d
                    pe.wait_ge(S["x2_dve"], at("x2_dve", s - 1))
                    for c in range(tn // P):
                        last = pe.transpose(bank(6 + (3 * j + d) % 2)[:, c * P:(c + 1) * P],
                                            stg[:, j, t0 + c * P:t0 + (c + 1) * P], ident[:])
                    last.then_inc(S["ot_pe"], 1)

            lin_loop(G_OUT, back)
            pe.wait_ge(S["x2_dve"], at("x2_dve", 3 * KD))
            pe.wait_ge(S["r_in"], 32)

            def logits(n):
                pe.wait_ge(S["r_hT"], n + 1)
                for k in range(KD):
                    last = pe.matmul(bank(6)[:, n * E:(n + 1) * E], h2T[:, n % 2, k * P:(k + 1) * P], wr[:, k],
                                     start=(k == 0), stop=(k == KD - 1))
                last.then_inc(S["rt_pe0"], 1)

            for n in range(NCH):
                pe.wait_ge(S["r_h"], n + 1)
                if n > 1:
                    pe.wait_ge(S["r_hT"], n - 1)
                for k in range(KD):
                    last = pe.transpose(bank(2 * (n % 2), D)[:, k * P:(k + 1) * P],
                                        h2[:, n % 2].rearrange("p k t -> p (k t)")[:, k * P:(k + 1) * P], ident[:])
                last.then_inc(S["r_t"], 1)
                if n:
                    logits(n - 1)
            logits(NCH - 1)
            pe.wait_ge(S["r_dve"], 5)
            for c in range(NCH):
                last = pe.transpose(PS[0:E, c * P:(c + 1) * P], aff[:, c, :], ident[:])
            last.then_inc(S["a_t"], 1)
            pe.wait_ge(S["tk"], 3 * (CAP_P + CAP_S) // 8 + 3)
            for n, src in enumerate((topv[:, 0], topv[:, 1], topf[:, 0], topf[:, 1])):
                pe.transpose(bank(3)[:, n * E:(n + 1) * E], src, ident[0:E, 0:E]).then_inc(S["rt_pe"], 1)

            def turn_x(e):
                pe.wait_ge(S["gath"], 32 * e + 32)
                for k in range(KD):
                    last = pe.transpose(bank(0, D)[:, k * P:(k + 1) * P], xs_p[:, k * P:(k + 1) * P], ident[:])
                last.then_inc(S["tx_pe"], 1)

            def turn_xs(e):
                pe.sem_inc(S["passed_pe"], 1)
                for k in range(KD):
                    last = pe.transpose(bank(7)[:, k * CAP_S:(k + 1) * CAP_S], xs_s[:, k * P:(k + 1) * P],
                                        ident[0:CAP_S, 0:CAP_S])
                last.then_inc(S["txs_pe"], 1)

            def product(b0, hi, lo, bs, few, slot, pt, kk, guard_s):
                for kin in range(2):
                    k = 2 * kk + kin
                    for rhs, lhs, st, sp_ in ((ehi, hi, k == 0, False), (elo, hi, False, False), (ehi, lo, False, k == KD - 1)):
                        for half in range(2):
                            pe.matmul(bank(b0 + half), lhs[:, k], rhs[:, pt, kin, half * BANK:(half + 1) * BANK],
                                      start=st, stop=sp_)
                guard_s()
                for kin in range(2):
                    k = 2 * kk + kin
                    for g in range(GRP):
                        last = pe.matmul(bank(bs)[CAP_S * g:CAP_S * (g + 1), 0:GN], few(k),
                                         raw[:, slot, kin, g * GN:(g + 1) * GN], start=(k == 0), stop=(k == KD - 1))
                last.then_inc(S["e_pe"], 1)

            pe.wait_ge(S["rows_s"], 5)
            turn_x(0)
            turn_xs(0)

            def frame(e):
                is0, is1, is_last = (isinstance(e, int) and e == v for v in (0, 1, E))
                for n, (kind, ee, kk, q, slot) in enumerate(pieces(e)):
                    l = n + (8 if is_last else 0)
                    if is_last and n == 0:
                        turn_h(E - 1)
                        pe.wait_ge(S["hl_dve"], E)
                        pe.wait_ge(S["hs_dve"], E)
                    if l == 0:
                        pe.wait_ge(S["xl_dve"], e + 1)
                        pe.wait_ge(S["xs_dve"], e + 1)
                    if l == 4 and not is0:
                        pe.wait_ge(S["hl_dve"], e)
                        pe.wait_ge(S["hs_dve"], e)
                    if l == 8 and not is1:
                        pe.wait_ge(S["ob_act"], e - 1)
                        pe.wait_ge(S["ob_dve"], e - 1) if is_last else None
                    pe.wait_ge(S["e_lo"], q + 1)

                    def guard_s():
                        if l == 0 and not (is0 or is1):
                            pe.wait_ge(S["ob_dve"], e - 1)
                        if l == 8 and not is_last:
                            pe.wait_ge(S["silu_s"], e + 1)
                    if kind == "d":
                        product(4, hT_hi, hT_lo, 6, lambda k: hT_s[:, k % 2 * P + k // 2 * CAP_S:k % 2 * P + k // 2 * CAP_S + CAP_S],
                                slot, part(n if is_last else l, False) if not is_last else q % 3, kk, guard_s)
                    else:
                        product(0 if kind == "g" else 2, xT_hi, xT_lo, 6 if kind == "g" else 7,
                                lambda k: xT_s[:, k], slot, part(l, is0), kk, guard_s)
                    if l == 0 and not is0:
                        turn_h(e - 1)
                    more = not (isinstance(e, int) and e >= E - 1)
                    if more and l == (7 if is0 else 8):
                        pe.wait_ge(S["silu_p"], e + 1)
                        turn_x(e + 1)
                    if more and l == (7 if is0 else 9):
                        pe.wait_ge(S["mul_s"], e + 1)
                        turn_xs(e + 1)

            def turn_h(e):
                pe.wait_ge(S["mul_p"], e + 1)
                for k in range(KD):
                    last = pe.transpose(bank(2, D)[:, k * P:(k + 1) * P], hid[:, k * P:(k + 1) * P], ident[:])
                last.then_inc(S["th_pe"], 1)
                pe.wait_ge(S["mul_s"], e + 1)
                pe.wait_ge(S["xs_dve"], e + 2) if not (isinstance(e, int) and e >= E - 1) else None
                for k in range(2):
                    last = pe.transpose(bank(7)[:, k * P:(k + 1) * P], hid_s[:, k * P:(k + 1) * P], ident[:])
                last.then_inc(S["ths_pe"], 1)

            run_frames(pe, frame)

        @block.scalar
        def _(act):
            for n in range(NCH):
                if n % 2 == 0:
                    act.wait_ge(x_in_s[n // 2], 16)
                if n > 1:
                    act.wait_ge(S["n1_ssq"], n - 1)
                act.activation(xn[:, n % 2], x_in[:, n], ACT.Square, accum_out=ssq1[:, n:n + 1]).then_inc(S["n1_ssq"], 1)
            act.wait_ge(S["n1_small"], 1)
            act.activation(std1, var1, ACT.Sqrt).then_inc(S["n1_small"], 1)
            with act.Fori(0, NCH // 2) as i:
                for j in range(2):
                    act.wait_ge(S["n1_h"], 2 * i + (j + 1))
                    act.activation(act_hi[:, :, bass.ds((2 * i + j) * P, P)], htmp[:, j], ACT.Copy).then_inc(S["n1_hi"], 1)

            dst = [ct[:, 0, :], ct[:, 1, :], ckv[:], ct[:, 2, :]]
            act.wait_ge(S["n1_lo"], NCH)
            for g in range(4):
                for b, (t0, tn) in enumerate(BLOCKS):
                    act.wait_ge(S["blk"], 3 * g + b + 1)
                    act.activation(dst[g][:, t0:t0 + tn], lin_set(g % 2, b), ACT.Copy).then_inc(S["evac"], 1)

            def evac(g, j, func, out, uses, guard=None):
                for b, (t0, tn) in enumerate(BLOCKS):
                    act.wait_ge(S["blk"], 3 * g + (b + 1))
                    if b == 0:
                        if uses is not None:
                            act.wait_ge(stored[j], 16 * uses)
                        if guard is not None:
                            guard()
                    act.activation(stg[:, j, t0:t0 + tn], lin_set(j, b), func).then_inc(S["evac"], 1)
                act.wait_ge(S["evac"], 3 * g + 3)
                act.dma_start(out, stg[:, j, :]).then_inc(stored[j], 16)

            for j in range(2):
                evac(G_V + j, j, ACT.Gelu, v_d[j], None)
            with act.Fori(1, KD // 2) as i:
                for j in range(2):
                    evac(2 * i + (G_V + j), j, ACT.Gelu, v_d[2 * i + j], i,
                         lambda: act.wait_ge(S["v_acc"], 2 * i + (j - 1)))

            rs = [rs_v, krf, rs_v]
            for n in range(3):
                for b, (t0, tn) in enumerate(BLOCKS):
                    q = 3 * n + b
                    act.wait_ge(S["c_sta"], q + 1)
                    if n == 2 and b == 0:
                        act.wait_ge(S["c_dve"], 10)
                        act.wait_ge(S["v_acc"], KD)
                    act.activation(rs[n][:, t0:t0 + tn], bank(6 + q % 2, tn), ACT.Sqrt, bias=epsc,
                                   scale=1.0 / (QR, KVR, D)[n]).then_inc(S["c_stev"], 1)
            for m in range(2):
                act.wait_ge(S["c_dve"], 9 + m)
                act.activation(cq_hi[:, m], ct[:, m, :], ACT.Copy, scale=gqn[:, m:m + 1]).then_inc(S["c_act"], 1)
            act.wait_ge(S["c_dve"], 13)
            act.activation(ckv_hi[:], ckv[:], ACT.Copy).then_inc(S["c_act"], 1)

            with act.Fori(0, KD // 2) as i:
                for j in range(2):
                    evac(2 * i + (G_U + j), j, ACT.Gelu, u_d[2 * i + j], i + 4)

            with act.Fori(0, KD) as i:
                def gated(j):
                    g = 2 * i + (G_GATE + j)
                    for b, (t0, tn) in enumerate(BLOCKS):
                        act.wait_ge(S["blk"], 3 * g + (b + 1))
                        if b == 0:
                            act.wait_ge(stored[j], 16 * i + 16 * KD)
                        act.activation(stg[:, j, t0:t0 + tn], lin_set(j, b), ACT.Sigmoid).then_inc(S["evac"], 1)
                        if j == 0:
                            act.wait_ge(S["sp_t"], at("sp_t", 3 * i + (b + 1)))
                            if b == 0:
                                act.wait_ge(S["sp_m"], at("sp_m", 3 * i))
                            act.activation(vtok[:, t0:t0 + tn], bank(6 + b % 2, tn), ACT.Copy).then_inc(S["sp_tok"], 1)
                            if b == 2:
                                act.activation(wsT[:], bank(6)[:, 2 * P:3 * P], ACT.Copy).then_inc(S["sp_tok"], 1)
                    act.wait_ge(S["evac"], 3 * g + 3)
                    act.dma_start(g_d[2 * i + j], stg[:, j, :]).then_inc(stored[j], 16)
                gated(0)
                gated(1)
                act.wait_ge(S["sp_y"], at("sp_y", 3 * i + 3))
                act.dma_start(y_d[i], yt[:]).then_inc(S["sp_stored"], 16)

            def split_hi(n0):
                with act.Fori(0, KD // 2) as i:
                    for j in range(2):
                        act.wait_ge(ld_in[j], 16 * i + (16 + 8 * n0))
                        act.activation(act_hi[:, 2 * i + j, :], stg[:, j, :], ACT.Copy).then_inc(S["ld_hi"], 1)

            act.wait_ge(S["blk"], 3 * G_A)
            split_hi(0)
            with act.Fori(0, KD // 2) as i:
                for j in range(2):
                    act.wait_ge(S["evac"], 6 * i + (3 * G_A + 3 * j + 3))
                    act.dma_start(za_d[2 * i + j], stg[:, j, :]).then_inc(stored[j], 16)

            for j in range(2):
                act.wait_ge(stored[j], 16 * 20)
            with act.Fori(0, H) as h:
                a0, d0, p0 = ACT_STEPS * h, DVE_STEPS * h, PE_STEPS * h

                def own(n):
                    act.wait_ge(S["ap_act"], at("ap_act", a0 + n))

                def dve(n):
                    act.wait_ge(S["ap_dve"], at("ap_dve", d0 + n))

                def products(n):
                    act.wait_ge(S["ap_pe"], at("ap_pe", p0 + n))

                def done(i_):
                    i_.then_inc(S["ap_act"], 1)

                products(3)
                done(act.activation(sq_k, lin_all(1), ACT.Square))
                products(6)
                done(act.activation(sq_q, lin_all(0), ACT.Square))
                done(act.activation(q_hi[:], lin_all(0), ACT.Copy, scale=gq))
                dve(2)
                done(act.activation(rk_s, rk_v, ACT.Sqrt))
                products(10)
                done(act.activation(sq_qr[0:ROPE], lin_all(1)[0:ROPE], ACT.Square))
                dve(8)
                done(act.activation(k_hi[:], kf[:], ACT.Copy))
                dve(9)
                done(act.activation(kr2[0:ROPE], rt3, ACT.Copy))
                done(act.activation(kr2[ROPE:P], rt3, ACT.Copy))
                dve(10)
                done(act.activation(qr2[0:ROPE], rt1, ACT.Copy))
                dve(14)
                done(act.activation(rq_s, rq_v, ACT.Sqrt))
                products(16)
                done(act.activation(v_hi[:], lin_all(1), ACT.Copy))

                def keys(c):
                    return TP if c < NCH_P else TS

                def expo(c):
                    n = keys(c)
                    act.wait_ge(S["nm_dve"], at("nm_dve", NCH * h + (c + 1)))
                    act.wait_ge(S["t_pe"], at("t_pe", NCH * h + (c - 1)))
                    act.activation(prob[:, c % 2, 0:n], bank(2 * (c % 2), n), ACT.Exp, bias=nmx[:, c:c + 1],
                                   scale=rq[:, c:c + 1], accum_out=psumr[:, c:c + 1]).then_inc(S["ex_act"], 1)

                def high(c):
                    n = keys(c) // P
                    o = (c % NCH_P) % 4 * P
                    act.wait_ge(S["t_pe"], at("t_pe", NCH * h + (c + 1)))
                    if c in (0, 4, 8):
                        act.wait_ge(S["pv_pe"], at("pv_pe", 3 * h + c // 4))
                    act.activation(pt_hi[:, 0:n, o:o + P], bank(4, n * P), ACT.Copy).then_inc(S["th_act"], 1)

                def out(b):
                    t0, tn = BLOCKS[b]
                    slot = b % 2
                    st = S[f"o_st{slot}"]
                    act.wait_ge(S["pv_pe"], at("pv_pe", 3 * h + (b + 1)))
                    act.wait_ge(st, 32 + (16 * h if slot else 32 * h + (16 if b else 0)))
                    act.activation(ostg[:, slot, 0:tn], bank(6 + slot, tn), ACT.Copy).then_inc(S["ov_act"], 1)
                    act.wait_ge(S["ov_act"], at("ov_act", 3 * h + (b + 1)))
                    act.dma_start(o_d[h][:, t0:t0 + tn], ostg[:, slot, 0:tn]).then_inc(st, 16)

                for c in range(NCH + 2):
                    if c > 1:
                        high(c - 2)
                    if c < NCH:
                        expo(c)
                    if c in (7, 11):
                        out(c // 4 - 1)
                out(2)

            act.wait_ge(S["pv_pe"], at("pv_pe", 3 * H))
            split_hi(KD)
            for j in range(2):
                act.wait_ge(S["z_mul"], at("z_mul", j + 1))
                act.dma_start(z_d[j], zt[:, j, :]).then_inc(stored[j], 16)
            with act.Fori(1, KD // 2) as i:
                for j in range(2):
                    act.wait_ge(S["z_mul"], at("z_mul", 2 * i + (j + 1)))
                    act.dma_start(z_d[2 * i + j], zt[:, j, :]).then_inc(stored[j], 16)
            split_hi(2 * KD)
            with act.Fori(0, KD // 2) as i:
                for j in range(2):
                    for b, (t0, tn) in enumerate(BLOCKS):
                        act.wait_ge(S["blk"], 3 * (2 * i + (G_OUT + j)) + (b + 1))
                        if b == 0:
                            act.wait_ge(S["ld_lo"], at("ld_lo", 3 * KD))
                            act.wait_ge(S["ot_pe"], at("ot_pe", 6 * i))
                        act.activation(stg[:, j, t0:t0 + tn], lin_set(j, b), ACT.Copy).then_inc(S["evac"], 1)
            act.wait_ge(S["x2_dve"], at("x2_dve", 3 * KD))
            for n in range(NCH):
                if n > 1:
                    act.wait_ge(S["r_ssq"], n - 1)
                act.activation(stg[:, n % 2, 0:D], x2[:, n, :], ACT.Square, accum_out=ssq2[:, n:n + 1]).then_inc(S["r_ssq"], 1)
            act.wait_ge(S["r_small"], 1)
            act.activation(std2, var2, ACT.Sqrt).then_inc(S["r_small"], 1)
            for n in range(NCH):
                act.wait_ge(S["r_h"], n + 1)
                act.dma_start(h_d.rearrange("(c p) d -> c p d", p=P)[n], h2[:, n % 2].rearrange("p k t -> p (k t)"))\
                    .then_inc(S[f"h_out{n % 2}"], 16)
                act.wait_ge(S["r_t"], n + 1)
                if n > 1:
                    act.wait_ge(S["rt_pe0"], n - 1)
                act.activation(h2T[:, n % 2], bank(2 * (n % 2), D), ACT.Copy).then_inc(S["r_hT"], 1)
            act.wait_ge(S["r_dve"], 2)
            act.activation(aff[:], lg[:], ACT.Exp).then_inc(S["r_exp"], 1)
            act.wait_ge(S["a_t"], 1)
            act.activation(affT[:], PS[0:E, 0:T], ACT.Copy).then_inc(S["a_T"], 1)

            def frame(e):
                is0, is1, is_last = (isinstance(e, int) and e == v for v in (0, 1, E))
                more = not (isinstance(e, int) and e >= E - 1)
                for n, (kind, ee, kk, q, slot) in enumerate(pieces(e)):
                    l = n + (8 if is_last else 0)
                    if is_last and n == 0:
                        out(e - 2)
                        hidden(e - 1)
                    act.wait_ge(S[f"e_in{slot}"], loads_of(e, n))
                    if not isinstance(q, int) or q >= 3:
                        act.wait_ge(S["e_pe"], q - 2)
                    pt = part(l, is0) if not is_last else q % 3
                    act.activation(ehi[:, pt], raw[:, slot], ACT.Copy).then_inc(S["e_hi"], 1)
                    if l == 1 and not (is0 or is1):
                        out(e - 2)
                    if l == 2 and not is0:
                        hidden(e - 1)
                    if l == 5:
                        act.wait_ge(S["e_pe"], q - 1)
                        if not is0:
                            act.wait_ge(S["ths_pe"], e)
                        act.activation(hid[:], bank(0, D), ACT.Silu).then_inc(S["silu_p"], 1)
                        act.activation(hid_s[:], bank(6, GN), ACT.Silu).then_inc(S["silu_s"], 1)
                    if more and l == (7 if is0 else 10):
                        rows_hi(e + 1)
                if is_last:
                    out(e - 1)

            def rows_hi(e):
                act.wait_ge(S["tx_pe"], e + 1)
                act.activation(xT_hi[:], bank(0, D), ACT.Copy).then_inc(S["xh_act"], 1)

            def hidden(e):
                act.wait_ge(S["th_pe"], e + 1)
                act.activation(hT_hi[:], bank(2, D), ACT.Copy).then_inc(S["hh_act"], 1)

            def out(e):
                act.wait_ge(S["e_pe"], 12 * E if isinstance(e, int) and e == E - 1 else 12 * e + 20)
                if not (isinstance(e, int) and e == 0):
                    act.wait_ge(S["scat"], 32 * e)
                act.activation(ob_p[:], bank(4, D), ACT.Copy, scale=gates[:, 0, bass.ds(e, 1)]).then_inc(S["ob_act"], 1)

            act.wait_ge(S["y_out"], 32)
            rows_hi(0)
            run_frames(act, frame)

        @block.vector
        def _(dve):
            dve.wait_ge(S["n1_ssq"], NCH)
            dve.tensor_scalar(var1, ssq1, 1.0 / D, EPS, ALU.mult, ALU.add).then_inc(S["n1_small"], 1)
            dve.wait_ge(S["n1_small"], 2)
            dve.reciprocal(rstd1, std1).then_inc(S["n1_small"], 1)
            dve.wait_ge(S["n1_small"], 3)
            dve.wait_ge(S["params"], 16 * 12)

            def scaled(n, j, free):
                if free is not None:
                    dve.wait_ge(S["n1_tr"], free)
                dve.tensor_scalar(xn[:, j], x_in[:, n, :], rstd1[:, n:n + 1] if isinstance(n, int) else rstd1[:, bass.ds(n, 1)],
                                  None, ALU.mult).then_inc(S["n1_xn"], 1)

            def gained(n, j):
                dve.wait_ge(S["n1_tr"], n + 1)
                if not isinstance(n, int) or n > 1:
                    dve.wait_ge(S["n1_lo"], n - 1)
                dve.tensor_tensor(htmp[:, j], bank(2 * j, D).rearrange("p (k t) -> p k t", k=KD),
                                  g1c.unsqueeze(2).to_broadcast([P, KD, P]), ALU.mult).then_inc(S["n1_h"], 1)

            scaled(0, 0, None)
            scaled(1, 1, None)
            gained(0, 0)
            scaled(2, 0, 1)
            gained(1, 1)
            scaled(3, 1, 2)
            with dve.Fori(1, NCH // 2 - 1) as i:
                for j in range(2):
                    gained(2 * i + j, j)
                    scaled(2 * i + (j + 2), j, 2 * i + (j + 1))
            gained(NCH - 2, 0)
            gained(NCH - 1, 1)

            def step(i_, n):
                i_.then_inc(S["c_dve"], 1)
                dve.wait_ge(S["c_dve"], n)
            step(dve.tensor_scalar(tab_k, tab_k, gkr, None, ALU.mult), 1)
            dve.wait_ge(S["evac"], 3 * 2)
            step(dve.tensor_tensor(rs_v[:], ct[:, 0, :], ct[:, 0, :], ALU.mult), 2)
            step(dve.tensor_tensor(acc_v[:], ct[:, 1, :], ct[:, 1, :], ALU.mult), 3)
            step(dve.tensor_tensor(rs_v[:], rs_v[:], acc_v[:], ALU.add), 4)
            dve.wait_ge(S["evac"], 3 * 3)
            step(dve.tensor_tensor(krf[:], ckv[:], ckv[:], ALU.mult), 5)
            dve.wait_ge(S["evac"], 3 * 4)
            step(dve.tensor_tensor(sq_kr[0:ROPE], ct[0:ROPE, 2, :], ct[0:ROPE, 2, :], ALU.mult), 6)
            step(dve.memset(acc_v[:], 0.0), 7)
            with dve.Fori(0, KD // 2) as i:
                for j in range(2):
                    dve.wait_ge(S["evac"], 6 * i + (3 * (G_V + j) + 3))
                    dve.tensor_tensor(sq_v, stg[:, j, :], stg[:, j, :], ALU.mult).then_inc(S["v_sq"], 1)
                    dve.wait_ge(S["v_sq"], 2 * i + (j + 1))
                    dve.tensor_tensor(acc_v[:], acc_v[:], sq_v, ALU.add).then_inc(S["v_acc"], 1)
                    dve.wait_ge(S["v_acc"], 2 * i + (j + 1))
            dve.wait_ge(S["c_stev"], 3)
            step(dve.reciprocal(rs_v[:], rs_v[:]), 8)
            for m in range(2):
                step(dve.tensor_tensor(ct[:, m, :], ct[:, m, :], rs_v[:], ALU.mult), 9 + m)
            dve.wait_ge(S["c_stev"], 6)
            step(dve.reciprocal(krf[:], krf[:]), 11)
            step(dve.tensor_tensor(ckv[:], ckv[:], krf[:], ALU.mult), 12)
            step(dve.tensor_scalar(ckv[:], ckv[:], gkvn, None, ALU.mult), 13)
            step(dve.tensor_tensor(krf[0:ROPE], ct[0:ROPE, 2, :], tab_k[0:ROPE], ALU.mult), 14)
            step(dve.tensor_tensor(ct[0:ROPE, 2, :], ct[ROPE:P, 2, :], tab_k[ROPE:P], ALU.mult), 15)
            step(dve.tensor_tensor(krf[0:ROPE], krf[0:ROPE], ct[0:ROPE, 2, :], ALU.add), 16)
            for m in range(2):
                dve.wait_ge(S["c_act"], m + 1)
                step(dve.scalar_tensor_tensor(out=cq_lo[:, m], in0=ct[:, m, :], scalar=gqn[:, m:m + 1],
                                              in1=f32(cq_hi[:, m]), op0=ALU.mult, op1=ALU.subtract), 17 + m)
            dve.wait_ge(S["c_act"], 3)
            step(dve.tensor_tensor(ckv_lo[:], ckv[:], f32(ckv_hi[:]), ALU.subtract), 19)
            dve.wait_ge(S["params"], 16 * 13)
            dve.wait_ge(S["c_stev"], 9)
            step(dve.tensor_scalar(tab_q[:], tab_q[:], gqr, None, ALU.mult), 20)
            step(dve.reciprocal(rs_v[:], rs_v[:]), 21)

            with dve.Fori(0, KD) as i:
                dve.wait_ge(S["sp_vin"], 16 * i + 16)
                dve.tensor_tensor(vt[:], vt[:], rs_v[:], ALU.mult).then_inc(S["sp_vn"], 1)
                dve.wait_ge(S["sp_bin"], 32 * i + 32)
                dve.wait_ge(S["sp_uin"], 16 * i + 16)
                dve.wait_ge(S["sp_stored"], at("sp_stored", 16 * i))
                for b, (t0, tn) in enumerate(BLOCKS):
                    dve.wait_ge(S["sp_m"], at("sp_m", 3 * i + (b + 1)))
                    dve.scalar_tensor_tensor(
                        out=yt[:, t0:t0 + tn].rearrange("p (c q) -> p c q", q=P),
                        in0=bank(7 - b % 2, tn).rearrange("p (c q) -> p c q", q=P), scalar=vg,
                        in1=bb[:].unsqueeze(1).to_broadcast([P, tn // P, P]), op0=ALU.mult,
                        op1=ALU.add).then_inc(S["sp_act"], 1)
                    dve.wait_ge(S["sp_act"], at("sp_act", 3 * i + (b + 1)))
                    dve.tensor_tensor(yt[:, t0:t0 + tn], yt[:, t0:t0 + tn], ut[:, t0:t0 + tn],
                                      ALU.mult).then_inc(S["sp_y"], 1)

            def split_lo(n0):
                with dve.Fori(0, KD // 2) as i:
                    for j in range(2):
                        dve.wait_ge(S["ld_hi"], 2 * i + (n0 + j + 1))
                        dve.tensor_tensor(act_lo[:, 2 * i + j, :], stg[:, j, :], f32(act_hi[:, 2 * i + j, :]),
                                          ALU.subtract).then_inc(S["ld_lo"], 1)

            split_lo(0)
            dve.wait_ge(S["ld_lo"], at("ld_lo", KD))
            def gate_a(i, j, g, uses):
                dve.wait_ge(gt_in[j], 16 * i + 16)
                if uses is not None:
                    dve.wait_ge(stored[j], uses)
                for b, (t0, tn) in enumerate(BLOCKS):
                    dve.wait_ge(S["blk"], 3 * g + (b + 1))
                    dve.tensor_tensor(stg[:, j, t0:t0 + tn], lin_set(j, b), gt[:, j, t0:t0 + tn],
                                      ALU.mult).then_inc(S["evac"], 1)
            with dve.Fori(0, KD // 2) as i:
                for j in range(2):
                    gate_a(i, j, 2 * i + (G_A + j), 16 * i + 16 * 2 * KD)

            dve.wait_ge(S["blk"], 3 * G_B)
            dve.memset(f32(krl[ROPE:P]), 0.0).then_inc(S["c_dve"], 1)
            with dve.Fori(0, H) as h:
                a0, d0, p0 = ACT_STEPS * h, DVE_STEPS * h, PE_STEPS * h

                def own(n):
                    dve.wait_ge(S["ap_dve"], at("ap_dve", d0 + n))

                def acts(n):
                    dve.wait_ge(S["ap_act"], at("ap_act", a0 + n))

                def products(n):
                    dve.wait_ge(S["ap_pe"], at("ap_pe", p0 + n))

                def done(i_):
                    i_.then_inc(S["ap_dve"], 1)

                acts(1)
                done(dve.tensor_scalar(kf[:], lin_all(1), gk, None, ALU.mult))
                products(7)
                done(dve.tensor_scalar(rk_v, bank(6, NCH), 1.0 / HEAD, EPS, ALU.mult, ALU.add))
                acts(3)
                done(dve.scalar_tensor_tensor(out=q_lo[:], in0=lin_all(0), scalar=gq, in1=f32(q_hi[:]),
                                              op0=ALU.mult, op1=ALU.subtract))
                acts(4)
                done(dve.reciprocal(rk_r, rk_s))
                own(4)
                done(dve.tensor_tensor(diag[:].rearrange("p (c t) -> p c t", t=P),
                                       ident[:].unsqueeze(1).to_broadcast([P, NCH, P]),
                                       rk_r.unsqueeze(2).to_broadcast([P, NCH, P]), ALU.mult))
                acts(5)
                done(dve.tensor_tensor(rt1, lin_all(1)[0:ROPE], tab_q[0:ROPE], ALU.mult))
                done(dve.tensor_tensor(rt2, lin_all(1)[ROPE:P], tab_q[ROPE:P], ALU.mult))
                products(13)
                done(dve.tensor_tensor(kf[:], kf[:], lin_all(0), ALU.mult))
                done(dve.tensor_tensor(rt3, krf[0:ROPE], lin_all(0)[0:ROPE], ALU.mult))
                own(9)
                done(dve.tensor_tensor(rt1, rt1, rt2, ALU.add))
                acts(6)
                done(dve.tensor_tensor(k_lo[:], kf[:], f32(k_hi[:]), ALU.subtract))
                acts(7)
                done(dve.tensor_tensor(krl[0:ROPE], rt3, f32(kr2[0:ROPE]), ALU.subtract))
                acts(9)
                done(dve.tensor_tensor(qr2[ROPE:P], rt1, f32(qr2[0:ROPE]), ALU.subtract))
                products(17)
                done(dve.tensor_scalar(rq_v, bank(7, NCH), 1.0 / HEAD, EPS, ALU.mult, ALU.add))
                acts(10)
                done(dve.reciprocal(rq_r, rq_s))
                own(15)
                done(dve.tensor_scalar(rq, rq_r, SCALE, None, ALU.mult))
                acts(11)
                done(dve.tensor_tensor(v_lo[:], lin_all(1), f32(v_hi[:]), ALU.subtract))
                own(17)

                def keys(c):
                    return TP if c < NCH_P else TS

                def top(c):
                    n = keys(c)
                    dve.wait_ge(S["qk_pe"], at("qk_pe", NCH * h + (c + 1)))
                    dve.tensor_reduce(mx[:, c:c + 1], bank(2 * (c % 2), n), AX_X, ALU.max).then_inc(S["mx_dve"], 1)
                    dve.wait_ge(S["mx_dve"], at("mx_dve", NCH * h + (c + 1)))
                    dve.tensor_scalar(nmx[:, c:c + 1], mx[:, c:c + 1], rq[:, c:c + 1], -1.0, ALU.mult,
                                      ALU.mult).then_inc(S["nm_dve"], 1)

                def norm(c):
                    n = keys(c)
                    dve.wait_ge(S["ex_act"], at("ex_act", NCH * h + (c + 1)))
                    dve.reciprocal(prec[:, c:c + 1], psumr[:, c:c + 1]).then_inc(S["rc_dve"], 1)
                    dve.wait_ge(S["rc_dve"], at("rc_dve", NCH * h + (c + 1)))
                    dve.tensor_scalar(prob[:, c % 2, 0:n], prob[:, c % 2, 0:n], prec[:, c:c + 1], None,
                                      ALU.mult).then_inc(S["pr_dve"], 1)

                def low(c):
                    n = keys(c) // P
                    o = (c % NCH_P) % 4 * P
                    dve.wait_ge(S["th_act"], at("th_act", NCH * h + (c + 1)))
                    dve.tensor_tensor(pt_lo[:, 0:n, o:o + P], bank(4, n * P).rearrange("p (k q) -> p k q", q=P),
                                      f32(pt_hi[:, 0:n, o:o + P]), ALU.subtract).then_inc(S["tl_dve"], 1)

                for c in range(NCH + 2):
                    if c < NCH:
                        top(c)
                    if c > 1:
                        low(c - 2)
                    if c < NCH:
                        norm(c)

            split_lo(KD)
            def gate_b(i, j, g):
                dve.wait_ge(gt_in[j], 16 * i + (16 * KD // 2 + 16))
                dve.wait_ge(zt_in[j], 16 * i + 16)
                for b, (t0, tn) in enumerate(BLOCKS):
                    dve.wait_ge(S["blk"], 3 * g + (b + 1))
                    dve.tensor_tensor(gt[:, j, t0:t0 + tn], lin_set(j, b), gt[:, j, t0:t0 + tn],
                                      ALU.mult).then_inc(S["evac"], 1)
                dve.wait_ge(S["evac"], 3 * g + 3)
                dve.tensor_tensor(zt[:, j, :], zt[:, j, :], gt[:, j, :], ALU.add).then_inc(S["z_mul"], 1)
            with dve.Fori(0, KD // 2) as i:
                for j in range(2):
                    gate_b(i, j, 2 * i + (G_B + j))
            split_lo(2 * KD)
            dve.wait_ge(S["x2_in"], 32)
            with dve.Fori(0, KD // 2) as i:
                for j in range(2):
                    m = 2 * i + j
                    for b, (t0, tn) in enumerate(BLOCKS):
                        dve.wait_ge(S["ot_pe"], at("ot_pe", 3 * m + (b + 1)))
                        x = x2[:, t0 // P:(t0 + tn) // P, bass.ds(m * P, P)]
                        dve.tensor_tensor(x, bank(6 + (3 * j + b) % 2, tn).rearrange("p (c q) -> p c q", q=P), x,
                                          ALU.add).then_inc(S["x2_dve"], 1)
            dve.wait_ge(S["r_ssq"], NCH)
            dve.wait_ge(S["r_in"], 32)
            dve.tensor_scalar(var2, ssq2, 1.0 / D, EPS, ALU.mult, ALU.add).then_inc(S["r_small"], 1)
            dve.wait_ge(S["r_small"], 2)
            dve.reciprocal(rstd2, std2).then_inc(S["r_small"], 1)
            dve.wait_ge(S["r_small"], 3)
            for n in range(NCH):
                if n > 1:
                    dve.wait_ge(S["r_t"], n - 1)
                    dve.wait_ge(S[f"h_out{n % 2}"], 16 * (n // 2))
                dve.scalar_tensor_tensor(out=h2[:, n % 2].rearrange("p k t -> p (k t)"), in0=x2[:, n, :],
                                         scalar=rstd2[:, n:n + 1], in1=g2b[:], op0=ALU.mult,
                                         op1=ALU.mult).then_inc(S["r_h"], 1)

            def rstep(i_, n):
                i_.then_inc(S["r_dve"], 1)
                dve.wait_ge(S["r_dve"], n)
            dve.wait_ge(S["rt_pe0"], NCH)
            logit = bank(6, NCH * E).rearrange("p (c e) -> p c e", e=E)
            rstep(dve.tensor_reduce(lmx, logit, AX_X, ALU.max), 1)
            rstep(dve.tensor_tensor(lg[:], logit, lmx.unsqueeze(2).to_broadcast([P, NCH, E]), ALU.subtract), 2)
            dve.wait_ge(S["r_exp"], 1)
            rstep(dve.tensor_reduce(lsum, aff[:], AX_X, ALU.add), 3)
            rstep(dve.reciprocal(lrec, lsum), 4)
            rstep(dve.tensor_tensor(aff[:], aff[:], lrec.unsqueeze(2).to_broadcast([P, NCH, E]), ALU.mult), 5)

            dve.wait_ge(S["a_T"], 1)
            count = [0]

            def kstep(i_):
                count[0] += 1
                i_.then_inc(S["tk"], 1)
                dve.wait_ge(S["tk"], count[0])
            for grp, (t0, tn, cap) in enumerate(((0, TP, CAP_P), (TP, TS, CAP_S))):
                work = affT[:, t0:t0 + tn]
                for r in range(cap // 8):
                    v, x = topv[:, grp, 8 * r:8 * r + 8], topi[:, grp, 8 * r:8 * r + 8]
                    kstep(dve.max(v, work))
                    kstep(dve.max_index(x, v, work))
                    kstep(dve.match_replace(work, v, work, -1.0))
            kstep(dve.tensor_copy(topv[:, 1, CAP_S:P].rearrange("e (g c) -> e g c", c=CAP_S),
                                  topv[:, 1, 0:CAP_S].unsqueeze(1).to_broadcast([E, GRP - 1, CAP_S])))
            kstep(dve.tensor_copy(topi[:, 1, CAP_S:P].rearrange("e (g c) -> e g c", c=CAP_S),
                                  topi[:, 1, 0:CAP_S].unsqueeze(1).to_broadcast([E, GRP - 1, CAP_S])))
            kstep(dve.tensor_copy(topf[:], topi[:]))
            dve.wait_ge(S["rt_pe"], 4)
            for n in range(2):
                dve.tensor_copy(gates[:, n], bank(3)[:, n * E:(n + 1) * E]).then_inc(S["rows_s"], 1)
                dve.tensor_copy(rows[:, n], bank(3)[:, (n + 2) * E:(n + 3) * E]).then_inc(S["rows_s"], 1)
            dve.tensor_scalar(rows[:, 2], bank(3)[:, 3 * E:4 * E], float(TP), None, ALU.add).then_inc(S["rows_s"], 1)
            dve.wait_ge(S["rows_s"], 5)
            dve.wait_ge(S["y_out"], 32)

            def frame(e):
                is0, is1, is_last = (isinstance(e, int) and e == v for v in (0, 1, E))
                more = not (isinstance(e, int) and e >= E - 1)
                for n, (kind, ee, kk, q, slot) in enumerate(pieces(e)):
                    l = n + (8 if is_last else 0)
                    if is_last and n == 0:
                        out(e - 2)
                        hidden(e - 1)
                    dve.wait_ge(S["e_hi"], q + 1)
                    pt = part(l, is0) if not is_last else q % 3
                    dve.tensor_tensor(elo[:, pt], raw[:, slot], f32(ehi[:, pt]), ALU.subtract).then_inc(S["e_lo"], 1)
                    if l == 1 and not (is0 or is1):
                        out(e - 2)
                    if l == 2 and not is0:
                        hidden(e - 1)
                    if l == (7 if is0 else 9) and not is_last:
                        gated(e)
                    if more and l == (7 if is0 else 10):
                        rows_lo(e + 1)
                if is_last:
                    out(e - 1)

            def gated(e):
                dve.wait_ge(S["e_pe"], 8 if isinstance(e, int) and e == 0 else 12 * e + 4)
                dve.wait_ge(S["silu_p"], e + 1)
                dve.wait_ge(S["silu_s"], e + 1)
                dve.tensor_tensor(hid[:], bank(2, D), hid[:], ALU.mult).then_inc(S["mul_p"], 1)
                dve.tensor_tensor(hid_s[:], bank(7, GN), hid_s[:], ALU.mult).then_inc(S["mul_s"], 1)

            def rows_lo(e):
                dve.wait_ge(S["xh_act"], e + 1)
                dve.tensor_tensor(xT_lo[:], bank(0, D).rearrange("p (k t) -> p k t", k=KD), f32(xT_hi[:]),
                                  ALU.subtract).then_inc(S["xl_dve"], 1)
                dve.wait_ge(S["txs_pe"], e + 1)
                dve.tensor_copy(xT_s[:], bank(7, GN).rearrange("p (k t) -> p k t", k=KD)).then_inc(S["xs_dve"], 1)

            def hidden(e):
                dve.wait_ge(S["hh_act"], e + 1)
                dve.tensor_tensor(hT_lo[:], bank(2, D).rearrange("p (k t) -> p k t", k=KD), f32(hT_hi[:]),
                                  ALU.subtract).then_inc(S["hl_dve"], 1)
                dve.wait_ge(S["ths_pe"], e + 1)
                dve.tensor_copy(hT_s[:], bank(7, GN)).then_inc(S["hs_dve"], 1)

            def out(e):
                dve.wait_ge(S["e_pe"], 12 * E if isinstance(e, int) and e == E - 1 else 12 * e + 20)
                if not (isinstance(e, int) and e == 0):
                    dve.wait_ge(S["scat"], 32 * e)
                for g in range(GRP):
                    r = slice(CAP_S * g, CAP_S * (g + 1))
                    last = dve.tensor_scalar(ob_s[:, g * GN:(g + 1) * GN], bank(6, GN)[r], gates[r, 1, bass.ds(e, 1)],
                                             None, ALU.mult)
                last.then_inc(S["ob_dve"], 1)

            rows_lo(0)
            run_frames(dve, frame)


_INS = ['x_prompt', 'x_sample', 'norm1_g', 'w_in', 'v_norm_g', 'w_spatial', 'b_spatial', 'w_a_out',
        'q_norm_g', 'w_uq', 'kv_norm_g', 'w_ukv', 'q_head_g', 'k_head_g', 'w_b_out', 'w_out',
        'norm2_g', 'w_router', 'w_gate', 'w_up', 'w_down']


def rope_table():
    import numpy as np
    half = ROPE // 2
    freq = (np.float32(10000.0) ** (-np.arange(half, dtype=np.float32) / np.float32(half))).astype(np.float32)
    pos = np.concatenate([np.arange(TP), np.arange(TS)]).astype(np.float32)
    ang = (freq[:, None] * pos[None, :]).astype(np.float32).astype(np.float64)
    c, s = np.cos(ang), np.sin(ang)
    return np.ascontiguousarray(np.concatenate([c, c, -s, s]).astype(np.float32))


def kernel(**inputs):
    import numpy as np
    import concourse.bacc as bacc
    from concourse.bass_utils import run_bass_kernel_spmd

    nc = bacc.Bacc("TRN2", target_bir_lowering=False, num_devices=1)
    arrays, args = {}, []
    for name in _INS:
        a = np.ascontiguousarray(inputs[name])
        a = a.reshape(a.shape[1:])
        arrays[f"in_{name}"] = a
    arrays["rope_cs"] = rope_table()
    for name, a in arrays.items():
        args.append(nc.dram_tensor(name, a.shape, mybir.dt.from_np(a.dtype), kind="ExternalInput").ap())
    args.append(nc.dram_tensor("y_p", (TP, D), F32, kind="ExternalOutput").ap())
    args.append(nc.dram_tensor("y_s", (TS, D), F32, kind="ExternalOutput").ap())
    build(nc, *args)
    r = run_bass_kernel_spmd(nc, [arrays], core_ids=[0])
    return (r.results[0]["y_p"].reshape(1, TP, D), r.results[0]["y_s"].reshape(1, TS, D))
```

```python
from contextlib import ExitStack

import concourse.bass as bass
from concourse import mybir

F32 = mybir.dt.float32
F32R = mybir.dt.float32r
U32 = mybir.dt.uint32
ALU = mybir.AluOpType
ACT = mybir.ActivationFunctionType
AX_X = mybir.AxisListType.X

P = 128
D = 1024
KD = D // P
TP, TS = 1024, 256
T = TP + TS
NCH = T // P
NCH_P = TP // P
BLOCKS = [(0, 512), (512, 512), (1024, 256)]
BANK = 512
H = 8
NOPE, ROPE = 128, 64
HEAD = NOPE + ROPE
QR, KVR = 256, 128
OFF_CQ = 2 * D
OFF_KR = OFF_CQ + QR + KVR
OFF_GA = OFF_KR + ROPE
EPS = 1e-6
SCALE = float(HEAD) ** -0.5
E = 16
CAP_P, CAP_S = 2 * TP // E, 2 * TS // E
GRP = P // CAP_S
GN = D // GRP
QN = 2 * P
QS = D // QN

G_C, G_V, G_U, G_GATE, G_A, G_B, G_OUT = 0, 4, 12, 20, 36, 44, 52


def build(nc, x_p, x_s, norm1_g, w_in, v_norm_g, w_spatial, b_spatial, w_a_out, q_norm_g, w_uq,
          kv_norm_g, w_ukv, q_head_g, k_head_g, w_b_out, w_out, norm2_g, w_router, w_gate, w_up,
          w_down, rope_cs, y_p, y_s):
    ctx = ExitStack()
    with ctx:
        def sem(name):
            return ctx.enter_context(nc.semaphore(name))

        def sb(stack, name, shape, dt=F32):
            return stack.enter_context(nc.sbuf_tensor(name, shape, dt))

        def f32(ap):
            return ap.bitcast(F32)

        v_d = nc.dram_tensor("v_d", [KD, P, T], F32).ap()
        u_d = nc.dram_tensor("u_d", [KD, P, T], F32).ap()
        g_d = nc.dram_tensor("g_d", [2 * KD, P, T], F32).ap()
        y_d = nc.dram_tensor("ya_d", [KD, P, T], F32).ap()
        za_d = nc.dram_tensor("za_d", [KD, P, T], F32).ap()
        o_d = nc.dram_tensor("o_d", [H, P, T], F32).ap()
        h_d = nc.dram_tensor("h_d", [T, D], F32).ap()

        PS = ctx.enter_context(nc.psum_tensor("PS", [P, 8 * BANK], F32))

        def bank(b, n=BANK, w=1):
            return PS[:, b * BANK:b * BANK + n * w]

        def lin_set(j, b):
            o = 3 * BANK * j + BLOCKS[b][0]
            return PS[:, o:o + BLOCKS[b][1]]

        def lin_all(j):
            return PS[:, 3 * BANK * j:3 * BANK * j + T]

        ident = sb(ctx, "ident", [P, P])
        ones = sb(ctx, "ones", [P, P])
        small = sb(ctx, "small", [P, 256])
        g1c = small[:, 0:8]
        gqn = small[:, 8:10]
        gkvn = small[:, 10:11]
        gq = small[:, 11:12]
        gqr = small[:, 12:13]
        gk = small[:, 13:14]
        gkr = small[:, 14:15]
        ssq1 = small[:, 16:26]
        rstd1 = small[:, 36:46]
        std1 = small[:, 46:56]
        ssq2 = small[:, 56:66]
        rstd2 = small[:, 76:86]
        std2 = small[:, 86:96]
        rq_v = small[:, 96:106]
        rq_s = small[:, 106:116]
        rq_r = small[:, 116:126]
        rq = small[:, 126:136]
        mx = small[:, 136:146]
        nmx = small[:, 146:156]
        psumr = small[:, 156:166]
        prec = small[:, 166:176]
        lmx = small[:, 176:186]
        lsum = small[:, 186:196]
        lrec = small[:, 196:206]
        vg = small[:, 206:207]
        gcol_p = small[:, 207:208]
        gcol_s = small[:, 208:209]
        epsc = small[:, 209:210]
        rk_v = small[:, 210:220]
        rk_s = small[:, 220:230]
        kr_sum = small[:, 241:251]
        rk_r = small[:, 230:240]
        spare = small[:, 240:241]


        w_raw = sb(ctx, "w_raw", [P, 2, KD, P])
        w_hi = sb(ctx, "w_hi", [P, 2, KD, P], F32R)
        w_lo = sb(ctx, "w_lo", [P, 2, KD, P], F32R)
        stg = sb(ctx, "stg", [P, 2, T])
        gt = sb(ctx, "gt", [P, 2, T])

        region_a = 2 * KD * T * 4
        with ExitStack() as s:
            act_hi = sb(s, "act_hi", [P, KD, T], F32R)
            act_lo = sb(s, "act_lo", [P, KD, T], F32R)
            with ExitStack() as s2:
                x_in = sb(s2, "x_in", [P, NCH, D])
                xn = sb(s2, "xn", [P, 2, D])
                htmp = sb(s2, "htmp", [P, 2, KD, P])
            with ExitStack() as s2:
                tab_q = sb(s2, "tab_q", [P, T])
                cq_hi = sb(s2, "cq_hi", [P, 2, T], F32R)
                cq_lo = sb(s2, "cq_lo", [P, 2, T], F32R)
                ckv = sb(s2, "ckv", [P, T])
                krf = sb(s2, "krf", [P, T])
                sq_kr = sb(s2, "sq_kr", [P, T])
                ckv_hi = sb(s2, "ckv_hi", [P, T], F32R)
                ckv_lo = sb(s2, "ckv_lo", [P, T], F32R)
                with ExitStack() as s3:
                    rs_v = sb(s3, "rs_v", [P, T])
                    with ExitStack() as s4:
                        acc_v = sb(s4, "acc_v", [P, T])
                        ct = sb(s4, "ct", [P, 3, T])
                    with ExitStack() as s4:
                        vt = sb(s4, "vt", [P, T])
                        vtok = sb(s4, "vtok", [P, T])
                        yt = sb(s4, "yt", [P, T])
                        ws = sb(s4, "ws", [P, P])
                        wsT = sb(s4, "wsT", [P, P])
                        bb = sb(s4, "bb", [P, P])
                with ExitStack() as s3:
                    aq_raw = sb(s3, "aq_raw", [P, 2, 256])
                    aq_hi = sb(s3, "aq_hi", [P, 2, 256], F32R)
                    aq_lo = sb(s3, "aq_lo", [P, 2, 256], F32R)
                    akv_raw = sb(s3, "akv_raw", [P, 256])
                    ak_hi = sb(s3, "ak_hi", [P, P], F32R)
                    ak_lo = sb(s3, "ak_lo", [P, P], F32R)
                    kf = sb(s3, "kf", [P, T])
                    diag = sb(s3, "diag", [P, T])
                    prob = sb(s3, "prob", [P, 2, TP])
                    ostg = sb(s3, "ostg", [P, 2, BANK])
            with ExitStack() as s2:
                o_all = sb(s2, "o_all", [P, KD, T])
                z_all = sb(s2, "z_all", [P, KD, T])
            with ExitStack() as s2:
                with ExitStack() as s3:
                    x2 = sb(s3, "x2", [P, NCH, D])
                with ExitStack() as s3:
                    xs_p = sb(s3, "xs_p", [P, D])
                    xs_s = sb(s3, "xs_s", [CAP_S, D])
                    xT_hi = sb(s3, "xT_hi", [P, KD, P], F32R)
                    xT_lo = sb(s3, "xT_lo", [P, KD, P], F32R)
                    hT_hi = sb(s3, "hT_hi", [P, KD, P], F32R)
                    hT_lo = sb(s3, "hT_lo", [P, KD, P], F32R)
                    hid = sb(s3, "hid", [P, D])
                    ob_p = sb(s3, "ob_p", [P, D])
                    ob_s = sb(s3, "ob_s", [CAP_S, D])
                    xT_s = sb(s3, "xT_s", [P, KD, CAP_S])
                    hid_s = sb(s3, "hid_s", [P, GN])
                    hT_s = sb(s3, "hT_s", [P, GN])
                    ixg_p = sb(s3, "ixg_p", [P, 1], U32)
                    ixg_s = sb(s3, "ixg_s", [CAP_S, 1], U32)
                    ixs_p = sb(s3, "ixs_p", [P, 1], U32)
                    ixs_s = sb(s3, "ixs_s", [CAP_S, 1], U32)
                x2_end = sb(s2, "x2_room", [P, NCH, D])
                g2b = sb(s2, "g2b", [P, D])
                wr = sb(s2, "wr", [P, KD, E])
                lg = sb(s2, "lg", [P, NCH, E])
                aff = sb(s2, "aff", [P, NCH, E])
                affT = sb(s2, "affT", [E, T])
                topv = sb(s2, "topv", [E, 2, P])
                topi = sb(s2, "topi", [E, 2, P], U32)
                topf = sb(s2, "topf", [E, 2, P])
                gates = sb(s2, "gates", [P, 2, E])
                rows = sb(s2, "rows", [P, 3, E], U32)
                w2_hi = sb(s2, "w2_hi", [P, 2, KD, P], F32R)
                w2_lo = sb(s2, "w2_lo", [P, 2, KD, P], F32R)
        with ExitStack() as s:
            q_hi = sb(s, "q_hi", [P, T], F32R)
            q_lo = sb(s, "q_lo", [P, T], F32R)
            qr2 = sb(s, "qr2", [P, T], F32R)
            k_hi = sb(s, "k_hi", [P, T], F32R)
            k_lo = sb(s, "k_lo", [P, T], F32R)
            kr2 = sb(s, "kr2", [P, T], F32R)
            krl = sb(s, "krl", [P, T], F32R)
            v_hi = sb(s, "v_hi", [P, T], F32R)
            v_lo = sb(s, "v_lo", [P, T], F32R)
            pt_hi = sb(s, "pt_hi", [P, NCH_P, BANK], F32R)
            pt_lo = sb(s, "pt_lo", [P, NCH_P, BANK], F32R)
        with ExitStack() as s:
            raw = sb(s, "raw", [P, 4, 2, D])
            ehi = sb(s, "ehi", [P, 3, 2, D], F32R)
            elo = sb(s, "elo", [P, 3, 2, D], F32R)
        h2, h2T = w_raw[:, :, :, :], gt[:, :, 0:D]
        tab_k, sq_v = gt[:, 0, :], gt[:, 1, :]
        ut = gt[:, 0, :]
        sq_q, sq_qr, sq_k = stg[:, 0, :], gt[:, 0, :], gt[:, 1, :]
        rt1, rt2 = stg[0:ROPE, 1, :], prob[:, :, :].rearrange("p a n -> p (a n)")[0:ROPE, 0:T]
        rt3 = diag[0:ROPE, :]

        names = """consts params g1_in tab_in n1_ssq n1_std n1_rec n1_xn n1_tr n1_h n1_hi n1_lo_even n1_lo_odd
            w_in0 w_in1 w_hi_s w_lo_s blk evac stored0 stored1 v_sq v_acc
            c_dve c_act c_sta c_stev
            sp_vin sp_wsin sp_uin sp_bin sp_vn sp_t sp_tok sp_m sp_act sp_y sp_stored
            ld_in0 ld_in1 ld_hi ld_lo gt_in0 gt_in1 o_back o_back_last za_in0 za_in1 z_sum
            aw_in aw_hi aw_lo ap_pe ap_act ap_dve kr_pe krl_pool
            qk_pe mx_dve nm_dve ex_act rc_dve pr_act pr_dve t_pe th_act tl_dve pv_pe ov_act o_st0 o_st1
            x2_in out_pe x2_dve
            r_in rt_pe0 r_ssq r_std r_rec r_h r_t r_hT r_exp r_dve y_out h_out0 h_out1 a_t a_T tk rt_pe rows_s
            e_in0 e_in1 e_in2 e_in3 e_hi e_lo e_pe g_ap g_as u_ap u_as d_ap d_as
           ix_g ix_s gath tx_pe txs_pe xh_act xl_dve xs_dve silu_p silu_s mul_p mul_s th_pe ths_pe hh_act
            hl_dve hs_dve ob_act ob_dve scat passed_pool passed_pe""".split()
        S = {n: sem(n) for n in names}
        credit = {n: 2 for n in """sp_t sp_y sp_m sp_act sp_tok sp_vn aw_lo aw_hi ap_pe ap_act ap_dve
            qk_pe mx_dve nm_dve ex_act rc_dve pr_act pr_dve t_pe th_act tl_dve pv_pe ov_act ld_lo
            z_sum""".split()}
        credit.update(o_st0=32, o_st1=32, sp_stored=32)

        def at(name, n):
            return n + credit.get(name, 0)

        w_in_s = [S["w_in0"], S["w_in1"]]
        stored = [S["stored0"], S["stored1"]]
        x_in_s = [sem(f"x_loaded{n}") for n in range(5)]
        ld_in = [S["ld_in0"], S["ld_in1"]]
        gt_in = [S["gt_in0"], S["gt_in1"]]

        def mm3(pe, out, lh, ll, rh, rl, first, last):
            pe.matmul(out, lh, rh, start=first, stop=False)
            pe.matmul(out, lh, rl, start=False, stop=False)
            return pe.matmul(out, ll, rh, start=False, stop=last)

        w_in_v = w_in.rearrange("(k p) n -> p k n", p=P)
        x_view = [x_p.rearrange("(c p) d -> p c d", p=P), x_s.rearrange("(c p) d -> p c d", p=P)]

        def w_tile(kind, m):
            if kind in "vug":
                first = {"v": D, "u": 0, "g": OFF_GA}[kind]
                return w_in_v[:, :, bass.ds(m * P + first, P)]
            w = {"a": w_a_out, "b": w_b_out, "o": w_out}[kind]
            return w.rearrange("(k p) n -> p k n", p=P)[:, :, bass.ds(m * P, P)]

        def pieces(e):
            first, last = isinstance(e, int) and e == 0, isinstance(e, int) and e == E
            q0 = 0 if first else 12 * e - 4
            out = []
            if not last:
                out += [("g", e, l, l) for l in range(4)] + [("u", e, l, l + 4) for l in range(4)]
            if not first:
                out += [("d", e - 1, l, (l if last else l + 8)) for l in range(4)]
            return [(kind, ee, kk, q0 + l, l % 4) for kind, ee, kk, l in out]

        def part(l, first):
            return l % 3 if first else (l + 2) % 3

        def loads_of(e, n):
            if isinstance(e, int):
                return 16 * ((0 if e == 0 else 12 * e - 4) + n + 4 >> 2)
            return 48 * e + (16 * (n // 4))

        def run_frames(eng, frame):
            frame(0)
            frame(1)
            with eng.Fori(2, E - 1) as e:
                frame(e)
            frame(E - 1)
            frame(E)

        def numbered(steps):
            out, n = {}, 0
            for step in steps.split():
                name, _, width = step.partition(":")
                n += int(width or 1)
                out[name] = n
            return out, n
        PE_STEP, PE_STEPS = numbered("k:3 q:3 sum_k v:3 scale_k:3 qr0 qr1 qr2 sum_q")
        ACT_STEP, ACT_STEPS = numbered(
            "sqrt_table sq_k kf sq_q q_hi rk_s v_hi sq_qr0 k_hi sq_qr1 kr2_up sq_qr2 kr2_down qr2_up rq_s exp_table")
        DVE_STEP, DVE_STEPS = numbered("rk_v q_lo rk_r diag v_lo kf rt3 rt_0:2 k_lo rt_1:2 rt_2:2 rt1 qr2_down rq_sum rq_v rq_r rq")

        def s_bank(c):
            return 3 if c == NCH - 1 else 2 * (c % 2)

        def t_bank(c):
            return 5 if c == NCH - 1 else 4

        block = ctx.enter_context(nc.Block())

        @block.sync
        def _(sp):
            def load_w(g, j, view):
                sp.wait_ge(S["w_lo_s"], g - 1)
                sp.dma_start(w_raw[:, j], view).then_inc(w_in_s[j], 16)

            col = lambda a: a.rearrange("(p o) -> p o", o=1)
            for n in range(5):
                src = x_view[0][:, 2 * n:2 * n + 2] if n < 4 else x_view[1][:, 0:2]
                sp.dma_start(x_in[:, 2 * n:2 * n + 2], src).then_inc(x_in_s[n], 16)
                if n == 0:
                    sp.dma_start(g1c, norm1_g.rearrange("(k p) -> p k", p=P),
                                 allow_slow_non_contiguous=True).then_inc(S["g1_in"], 16)
                if n in (1, 2):
                    j = n - 1
                    sp.dma_start(w_raw[:, j], w_in_v[:, :, OFF_CQ + j * P:OFF_CQ + (j + 1) * P]).then_inc(w_in_s[j], 16)
            for dst, src in ((gqn, q_norm_g.rearrange("(k p) -> p k", p=P)), (gkvn, col(kv_norm_g)),
                             (gq, col(q_head_g)[0:NOPE]), (gqr[0:64], col(q_head_g)[NOPE:HEAD]),
                             (gqr[64:96], col(q_head_g)[NOPE + 32:HEAD]),
                             (gqr[96:128], col(q_head_g)[NOPE:NOPE + 32]),
                             (gk, col(k_head_g)[0:NOPE]), (gkr[0:64], col(k_head_g)[NOPE:HEAD]),
                             (gkr[64:96], col(k_head_g)[NOPE + 32:HEAD]),
                             (gkr[96:128], col(k_head_g)[NOPE:NOPE + 32]), (tab_k, rope_cs)):
                sp.dma_start(dst, src, allow_slow_non_contiguous=True).then_inc(S["params"], 16)

            sp.wait_ge(S["w_lo_s"], 1)
            sp.dma_start(w_raw[:, 0], w_in_v[:, :, OFF_CQ + 2 * P:OFF_CQ + 3 * P]).then_inc(w_in_s[0], 16)
            sp.wait_ge(S["w_lo_s"], 2)
            for a, b, c in ((0, 64, 0), (64, 96, 32), (96, 128, 0)):
                sp.dma_start(w_raw[:, 1, :, a:b], w_in_v[:, :, OFF_KR + c:OFF_KR + c + b - a])\
                    .then_inc(w_in_s[1], 16)
            sp.wait_ge(S["n1_lo_even"], NCH // 2)
            sp.wait_ge(S["n1_lo_odd"], NCH // 2)
            sp.dma_start(tab_q[:], rope_cs).then_inc(S["tab_in"], 16)

            for kind, g0 in (("v", G_V), ("u", G_U)):
                with sp.Fori(0, KD // 2) as i:
                    for j in range(2):
                        load_w(g0 + 2 * i + j, j, w_tile(kind, 2 * i + j))

            for j in range(2):
                sp.wait_ge(stored[j], 16 * KD)
            sp.wait_ge(S["c_dve"], 21)
            with sp.Fori(0, KD) as i:
                load_w(G_GATE + 2 * i, 0, w_tile("g", 2 * i))
                sp.wait_ge(S["sp_t"], at("sp_t", 3 * i))
                sp.dma_start(vt[:], v_d[i]).then_inc(S["sp_vin"], 16)
                sp.dma_start(ws[:], w_spatial[i]).then_inc(S["sp_wsin"], 16)
                load_w(G_GATE + 2 * i + 1, 1, w_tile("g", 2 * i + 1))
                sp.wait_ge(S["sp_y"], at("sp_y", 3 * i))
                sp.dma_start(ut, u_d[i]).then_inc(S["sp_uin"], 16)
                sp.dma_start(bb[:], b_spatial[bass.ds(i, 1), :].to_broadcast([P, P])).then_inc(S["sp_bin"], 16)
                sp.dma_start(vg, v_norm_g.rearrange("(k p o) -> k p o", p=P, o=1)[i]).then_inc(S["sp_bin"], 16)

            sp.wait_ge(S["sp_stored"], at("sp_stored", 16 * KD))
            for j in range(2):
                sp.wait_ge(stored[j], 16 * 2 * KD)
            for j in range(2):
                sp.dma_start(stg[:, j, :], y_d[j]).then_inc(ld_in[j], 16)
                load_w(G_A + j, j, w_tile("a", j))
            with sp.Fori(1, KD // 2) as i:
                for j in range(2):
                    sp.wait_ge(S["ld_lo"], at("ld_lo", 2 * i + (j - 1)))
                    sp.dma_start(stg[:, j, :], y_d[2 * i + j]).then_inc(ld_in[j], 16)
            for j in range(2):
                sp.dma_start(gt[:, j, :], g_d[j]).then_inc(gt_in[j], 16)
            with sp.Fori(1, KD // 2) as i:
                for j in range(2):
                    load_w(G_A + 2 * i + j, j, w_tile("a", 2 * i + j))
                    sp.wait_ge(S["evac"], 3 * (G_A - 1) + 3 * (2 * i + j))
                    sp.dma_start(gt[:, j, :], g_d[2 * i + j]).then_inc(gt_in[j], 16)

            uq = w_uq.rearrange("(k p) n -> p k n", p=P)
            sp.wait_ge(S["evac"], 3 * G_A)
            with sp.Fori(0, H) as h:
                sp.wait_ge(S["ap_pe"], at("ap_pe", PE_STEPS * h))
                sp.dma_start(aq_raw[:, :, 0:HEAD], uq[:, :, bass.ds(h * HEAD, HEAD)]).then_inc(S["aw_in"], 16)
                sp.dma_start(aq_raw[:, :, 192:224], uq[:, :, bass.ds(h * HEAD + (NOPE + 32), 32)]).then_inc(S["aw_in"], 16)
                sp.dma_start(aq_raw[:, :, 224:256], uq[:, :, bass.ds(h * HEAD + NOPE, 32)]).then_inc(S["aw_in"], 16)
                sp.dma_start(akv_raw[:], w_ukv[:, bass.ds(h * 256, 256)]).then_inc(S["aw_in"], 16)

            for j in range(2):
                load_w(G_B + j, j, w_tile("b", j))
            sp.wait_ge(S["ap_pe"], at("ap_pe", PE_STEPS * H))
            sp.wait_ge(S["ap_dve"], at("ap_dve", DVE_STEPS * H))
            sp.wait_ge(S["ap_act"], at("ap_act", ACT_STEPS * H))
            sp.wait_ge(S["o_st0"], at("o_st0", 32 * (H - 1)))
            sp.wait_ge(S["o_st1"], at("o_st1", 16 * (H - 1)))
            sp.dma_start(o_all[:, 0:H - 1], o_d[0:H - 1].rearrange("h p t -> p h t")).then_inc(S["o_back"], 16)
            for j in range(2):
                sp.dma_start(gt[:, j, :], g_d[KD + j]).then_inc(gt_in[j], 16)
            sp.wait_ge(S["o_st0"], at("o_st0", 32 * H))
            sp.wait_ge(S["o_st1"], at("o_st1", 16 * H))
            sp.dma_start(o_all[:, H - 1], o_d[H - 1]).then_inc(S["o_back_last"], 16)
            for j in range(2):
                sp.wait_ge(stored[j], 16 * 20)
            sp.wait_ge(S["tl_dve"], at("tl_dve", NCH * H))
            for n, (k0, k1) in enumerate(((0, 2), (2, KD))):
                sp.dma_start(z_all[:, k0:k1], za_d[k0:k1].rearrange("k p t -> p k t")).then_inc(S[f"za_in{n}"], 16)
            with sp.Fori(1, KD // 2) as i:
                for j in range(2):
                    load_w(G_B + 2 * i + j, j, w_tile("b", 2 * i + j))
                    sp.wait_ge(S["z_sum"], at("z_sum", 2 * i + (j - 1)))
                    sp.dma_start(gt[:, j, :], g_d[2 * i + (KD + j)]).then_inc(gt_in[j], 16)

            sp.wait_ge(S["ld_lo"], at("ld_lo", 2 * KD))
            sp.dma_start(x2[:, 0:NCH_P], x_view[0]).then_inc(S["x2_in"], 16)
            sp.dma_start(x2[:, NCH_P:NCH], x_view[1]).then_inc(S["x2_in"], 16)
            with sp.Fori(0, KD // 2) as i:
                for j in range(2):
                    load_w(G_OUT + 2 * i + j, j, w_tile("o", 2 * i + j))
            sp.wait_ge(S["ld_lo"], at("ld_lo", 3 * KD))
            sp.dma_start(g2b[:], norm2_g.rearrange("(o d) -> o d", o=1).to_broadcast([P, D])).then_inc(S["r_in"], 16)
            sp.dma_start(wr[:], w_router.rearrange("(k p) e -> p k e", p=P)).then_inc(S["r_in"], 16)
            for n in range(NCH):
                sp.wait_ge(S["r_h"], n + 1)
                sp.dma_start(h_d[n * P:(n + 1) * P], h2[:, n % 2].rearrange("p k t -> p (k t)"))\
                    .then_inc(S[f"h_out{n % 2}"], 16)
            sp.wait_ge(S["x2_dve"], QS * NCH)
            sp.dma_start(y_p.rearrange("(c p) d -> p c d", p=P), x2[:, 0:NCH_P]).then_inc(S["y_out"], 16)
            sp.dma_start(y_s.rearrange("(c p) d -> p c d", p=P), x2[:, NCH_P:NCH]).then_inc(S["y_out"], 16)

            sp.wait_ge(S["out_pe"], QS * NCH)
            mats = {"g": w_gate, "u": w_up, "d": w_down}

            def load_piece(kind, e, kk, q, slot):
                if not isinstance(q, int) or q >= 4:
                    sp.wait_ge(S["e_pe"], q - 3)
                sp.dma_start(raw[:, slot], mats[kind][e].rearrange("(k p) n -> p k n", p=P)[:, 2 * kk:2 * kk + 2])\
                    .then_inc(S[f"e_in{slot}"], 16)

            def frame(e):
                for kind, ee, kk, q, slot in pieces(e):
                    load_piece(kind, ee, kk, q, slot)
            run_frames(sp, frame)
            sp.wait_ge(S["scat"], 32 * E)

        @block.gpsimd
        def _(pool):
            def settled():
                pool.sem_inc(S["passed_pool"], 1)

            for n, c in credit.items():
                pool.sem_inc(S[n], c)
            pool.memset(ones[:], 1.0).then_inc(S["consts"], 1)
            pool.memset(ident[:], 1.0).then_inc(S["consts"], 1)
            pool.memset(epsc, EPS).then_inc(S["consts"], 1)
            pool.wait_ge(S["consts"], 3)
            pool.affine_select(out=ident[:], in_=ident[:], compare_op=ALU.is_equal, fill=0.0, base=0,
                               pattern=[[-1, P]], channel_multiplier=1).then_inc(S["consts"], 1)

            def split(g, j, loads):
                pool.wait_ge(w_in_s[j], 16 * loads)
                if not isinstance(g, int) or g > 1:
                    pool.wait_ge(S["blk"], {2: 5, 3: 6}.get(g, 0) if isinstance(g, int) and g < 4 else 3 * (g - 1))
                settled()
                pool.tensor_scalar(w_hi[:, j], w_raw[:, j], 1.0, 0.0, ALU.mult, ALU.add).then_inc(S["w_hi_s"], 1)
                pool.wait_ge(S["w_hi_s"], g + 1)
                pool.tensor_tensor(w_lo[:, j], w_raw[:, j], f32(w_hi[:, j]), ALU.subtract).then_inc(S["w_lo_s"], 1)

            for n in range(0, NCH, 2):
                pool.wait_ge(S["n1_hi"], n + 1)
                pool.tensor_tensor(act_lo[:, :, n * P:(n + 1) * P], htmp[:, 0], f32(act_hi[:, :, n * P:(n + 1) * P]),
                                   ALU.subtract).then_inc(S["n1_lo_even"], 1)
                if n in (2, 4):
                    split(n // 2 - 1, n // 2 - 1, 1)
            split(2, 0, 2)
            split(3, 1, 4)

            def split_loop(g0):
                with pool.Fori(0, KD // 2) as i:
                    for j in range(2):
                        split(g0 + 2 * i + j, j, i + (g0 // 2 + 1 + 2 * j))

            split_loop(G_V)
            split_loop(G_U)
            with pool.Fori(0, KD) as i:
                split(G_GATE + 2 * i, 0, i + (G_GATE // 2 + 1))
                split(G_GATE + 2 * i + 1, 1, i + (G_GATE // 2 + 3))
            split_loop(G_A)

            def head_weights(h):
                pool.wait_ge(S["aw_in"], 64 * h + 64)
                settled()
                pool.tensor_scalar(ak_hi[:], akv_raw[:, 0:P], 1.0, 0.0, ALU.mult, ALU.add).then_inc(S["aw_hi"], 1)
                pool.tensor_scalar(aq_hi[:], aq_raw[:], 1.0, 0.0, ALU.mult, ALU.add).then_inc(S["aw_hi"], 1)
                pool.wait_ge(S["aw_hi"], at("aw_hi", 2 * h + 2))
                pool.tensor_tensor(ak_lo[:], akv_raw[:, 0:P], f32(ak_hi[:]), ALU.subtract).then_inc(S["aw_lo"], 1)
                pool.tensor_tensor(aq_lo[:], aq_raw[:], f32(aq_hi[:]), ALU.subtract).then_inc(S["aw_lo"], 1)

            def head(h, more):
                pool.wait_ge(S["ap_act"], at("ap_act", ACT_STEPS * h + ACT_STEP["kr2_up"]))
                settled()
                pool.tensor_tensor(krl[0:ROPE], rt3, f32(kr2[0:ROPE]), ALU.subtract).then_inc(S["krl_pool"], 1)
                if more:
                    head_weights(h + 1)

            head_weights(0)
            with pool.Fori(0, H - 1) as h:
                head(h, True)
            head(H - 1, False)
            split_loop(G_B)

            for q in range(QS):
                wh, wl = (w_hi, w_lo) if q % 2 == 0 else (w2_hi, w2_lo)
                if q == 0:
                    pool.wait_ge(S["blk"], 3 * G_OUT)
                elif q == 1:
                    pool.wait_ge(S["ld_lo"], at("ld_lo", 3 * KD))
                else:
                    pool.wait_ge(S["out_pe"], (q - 1) * NCH)
                for j in range(2):
                    g = G_OUT + 2 * q + j
                    pool.wait_ge(w_in_s[j], 16 * (g // 2 + 1 + 2 * j))
                    settled()
                    pool.tensor_scalar(wh[:, j], w_raw[:, j], 1.0, 0.0, ALU.mult, ALU.add).then_inc(S["w_hi_s"], 1)
                    pool.wait_ge(S["w_hi_s"], g + 1)
                    pool.tensor_tensor(wl[:, j], w_raw[:, j], f32(wh[:, j]), ALU.subtract).then_inc(S["w_lo_s"], 1)
            def gather(e):
                if not (isinstance(e, int) and e == 0):
                    pool.wait_ge(S["tx_pe"], e)
                    pool.wait_ge(S["txs_pe"], e)
                settled()
                for dst, k, n in ((ixg_p, 0, P), (ixg_s, 2, CAP_S)):
                    pool.tensor_copy(dst[:], rows[0:n, k, bass.ds(e, 1)]).then_inc(S["ix_g"], 1)
                pool.wait_ge(S["ix_g"], 2 * e + 2)
                settled()
                pool.indirect_dma_start(xs_p[:], None, h_d, bass.IndirectOffsetOnAxis(ap=ixg_p[:, 0:1], axis=0)).then_inc(S["gath"], 16)
                pool.indirect_dma_start(xs_s[:], None, h_d, bass.IndirectOffsetOnAxis(ap=ixg_s[:, 0:1], axis=0)).then_inc(S["gath"], 16)
                pool.wait_ge(S["gath"], 32 * e + 32)

            def scatter(e):
                settled()
                for dst, k, n in ((ixs_p, 0, P), (ixs_s, 1, CAP_S)):
                    pool.tensor_copy(dst[:], rows[0:n, k, bass.ds(e, 1)]).then_inc(S["ix_s"], 1)
                pool.wait_ge(S["ix_s"], 2 * e + 2)
                pool.wait_ge(S["ob_act"], e + 1)
                pool.wait_ge(S["ob_dve"], e + 1)
                settled()
                pool.indirect_dma_start(y_p, bass.IndirectOffsetOnAxis(ap=ixs_p[:, 0:1], axis=0), ob_p[:], None,
                                        compute_op=ALU.add).then_inc(S["scat"], 16)
                pool.indirect_dma_start(y_s, bass.IndirectOffsetOnAxis(ap=ixs_s[:, 0:1], axis=0), ob_s[:], None,
                                        compute_op=ALU.add).then_inc(S["scat"], 16)
                pool.wait_ge(S["scat"], 32 * e + 32)

            pool.wait_ge(S["rows_s"], 5)
            pool.wait_ge(S["h_out0"], 16 * NCH // 2)
            pool.wait_ge(S["h_out1"], 16 * NCH // 2)
            pool.wait_ge(S["y_out"], 32)
            gather(0)

            def frame(e):
                first, last = isinstance(e, int) and e == 0, isinstance(e, int) and e >= E - 1
                if not (first or (isinstance(e, int) and e == 1)):
                    scatter(e - 2)
                if not last:
                    gather(e + 1)
            run_frames(pool, frame)
            scatter(E - 1)

        @block.tensor
        def _(pe):
            pe.wait_ge(S["consts"], 4)
            def lin(g, j, between=None):
                pe.wait_ge(S["w_lo_s"], g + 1)
                pe.wait_ge(S["evac"], 5 if isinstance(g, int) and g == 2 else 3 * (g - 1))
                for b, (t0, tn) in enumerate(BLOCKS):
                    for k in range(KD):
                        last = mm3(pe, lin_set(j, b), w_hi[:, j, k], w_lo[:, j, k],
                                   act_hi[:, k, t0:t0 + tn], act_lo[:, k, t0:t0 + tn], k == 0, k == KD - 1)
                    last.then_inc(S["blk"], 1)
                    if between:
                        between(b)

            def lin_loop(g0, between=None):
                with pe.Fori(0, KD // 2) as i:
                    for j in range(2):
                        lin(g0 + 2 * i + j, j, (lambda b: between(i, j, b)) if between else None)

            def n1_turn(n):
                pe.wait_ge(S["n1_xn"], n + 1)
                if n > 0:
                    pe.wait_ge(S["n1_h"], n)
                for k in range(KD):
                    last = pe.transpose(bank(6, D)[:, k * P:(k + 1) * P], xn[:, n % 2, k * P:(k + 1) * P], ident[:])
                last.then_inc(S["n1_tr"], 1)

            def first_tiles(g, b):
                t0, tn = BLOCKS[b]
                pe.wait_ge(S["w_lo_s"], g + 1)
                pe.wait_ge(S["n1_lo_even"], (t0 + tn) // (2 * P))
                pe.wait_ge(S["n1_lo_odd"], (t0 + tn) // (2 * P))
                for k in range(KD):
                    last = mm3(pe, lin_set(g, b), w_hi[:, g, k], w_lo[:, g, k], act_hi[:, k, t0:t0 + tn],
                               act_lo[:, k, t0:t0 + tn], k == 0, k == KD - 1)
                last.then_inc(S["blk"], 1)

            for n in range(7):
                n1_turn(n)
            first_tiles(0, 0)
            n1_turn(7)
            n1_turn(8)
            first_tiles(1, 0)
            n1_turn(9)
            for b in (1, 2):
                first_tiles(0, b)
                first_tiles(1, b)
            for g in (2, 3):
                lin(g, g % 2)
            lin_loop(G_V)

            for n, (src, need, sem_) in enumerate(((rs_v, 4, "c_dve"), (krf, 5, "c_dve"), (acc_v, KD, "v_acc"))):
                pe.wait_ge(S[sem_], need)
                for b, (t0, tn) in enumerate(BLOCKS):
                    q = 3 * n + b
                    if q > 1:
                        pe.wait_ge(S["c_stev"], q - 1)
                    pe.matmul(bank(6 + q % 2, tn), ones[:], src[:, t0:t0 + tn], start=True,
                              stop=True).then_inc(S["c_sta"], 1)
            lin_loop(G_U)

            pe.wait_ge(S["c_stev"], 9)
            with pe.Fori(0, KD) as i:
                def gating(j, b):
                    t0, tn = BLOCKS[b]
                    if j == 0:
                        pe.wait_ge(S["sp_vn"], at("sp_vn", i + 1))
                        if b == 0:
                            pe.wait_ge(S["sp_act"], at("sp_act", 3 * i - 1))
                        elif b == 1:
                            pe.wait_ge(S["sp_act"], at("sp_act", 3 * i))
                        else:
                            pe.wait_ge(S["sp_tok"], at("sp_tok", 4 * i + 1))
                        o = bank(6 + b % 2)
                        for c in range(tn // P):
                            last = pe.transpose(o[:, c * P:(c + 1) * P], vt[:, t0 + c * P:t0 + (c + 1) * P], ident[:])
                        if b == 2:
                            pe.wait_ge(S["sp_wsin"], 16 * i + 16)
                            last = pe.transpose(o[:, 2 * P:3 * P], ws[:], ident[:])
                        last.then_inc(S["sp_t"], 1)
                    else:
                        if b == 0:
                            pe.wait_ge(S["sp_tok"], at("sp_tok", 4 * i + 4))
                        else:
                            pe.wait_ge(S["sp_act"], at("sp_act", 3 * i + (b - 1)))
                        o = bank(7 - b % 2)
                        for c in range(tn // P):
                            last = pe.matmul(o[:, c * P:(c + 1) * P], vtok[:, t0 + c * P:t0 + (c + 1) * P],
                                             wsT[:], start=True, stop=True)
                        last.then_inc(S["sp_m"], 1)
                lin(G_GATE + 2 * i, 0, lambda b: gating(0, b))
                lin(G_GATE + 2 * i + 1, 1, lambda b: gating(1, b))

            def lin_split(g0, n0, between=None):
                for j in range(2):
                    pe.wait_ge(S["w_lo_s"], g0 + j + 1)
                    pe.wait_ge(S["evac"], 3 * (g0 + j - 1))
                for k in range(KD):
                    pe.wait_ge(S["ld_lo"], at("ld_lo", n0 + k + 1))
                    for j in range(2):
                        for b, (t0, tn) in enumerate(BLOCKS):
                            last = mm3(pe, lin_set(j, b), w_hi[:, j, k], w_lo[:, j, k],
                                       act_hi[:, k, t0:t0 + tn], act_lo[:, k, t0:t0 + tn], k == 0, k == KD - 1)
                            if k == KD - 1:
                                last.then_inc(S["blk"], 1)
                                if between:
                                    between(0, j, b)
                with pe.Fori(1, KD // 2) as i:
                    for j in range(2):
                        lin(g0 + 2 * i + j, j, (lambda b: between(i, j, b)) if between else None)

            lin_split(G_A, 0)

            pe.wait_ge(S["evac"], 3 * G_B)
            pe.wait_ge(S["c_dve"], 22)

            def project_k(h):
                pe.wait_ge(S["aw_lo"], at("aw_lo", 2 * h + 1))
                for b, (t0, tn) in enumerate(BLOCKS):
                    mm3(pe, lin_set(0, b), ak_hi[:], ak_lo[:], ckv_hi[:, t0:t0 + tn],
                        ckv_lo[:, t0:t0 + tn], True, True).then_inc(S["ap_pe"], 1)

            def column_sums(out, src):
                for c in range(NCH):
                    last = pe.matmul(out[:, c:c + 1], src[:, c * P:(c + 1) * P], ones[0:src.shape[0], 0:1],
                                     start=True, stop=True)
                return last

            def head(h, more):
                def dve(name):
                    pe.wait_ge(S["ap_dve"], at("ap_dve", DVE_STEPS * h + DVE_STEP[name]))

                def acts(name):
                    pe.wait_ge(S["ap_act"], at("ap_act", ACT_STEPS * h + ACT_STEP[name]))

                def project_q(half, j):
                    for b, (t0, tn) in enumerate(BLOCKS):
                        for k in range(2):
                            w = slice(half * P, half * P + P)
                            last = mm3(pe, lin_set(j, b), aq_hi[:, k, w], aq_lo[:, k, w],
                                       cq_hi[:, k, t0:t0 + tn], cq_lo[:, k, t0:t0 + tn], k == 0, k == 1)
                        last.then_inc(S["ap_pe"], 1)

                pe.wait_ge(S["aw_lo"], at("aw_lo", 2 * h + 2))
                pe.wait_ge(S["tl_dve"], at("tl_dve", NCH * h))
                project_q(0, 1)
                acts("sq_k")
                pe.wait_ge(S["ov_act"], at("ov_act", 3 * h))
                pe.wait_ge(S["c_dve"], 23)
                column_sums(bank(6), sq_k).then_inc(S["ap_pe"], 1)
                acts("kf")
                for b, (t0, tn) in enumerate(BLOCKS):
                    for c in range(t0, t0 + tn, P):
                        last = pe.matmul(lin_all(0)[:, c:c + P], ckv[:, c:c + P], akv_raw[:, P:2 * P],
                                         start=True, stop=True)
                    last.then_inc(S["ap_pe"], 1)
                dve("diag")
                for b, (t0, tn) in enumerate(BLOCKS):
                    pe.matmul(lin_set(1, b), ones[:], diag[:, t0:t0 + tn], start=True,
                              stop=True).then_inc(S["ap_pe"], 1)
                dve("v_lo")
                project_q(1, 0)
                column_sums(bank(7), sq_q)
                acts("sq_qr2")
                column_sums(bank(7)[:, NCH:2 * NCH], sq_qr[0:ROPE]).then_inc(S["ap_pe"], 1)
                acts("k_hi")
                dve("rt_2")

                def keys(c):
                    return (0, TP) if c < NCH_P else (TP, TS)

                def scores(c):
                    k0, kn = keys(c)
                    pe.wait_ge(S["ex_act"], at("ex_act", NCH * h + (c - 1)))
                    q = slice(c * P, (c + 1) * P)
                    halves = []
                    for o in range(0, kn, BANK):
                        n = min(BANK, kn - o)
                        halves.append((bank(s_bank(c) + o // BANK, n), slice(k0 + o, k0 + o + n)))
                    for out, k in halves:
                        pe.matmul(out, q_hi[:, q], k_hi[:, k], start=True, stop=False)
                        pe.matmul(out, q_hi[:, q], k_lo[:, k], start=False, stop=False)
                        pe.matmul(out, q_lo[:, q], k_hi[:, k], start=False, stop=False)
                    if c == 0:
                        acts("qr2_up")
                        dve("qr2_down")
                        pe.wait_ge(S["krl_pool"], h + 1)
                    for out, k in halves:
                        pe.matmul(out, qr2[:, q], kr2[:, k], start=False, stop=False)
                        last = pe.matmul(out, qr2[:, q], krl[:, k], start=False, stop=True)
                    last.then_inc(S["qk_pe"], 1)

                def turn(c):
                    kn = keys(c)[1]
                    pr = "pr_dve" if c % 2 else "pr_act"
                    pe.wait_ge(S[pr], at(pr, NCH // 2 * h + (c // 2 + 1)))
                    pe.wait_ge(S["tl_dve"], at("tl_dve", NCH * h + min(c, NCH - 2)))
                    for k in range(kn // P):
                        last = pe.transpose(bank(t_bank(c), kn)[:, k * P:(k + 1) * P],
                                            prob[:, c % 2, k * P:(k + 1) * P], ident[:])
                    last.then_inc(S["t_pe"], 1)

                def values(b):
                    t0, tn = BLOCKS[b]
                    k0, kn = keys(t0 // P)
                    pe.wait_ge(S["tl_dve"], at("tl_dve", NCH * h + (t0 + tn) // P))
                    pe.wait_ge(S["ov_act"], at("ov_act", 3 * h + max(b - 1, 0)))
                    for k in range(kn // P):
                        v = slice(k0 + k * P, k0 + (k + 1) * P)
                        last = mm3(pe, bank(6 + b % 2, tn), v_hi[:, v], v_lo[:, v], pt_hi[:, k, 0:tn],
                                   pt_lo[:, k, 0:tn], k == 0, k == kn // P - 1)
                    last.then_inc(S["pv_pe"], 1)

                for c in range(NCH):
                    scores(c)
                    if c == 6:
                        values(0)
                    if c > 1:
                        turn(c - 2)
                if more:
                    pe.wait_ge(S["ex_act"], at("ex_act", NCH * h + (NCH - 1)))
                    project_k(h + 1)
                values(1)
                turn(NCH - 2)
                turn(NCH - 1)
                values(2)

            project_k(0)
            column_sums(bank(7), sq_kr[0:ROPE]).then_inc(S["kr_pe"], 1)
            with pe.Fori(0, H - 1) as h:
                head(h, True)
            head(H - 1, False)

            lin_split(G_B, KD)

            def out_product(q, c, k, acc):
                wh, wl = (w_hi, w_lo) if q % 2 == 0 else (w2_hi, w2_lo)
                t = slice(c * P, (c + 1) * P)
                last = mm3(pe, bank(acc)[:, 0:QN], act_hi[:, k, t], act_lo[:, k, t], wh[:, :, k], wl[:, :, k],
                           k == 0, k == KD - 1)
                if k == KD - 1:
                    last.then_inc(S["out_pe"], 1)

            def out_chunk(q, c):
                pe.wait_ge(S["x2_dve"], q * NCH + c - 1)
                for k in range(KD):
                    out_product(q, c, k, 4 + c % 2)

            pe.wait_ge(S["w_lo_s"], G_OUT + 2)
            pe.wait_ge(S["evac"], 3 * G_OUT)
            for k in range(KD):
                pe.wait_ge(S["ld_lo"], at("ld_lo", 2 * KD + k + 1))
                for c in range(8):
                    out_product(0, c, k, c)
            out_chunk(0, 8)
            out_chunk(0, 9)
            for q in range(1, QS - 1):
                pe.wait_ge(S["w_lo_s"], G_OUT + 2 * q + 2)
                for c in range(NCH):
                    out_chunk(q, c)
            pe.wait_ge(S["w_lo_s"], G_OUT + 2 * QS)
            pe.wait_ge(S["r_in"], 32)

            def channels(n):
                pe.wait_ge(S["r_h"], n + 1)
                if n > 1:
                    pe.wait_ge(S["r_hT"], n - 1)
                for k in range(KD):
                    last = pe.transpose(bank(2 * (n % 2), D)[:, k * P:(k + 1) * P], h2[:, n % 2, k], ident[:])
                last.then_inc(S["r_t"], 1)

            def logits(n):
                pe.wait_ge(S["r_hT"], n + 1)
                for k in range(KD):
                    last = pe.matmul(bank(6)[:, n * E:(n + 1) * E], h2T[:, n % 2, k * P:(k + 1) * P], wr[:, k],
                                     start=(k == 0), stop=(k == KD - 1))
                last.then_inc(S["rt_pe0"], 1)

            for c in range(NCH + 2):
                if c < NCH:
                    out_chunk(QS - 1, c)
                if 0 < c <= NCH:
                    channels(c - 1)
                if c > 1:
                    logits(c - 2)
            pe.wait_ge(S["r_dve"], 5)
            for c in range(NCH):
                last = pe.transpose(PS[0:E, c * P:(c + 1) * P], aff[:, c, :], ident[:])
            last.then_inc(S["a_t"], 1)
            pe.wait_ge(S["tk"], 3 * (CAP_P + CAP_S) // 8 + 3)
            for n, src in enumerate((topv[:, 0], topv[:, 1], topf[:, 0], topf[:, 1])):
                pe.transpose(bank(3)[:, n * E:(n + 1) * E], src, ident[0:E, 0:E]).then_inc(S["rt_pe"], 1)

            def turn_x(e):
                pe.wait_ge(S["gath"], 32 * e + 32)
                for k in range(KD):
                    last = pe.transpose(bank(0, D)[:, k * P:(k + 1) * P], xs_p[:, k * P:(k + 1) * P], ident[:])
                last.then_inc(S["tx_pe"], 1)

            def turn_xs(e):
                pe.sem_inc(S["passed_pe"], 1)
                for k in range(KD):
                    last = pe.transpose(bank(7)[:, k * CAP_S:(k + 1) * CAP_S], xs_s[:, k * P:(k + 1) * P],
                                        ident[0:CAP_S, 0:CAP_S])
                last.then_inc(S["txs_pe"], 1)

            def product(b0, hi, lo, bs, few, slot, pt, kk, guard_s):
                for kin in range(2):
                    k = 2 * kk + kin
                    for rhs, lhs, st, sp_ in ((ehi, hi, k == 0, False), (elo, hi, False, False), (ehi, lo, False, k == KD - 1)):
                        for half in range(2):
                            pe.matmul(bank(b0 + half), lhs[:, k], rhs[:, pt, kin, half * BANK:(half + 1) * BANK],
                                      start=st, stop=sp_)
                guard_s()
                for kin in range(2):
                    k = 2 * kk + kin
                    for g in range(GRP):
                        last = pe.matmul(bank(bs)[CAP_S * g:CAP_S * (g + 1), 0:GN], few(k),
                                         raw[:, slot, kin, g * GN:(g + 1) * GN], start=(k == 0), stop=(k == KD - 1))
                last.then_inc(S["e_pe"], 1)

            pe.wait_ge(S["rows_s"], 5)
            turn_x(0)
            turn_xs(0)

            def frame(e):
                is0, is1, is_last = (isinstance(e, int) and e == v for v in (0, 1, E))
                for n, (kind, ee, kk, q, slot) in enumerate(pieces(e)):
                    l = n + (8 if is_last else 0)
                    if is_last and n == 0:
                        turn_h(E - 1)
                        pe.wait_ge(S["hl_dve"], E)
                        pe.wait_ge(S["hs_dve"], E)
                    if l == 0:
                        pe.wait_ge(S["xl_dve"], e + 1)
                        pe.wait_ge(S["xs_dve"], e + 1)
                    if l == 4 and not is0:
                        pe.wait_ge(S["hl_dve"], e)
                        pe.wait_ge(S["hs_dve"], e)
                    if l == 8 and not is1:
                        pe.wait_ge(S["ob_act"], e - 1)
                        pe.wait_ge(S["ob_dve"], e - 1) if is_last else None
                    pe.wait_ge(S["e_lo"], q + 1)

                    def guard_s():
                        if l == 0 and not (is0 or is1):
                            pe.wait_ge(S["ob_dve"], e - 1)
                        if l == 8 and not is_last:
                            pe.wait_ge(S["silu_s"], e + 1)
                    if kind == "d":
                        product(4, hT_hi, hT_lo, 6, lambda k: hT_s[:, k % 2 * P + k // 2 * CAP_S:k % 2 * P + k // 2 * CAP_S + CAP_S],
                                slot, part(n if is_last else l, False) if not is_last else q % 3, kk, guard_s)
                    else:
                        product(0 if kind == "g" else 2, xT_hi, xT_lo, 6 if kind == "g" else 7,
                                lambda k: xT_s[:, k], slot, part(l, is0), kk, guard_s)
                    if l == 0 and not is0:
                        turn_h(e - 1)
                    more = not (isinstance(e, int) and e >= E - 1)
                    if more and l == (7 if is0 else 8):
                        pe.wait_ge(S["silu_p"], e + 1)
                        turn_x(e + 1)
                    if more and l == (7 if is0 else 9):
                        pe.wait_ge(S["mul_s"], e + 1)
                        turn_xs(e + 1)

            def turn_h(e):
                pe.wait_ge(S["mul_p"], e + 1)
                for k in range(KD):
                    last = pe.transpose(bank(2, D)[:, k * P:(k + 1) * P], hid[:, k * P:(k + 1) * P], ident[:])
                last.then_inc(S["th_pe"], 1)
                pe.wait_ge(S["mul_s"], e + 1)
                pe.wait_ge(S["xs_dve"], e + 2) if not (isinstance(e, int) and e >= E - 1) else None
                for k in range(2):
                    last = pe.transpose(bank(7)[:, k * P:(k + 1) * P], hid_s[:, k * P:(k + 1) * P], ident[:])
                last.then_inc(S["ths_pe"], 1)

            run_frames(pe, frame)

        @block.scalar
        def _(act):
            for n in range(NCH + 2):
                if n < NCH:
                    if n % 2 == 0:
                        act.wait_ge(x_in_s[n // 2], 16)
                    if n > 1:
                        act.wait_ge(S["n1_ssq"], n - 1)
                    act.activation(stg[:, n % 2, 0:D], x_in[:, n], ACT.Square, accum_out=ssq1[:, n:n + 1]).then_inc(S["n1_ssq"], 1)
                    act.wait_ge(S["n1_ssq"], n + 1)
                    if n == 0:
                        act.wait_ge(S["consts"], 3)
                    act.activation(std1[:, n:n + 1], ssq1[:, n:n + 1], ACT.Sqrt, bias=epsc,
                                   scale=1.0 / D).then_inc(S["n1_std"], 1)
                if n > 1:
                    act.wait_ge(S["n1_h"], n - 1)
                    act.activation(act_hi[:, :, (n - 2) * P:(n - 1) * P], htmp[:, n % 2], ACT.Copy).then_inc(S["n1_hi"], 1)

            dst = [ct[:, 0, :], ct[:, 1, :], ckv[:], ct[:, 2, :]]
            order = [(g, b) for b in range(3) for g in range(2)] + [(g, b) for g in (2, 3) for b in range(3)]
            for n, (g, b) in enumerate(order):
                t0, tn = BLOCKS[b]
                act.wait_ge(S["blk"], n + 1)
                if g == 2 and b == 0:
                    act.wait_ge(S["n1_lo_even"], NCH // 2)
                    act.wait_ge(S["n1_lo_odd"], NCH // 2)
                act.activation(dst[g][:, t0:t0 + tn], lin_set(g % 2, b), ACT.Copy).then_inc(S["evac"], 1)

            def evac(g, j, func, out, uses, guard=None):
                for b, (t0, tn) in enumerate(BLOCKS):
                    act.wait_ge(S["blk"], 3 * g + (b + 1))
                    if b == 0:
                        if uses is not None:
                            act.wait_ge(stored[j], 16 * uses)
                        if guard is not None:
                            guard()
                    act.activation(stg[:, j, t0:t0 + tn], lin_set(j, b), func).then_inc(S["evac"], 1)
                act.wait_ge(S["evac"], 3 * g + 3)
                act.dma_start(out, stg[:, j, :]).then_inc(stored[j], 16)

            for j in range(2):
                evac(G_V + j, j, ACT.Gelu, v_d[j], None)
            with act.Fori(1, KD // 2) as i:
                for j in range(2):
                    evac(2 * i + (G_V + j), j, ACT.Gelu, v_d[2 * i + j], i,
                         lambda: act.wait_ge(S["v_acc"], 2 * i + (j - 1)))

            rs = [rs_v, krf, rs_v]
            for n in range(3):
                for b, (t0, tn) in enumerate(BLOCKS):
                    q = 3 * n + b
                    act.wait_ge(S["c_sta"], q + 1)
                    if n == 2 and b == 0:
                        act.wait_ge(S["c_dve"], 10)
                        act.wait_ge(S["v_acc"], KD)
                    act.activation(rs[n][:, t0:t0 + tn], bank(6 + q % 2, tn), ACT.Sqrt, bias=epsc,
                                   scale=1.0 / (QR, KVR, D)[n]).then_inc(S["c_stev"], 1)
            for m in range(2):
                act.wait_ge(S["c_dve"], 9 + m)
                act.activation(cq_hi[:, m], ct[:, m, :], ACT.Copy, scale=gqn[:, m:m + 1]).then_inc(S["c_act"], 1)
            act.wait_ge(S["c_dve"], 13)
            act.activation(ckv_hi[:], ckv[:], ACT.Copy).then_inc(S["c_act"], 1)

            with act.Fori(0, KD // 2) as i:
                for j in range(2):
                    evac(2 * i + (G_U + j), j, ACT.Gelu, u_d[2 * i + j], i + 4)

            with act.Fori(0, KD) as i:
                def gated(j):
                    g = 2 * i + (G_GATE + j)
                    for b, (t0, tn) in enumerate(BLOCKS):
                        act.wait_ge(S["blk"], 3 * g + (b + 1))
                        if b == 0:
                            act.wait_ge(stored[j], 16 * i + 16 * KD)
                        act.activation(stg[:, j, t0:t0 + tn], lin_set(j, b), ACT.Sigmoid).then_inc(S["evac"], 1)
                        if j == 0:
                            act.wait_ge(S["sp_t"], at("sp_t", 3 * i + (b + 1)))
                            if b == 0:
                                act.wait_ge(S["sp_m"], at("sp_m", 3 * i))
                            act.activation(vtok[:, t0:t0 + tn], bank(6 + b % 2, tn), ACT.Copy).then_inc(S["sp_tok"], 1)
                            if b == 2:
                                act.activation(wsT[:], bank(6)[:, 2 * P:3 * P], ACT.Copy).then_inc(S["sp_tok"], 1)
                    act.wait_ge(S["evac"], 3 * g + 3)
                    act.dma_start(g_d[2 * i + j], stg[:, j, :]).then_inc(stored[j], 16)
                gated(0)
                gated(1)
                act.wait_ge(S["sp_y"], at("sp_y", 3 * i + 3))
                act.dma_start(y_d[i], yt[:]).then_inc(S["sp_stored"], 16)

            act.wait_ge(S["blk"], 3 * G_A)
            with act.Fori(0, KD // 2) as i:
                for j in range(2):
                    act.wait_ge(ld_in[j], 16 * i + 16)
                    act.activation(act_hi[:, 2 * i + j, :], stg[:, j, :], ACT.Copy).then_inc(S["ld_hi"], 1)
            with act.Fori(0, KD // 2) as i:
                for j in range(2):
                    act.wait_ge(S["evac"], 6 * i + (3 * G_A + 3 * j + 3))
                    act.dma_start(za_d[2 * i + j], stg[:, j, :]).then_inc(stored[j], 16)

            for j in range(2):
                act.wait_ge(stored[j], 16 * 20)
            with act.Fori(0, H) as h:
                def own(name):
                    act.wait_ge(S["ap_act"], at("ap_act", ACT_STEPS * h + ACT_STEP[name]))

                def dve(name):
                    act.wait_ge(S["ap_dve"], at("ap_dve", DVE_STEPS * h + DVE_STEP[name]))

                def products(name):
                    act.wait_ge(S["ap_pe"], at("ap_pe", PE_STEPS * h + PE_STEP[name]))

                def done(i_):
                    i_.then_inc(S["ap_act"], 1)

                def sq_rotary(b):
                    t0, tn = BLOCKS[b]
                    products(f"qr{b}")
                    done(act.activation(sq_qr[0:ROPE, t0:t0 + tn], lin_set(0, b)[0:ROPE], ACT.Square))

                done(act.activation(spare, epsc, ACT.Sqrt))
                products("k")
                done(act.activation(sq_k, lin_all(0), ACT.Square))
                done(act.activation(kf[:], lin_all(0), ACT.Copy, scale=gk))
                products("q")
                done(act.activation(sq_q, lin_all(1), ACT.Square))
                done(act.activation(q_hi[:], lin_all(1), ACT.Copy, scale=gq))
                dve("rk_v")
                done(act.activation(rk_s, rk_v, ACT.Sqrt, bias=epsc, scale=1.0 / HEAD))
                products("v")
                done(act.activation(v_hi[:], lin_all(0), ACT.Copy))
                sq_rotary(0)
                dve("kf")
                done(act.activation(k_hi[:], kf[:], ACT.Copy))
                sq_rotary(1)
                dve("rt3")
                done(act.activation(kr2[0:ROPE], rt3, ACT.Copy))
                sq_rotary(2)
                done(act.activation(kr2[ROPE:P], rt3, ACT.Copy))
                dve("rt1")
                done(act.activation(qr2[0:ROPE], rt1, ACT.Copy))
                dve("rq_v")
                done(act.activation(rq_s, rq_v, ACT.Sqrt, bias=epsc, scale=1.0 / HEAD))
                own("rq_s")
                done(act.activation(spare, epsc, ACT.Exp))

                def keys(c):
                    return TP if c < NCH_P else TS

                def expo(c):
                    n = keys(c)
                    act.wait_ge(S["nm_dve"], at("nm_dve", NCH * h + (c + 1)))
                    act.wait_ge(S["t_pe"], at("t_pe", NCH * h + (c - 1)))
                    act.activation(prob[:, c % 2, 0:n], bank(s_bank(c), n), ACT.Exp, bias=nmx[:, c:c + 1],
                                   scale=rq[:, c:c + 1], accum_out=psumr[:, c:c + 1]).then_inc(S["ex_act"], 1)

                def norm(c):
                    n = keys(c)
                    act.wait_ge(S["rc_dve"], at("rc_dve", NCH * h + (c + 1)))
                    act.activation(prob[:, c % 2, 0:n], prob[:, c % 2, 0:n], ACT.Copy,
                                   scale=prec[:, c:c + 1]).then_inc(S["pr_act"], 1)

                def high(c):
                    n = keys(c) // P
                    o = (c % NCH_P) % 4 * P
                    act.wait_ge(S["t_pe"], at("t_pe", NCH * h + (c + 1)))
                    if c in (0, 4, 8):
                        act.wait_ge(S["pv_pe"], at("pv_pe", 3 * h + c // 4))
                    act.activation(pt_hi[:, 0:n, o:o + P], bank(t_bank(c), n * P), ACT.Copy).then_inc(S["th_act"], 1)

                def out(b):
                    t0, tn = BLOCKS[b]
                    slot = b % 2
                    st = S[f"o_st{slot}"]
                    act.wait_ge(S["pv_pe"], at("pv_pe", 3 * h + (b + 1)))
                    act.wait_ge(st, 32 + (16 * h if slot else 32 * h + (16 if b else 0)))
                    act.activation(ostg[:, slot, 0:tn], bank(6 + slot, tn), ACT.Copy).then_inc(S["ov_act"], 1)
                    act.wait_ge(S["ov_act"], at("ov_act", 3 * h + (b + 1)))
                    act.dma_start(o_d[h][:, t0:t0 + tn], ostg[:, slot, 0:tn]).then_inc(st, 16)

                for c in range(NCH + 2):
                    if c > 1:
                        high(c - 2)
                    if c < NCH:
                        expo(c)
                        if c % 2 == 0:
                            norm(c)
                    if c in (7, 11):
                        out(c // 4 - 1)
                out(2)

            act.wait_ge(S["pv_pe"], at("pv_pe", 3 * H))
            act.wait_ge(S["o_back"], 16)
            with act.Fori(0, H - 1) as h:
                act.activation(act_hi[:, h, :], o_all[:, h, :], ACT.Copy).then_inc(S["ld_hi"], 1)
            act.wait_ge(S["o_back_last"], 16)
            act.activation(act_hi[:, H - 1, :], o_all[:, H - 1, :], ACT.Copy).then_inc(S["ld_hi"], 1)
            act.wait_ge(S["blk"], 3 * G_OUT)
            with act.Fori(0, KD) as k:
                act.wait_ge(S["z_sum"], at("z_sum", k + 1))
                act.activation(act_hi[:, k, :], z_all[:, k, :], ACT.Copy).then_inc(S["ld_hi"], 1)
            for n in range(NCH + 1):
                if n < NCH:
                    act.wait_ge(S["x2_dve"], (QS - 1) * NCH + n + 1)
                    if n > 1:
                        act.wait_ge(S["r_ssq"], n - 1)
                    act.activation(stg[:, n % 2, 0:D], x2[:, n, :], ACT.Square, accum_out=ssq2[:, n:n + 1]).then_inc(S["r_ssq"], 1)
                    act.wait_ge(S["r_ssq"], n + 1)
                    act.activation(std2[:, n:n + 1], ssq2[:, n:n + 1], ACT.Sqrt, bias=epsc,
                                   scale=1.0 / D).then_inc(S["r_std"], 1)
                if n > 0:
                    act.wait_ge(S["r_t"], n)
                    if n > 2:
                        act.wait_ge(S["rt_pe0"], n - 2)
                    m = (n - 1) % 2
                    act.activation(h2T[:, m], bank(2 * m, D), ACT.Copy).then_inc(S["r_hT"], 1)
            act.wait_ge(S["r_dve"], 2)
            act.activation(aff[:], lg[:], ACT.Exp).then_inc(S["r_exp"], 1)
            act.wait_ge(S["a_t"], 1)
            act.activation(affT[:], PS[0:E, 0:T], ACT.Copy).then_inc(S["a_T"], 1)

            def frame(e):
                is0, is1, is_last = (isinstance(e, int) and e == v for v in (0, 1, E))
                more = not (isinstance(e, int) and e >= E - 1)
                for n, (kind, ee, kk, q, slot) in enumerate(pieces(e)):
                    l = n + (8 if is_last else 0)
                    if is_last and n == 0:
                        out(e - 2)
                        hidden(e - 1)
                    act.wait_ge(S[f"e_in{slot}"], loads_of(e, n))
                    if not isinstance(q, int) or q >= 3:
                        act.wait_ge(S["e_pe"], q - 2)
                    pt = part(l, is0) if not is_last else q % 3
                    act.activation(ehi[:, pt], raw[:, slot], ACT.Copy).then_inc(S["e_hi"], 1)
                    if l == 1 and not (is0 or is1):
                        out(e - 2)
                    if l == 2 and not is0:
                        hidden(e - 1)
                    if l == 5:
                        act.wait_ge(S["e_pe"], q - 1)
                        if not is0:
                            act.wait_ge(S["ths_pe"], e)
                        act.activation(hid[:], bank(0, D), ACT.Silu).then_inc(S["silu_p"], 1)
                        act.activation(hid_s[:], bank(6, GN), ACT.Silu).then_inc(S["silu_s"], 1)
                    if more and l == (7 if is0 else 10):
                        rows_hi(e + 1)
                if is_last:
                    out(e - 1)

            def rows_hi(e):
                act.wait_ge(S["tx_pe"], e + 1)
                act.activation(xT_hi[:], bank(0, D), ACT.Copy).then_inc(S["xh_act"], 1)

            def hidden(e):
                act.wait_ge(S["th_pe"], e + 1)
                act.activation(hT_hi[:], bank(2, D), ACT.Copy).then_inc(S["hh_act"], 1)

            def out(e):
                act.wait_ge(S["e_pe"], 12 * E if isinstance(e, int) and e == E - 1 else 12 * e + 20)
                if not (isinstance(e, int) and e == 0):
                    act.wait_ge(S["scat"], 32 * e)
                act.activation(ob_p[:], bank(4, D), ACT.Copy, scale=gates[:, 0, bass.ds(e, 1)]).then_inc(S["ob_act"], 1)

            act.wait_ge(S["y_out"], 32)
            rows_hi(0)
            run_frames(act, frame)

        @block.vector
        def _(dve):
            for n in range(NCH + 2):
                if n < NCH:
                    dve.wait_ge(S["n1_std"], n + 1)
                    dve.reciprocal(rstd1[:, n:n + 1], std1[:, n:n + 1]).then_inc(S["n1_rec"], 1)
                    dve.wait_ge(S["n1_rec"], n + 1)
                    if n > 1:
                        dve.wait_ge(S["n1_tr"], n - 1)
                    dve.tensor_scalar(xn[:, n % 2], x_in[:, n, :], rstd1[:, n:n + 1], None, ALU.mult).then_inc(S["n1_xn"], 1)
                if n >= 2 and n % 2:
                    m = n - 2
                    dve.wait_ge(S["n1_hi"], m + 1)
                    dve.tensor_tensor(act_lo[:, :, m * P:(m + 1) * P], htmp[:, 1], f32(act_hi[:, :, m * P:(m + 1) * P]),
                                      ALU.subtract).then_inc(S["n1_lo_odd"], 1)
                if 1 <= n <= NCH:
                    m = n - 1
                    dve.wait_ge(S["n1_tr"], m + 1)
                    if m == 0:
                        dve.wait_ge(S["g1_in"], 16)
                    if m > 1:
                        dve.wait_ge(S["n1_lo_odd" if m % 2 else "n1_lo_even"], m // 2)
                    dve.tensor_tensor(htmp[:, m % 2], bank(6, D).rearrange("p (k t) -> p k t", k=KD),
                                      g1c.unsqueeze(2).to_broadcast([P, KD, P]), ALU.mult).then_inc(S["n1_h"], 1)
            dve.wait_ge(S["params"], 16 * 11)

            def step(i_, n):
                i_.then_inc(S["c_dve"], 1)
                dve.wait_ge(S["c_dve"], n)
            step(dve.tensor_scalar(tab_k, tab_k, gkr, None, ALU.mult), 1)
            dve.wait_ge(S["evac"], 3 * 2)
            step(dve.tensor_tensor(rs_v[:], ct[:, 0, :], ct[:, 0, :], ALU.mult), 2)
            step(dve.tensor_tensor(acc_v[:], ct[:, 1, :], ct[:, 1, :], ALU.mult), 3)
            step(dve.tensor_tensor(rs_v[:], rs_v[:], acc_v[:], ALU.add), 4)
            dve.wait_ge(S["evac"], 3 * 3)
            step(dve.tensor_tensor(krf[:], ckv[:], ckv[:], ALU.mult), 5)
            dve.wait_ge(S["evac"], 3 * 4)
            step(dve.tensor_tensor(sq_kr[0:ROPE], ct[0:ROPE, 2, :], ct[0:ROPE, 2, :], ALU.mult), 6)
            step(dve.memset(acc_v[:], 0.0), 7)
            with dve.Fori(0, KD // 2) as i:
                for j in range(2):
                    dve.wait_ge(S["evac"], 6 * i + (3 * (G_V + j) + 3))
                    dve.tensor_tensor(sq_v, stg[:, j, :], stg[:, j, :], ALU.mult).then_inc(S["v_sq"], 1)
                    dve.wait_ge(S["v_sq"], 2 * i + (j + 1))
                    dve.tensor_tensor(acc_v[:], acc_v[:], sq_v, ALU.add).then_inc(S["v_acc"], 1)
                    dve.wait_ge(S["v_acc"], 2 * i + (j + 1))
            dve.wait_ge(S["c_stev"], 3)
            step(dve.reciprocal(rs_v[:], rs_v[:]), 8)
            for m in range(2):
                step(dve.tensor_tensor(ct[:, m, :], ct[:, m, :], rs_v[:], ALU.mult), 9 + m)
            dve.wait_ge(S["c_stev"], 6)
            step(dve.reciprocal(krf[:], krf[:]), 11)
            step(dve.tensor_tensor(ckv[:], ckv[:], krf[:], ALU.mult), 12)
            step(dve.tensor_scalar(ckv[:], ckv[:], gkvn, None, ALU.mult), 13)
            step(dve.tensor_tensor(krf[0:ROPE], ct[0:ROPE, 2, :], tab_k[0:ROPE], ALU.mult), 14)
            step(dve.tensor_tensor(ct[0:ROPE, 2, :], ct[ROPE:P, 2, :], tab_k[ROPE:P], ALU.mult), 15)
            step(dve.tensor_tensor(krf[0:ROPE], krf[0:ROPE], ct[0:ROPE, 2, :], ALU.add), 16)
            for m in range(2):
                dve.wait_ge(S["c_act"], m + 1)
                step(dve.scalar_tensor_tensor(out=cq_lo[:, m], in0=ct[:, m, :], scalar=gqn[:, m:m + 1],
                                              in1=f32(cq_hi[:, m]), op0=ALU.mult, op1=ALU.subtract), 17 + m)
            dve.wait_ge(S["c_act"], 3)
            step(dve.tensor_tensor(ckv_lo[:], ckv[:], f32(ckv_hi[:]), ALU.subtract), 19)
            dve.wait_ge(S["tab_in"], 16)
            dve.wait_ge(S["c_stev"], 9)
            step(dve.tensor_scalar(tab_q[:], tab_q[:], gqr, None, ALU.mult), 20)
            step(dve.reciprocal(rs_v[:], rs_v[:]), 21)

            with dve.Fori(0, KD) as i:
                dve.wait_ge(S["sp_vin"], 16 * i + 16)
                dve.tensor_tensor(vt[:], vt[:], rs_v[:], ALU.mult).then_inc(S["sp_vn"], 1)
                dve.wait_ge(S["sp_bin"], 32 * i + 32)
                dve.wait_ge(S["sp_uin"], 16 * i + 16)
                dve.wait_ge(S["sp_stored"], at("sp_stored", 16 * i))
                for b, (t0, tn) in enumerate(BLOCKS):
                    dve.wait_ge(S["sp_m"], at("sp_m", 3 * i + (b + 1)))
                    dve.scalar_tensor_tensor(
                        out=yt[:, t0:t0 + tn].rearrange("p (c q) -> p c q", q=P),
                        in0=bank(7 - b % 2, tn).rearrange("p (c q) -> p c q", q=P), scalar=vg,
                        in1=bb[:].unsqueeze(1).to_broadcast([P, tn // P, P]), op0=ALU.mult,
                        op1=ALU.add).then_inc(S["sp_act"], 1)
                    dve.wait_ge(S["sp_act"], at("sp_act", 3 * i + (b + 1)))
                    dve.tensor_tensor(yt[:, t0:t0 + tn], yt[:, t0:t0 + tn], ut[:, t0:t0 + tn],
                                      ALU.mult).then_inc(S["sp_y"], 1)

            with dve.Fori(0, KD // 2) as i:
                for j in range(2):
                    dve.wait_ge(S["ld_hi"], 2 * i + (j + 1))
                    dve.tensor_tensor(act_lo[:, 2 * i + j, :], stg[:, j, :], f32(act_hi[:, 2 * i + j, :]),
                                      ALU.subtract).then_inc(S["ld_lo"], 1)
            dve.wait_ge(S["ld_lo"], at("ld_lo", KD))

            def split_lo(n0, src):
                with dve.Fori(0, KD) as k:
                    dve.wait_ge(S["ld_hi"], k + (n0 + 1))
                    dve.tensor_tensor(act_lo[:, k, :], src[:, k, :], f32(act_hi[:, k, :]),
                                      ALU.subtract).then_inc(S["ld_lo"], 1)

            def gate_a(i, j, g, uses):
                dve.wait_ge(gt_in[j], 16 * i + 16)
                if uses is not None:
                    dve.wait_ge(stored[j], uses)
                for b, (t0, tn) in enumerate(BLOCKS):
                    dve.wait_ge(S["blk"], 3 * g + (b + 1))
                    dve.tensor_tensor(stg[:, j, t0:t0 + tn], lin_set(j, b), gt[:, j, t0:t0 + tn],
                                      ALU.mult).then_inc(S["evac"], 1)
            with dve.Fori(0, KD // 2) as i:
                for j in range(2):
                    gate_a(i, j, 2 * i + (G_A + j), 16 * i + 16 * 2 * KD)

            dve.wait_ge(S["blk"], 3 * G_B)
            dve.memset(f32(krl[ROPE:P]), 0.0).then_inc(S["c_dve"], 1)
            dve.wait_ge(S["kr_pe"], 1)
            dve.tensor_copy(kr_sum, bank(7, NCH)).then_inc(S["c_dve"], 1)
            dve.wait_ge(S["c_dve"], 23)
            with dve.Fori(0, H) as h:
                def own(name):
                    dve.wait_ge(S["ap_dve"], at("ap_dve", DVE_STEPS * h + DVE_STEP[name]))

                def acts(name):
                    dve.wait_ge(S["ap_act"], at("ap_act", ACT_STEPS * h + ACT_STEP[name]))

                def products(name):
                    dve.wait_ge(S["ap_pe"], at("ap_pe", PE_STEPS * h + PE_STEP[name]))

                def done(i_):
                    i_.then_inc(S["ap_dve"], 1)

                def turned(b):
                    t0, tn = BLOCKS[b]
                    t = slice(t0, t0 + tn)
                    acts(f"sq_qr{b}")
                    done(dve.tensor_tensor(rt1[:, t], lin_set(0, b)[0:ROPE], tab_q[0:ROPE, t], ALU.mult))
                    done(dve.tensor_tensor(rt2[:, t], lin_set(0, b)[ROPE:P], tab_q[ROPE:P, t], ALU.mult))

                products("sum_k")
                done(dve.tensor_tensor(rk_v, kr_sum, bank(6, NCH), ALU.add))
                acts("q_hi")
                done(dve.scalar_tensor_tensor(out=q_lo[:], in0=lin_all(1), scalar=gq, in1=f32(q_hi[:]),
                                              op0=ALU.mult, op1=ALU.subtract))
                acts("rk_s")
                done(dve.reciprocal(rk_r, rk_s))
                own("rk_r")
                done(dve.tensor_tensor(diag[:].rearrange("p (c t) -> p c t", t=P),
                                       ident[:].unsqueeze(1).to_broadcast([P, NCH, P]),
                                       rk_r.unsqueeze(2).to_broadcast([P, NCH, P]), ALU.mult))
                acts("v_hi")
                done(dve.tensor_tensor(v_lo[:], lin_all(0), f32(v_hi[:]), ALU.subtract))
                products("scale_k")
                done(dve.tensor_tensor(kf[:], kf[:], lin_all(1), ALU.mult))
                done(dve.tensor_tensor(rt3, krf[0:ROPE], lin_all(1)[0:ROPE], ALU.mult))
                turned(0)
                acts("k_hi")
                done(dve.tensor_tensor(k_lo[:], kf[:], f32(k_hi[:]), ALU.subtract))
                turned(1)
                turned(2)
                own("rt_2")
                done(dve.tensor_tensor(rt1, rt1, rt2, ALU.add))
                acts("qr2_up")
                done(dve.tensor_tensor(qr2[ROPE:P], rt1, f32(qr2[0:ROPE]), ALU.subtract))
                products("sum_q")
                done(dve.tensor_copy(rq_r, bank(7, NCH)))
                own("rq_sum")
                done(dve.tensor_tensor(rq_v, rq_r, bank(7)[:, NCH:2 * NCH], ALU.add))
                acts("rq_s")
                done(dve.reciprocal(rq_r, rq_s))
                own("rq_r")
                done(dve.tensor_scalar(rq, rq_r, SCALE, None, ALU.mult))
                own("rq")

                def keys(c):
                    return TP if c < NCH_P else TS

                def top(c):
                    n = keys(c)
                    dve.wait_ge(S["qk_pe"], at("qk_pe", NCH * h + (c + 1)))
                    dve.tensor_reduce(mx[:, c:c + 1], bank(s_bank(c), n), AX_X, ALU.max).then_inc(S["mx_dve"], 1)
                    dve.wait_ge(S["mx_dve"], at("mx_dve", NCH * h + (c + 1)))
                    dve.tensor_scalar(nmx[:, c:c + 1], mx[:, c:c + 1], rq[:, c:c + 1], -1.0, ALU.mult,
                                      ALU.mult).then_inc(S["nm_dve"], 1)

                def inverse(c):
                    dve.wait_ge(S["ex_act"], at("ex_act", NCH * h + (c + 1)))
                    dve.reciprocal(prec[:, c:c + 1], psumr[:, c:c + 1]).then_inc(S["rc_dve"], 1)

                def norm(c):
                    n = keys(c)
                    dve.wait_ge(S["rc_dve"], at("rc_dve", NCH * h + (c + 1)))
                    dve.tensor_scalar(prob[:, c % 2, 0:n], prob[:, c % 2, 0:n], prec[:, c:c + 1], None,
                                      ALU.mult).then_inc(S["pr_dve"], 1)

                def low(c):
                    n = keys(c) // P
                    o = (c % NCH_P) % 4 * P
                    dve.wait_ge(S["th_act"], at("th_act", NCH * h + (c + 1)))
                    dve.tensor_tensor(pt_lo[:, 0:n, o:o + P], bank(t_bank(c), n * P).rearrange("p (k q) -> p k q", q=P),
                                      f32(pt_hi[:, 0:n, o:o + P]), ALU.subtract).then_inc(S["tl_dve"], 1)

                for c in range(NCH + 2):
                    if c < NCH:
                        top(c)
                    if c > 1:
                        low(c - 2)
                    if c < NCH:
                        inverse(c)
                        if c % 2:
                            norm(c)

            split_lo(KD, o_all)
            def gate_b(i, j, g):
                dve.wait_ge(gt_in[j], 16 * i + (16 * KD // 2 + 16))
                for b, (t0, tn) in enumerate(BLOCKS):
                    dve.wait_ge(S["blk"], 3 * g + (b + 1))
                    dve.tensor_tensor(gt[:, j, t0:t0 + tn], lin_set(j, b), gt[:, j, t0:t0 + tn],
                                      ALU.mult).then_inc(S["evac"], 1)
                dve.wait_ge(S["evac"], 3 * g + 3)
                z = z_all[:, 2 * i + j, :]
                dve.tensor_tensor(z, z, gt[:, j, :], ALU.add).then_inc(S["z_sum"], 1)
            dve.wait_ge(S["za_in0"], 16)
            for j in range(2):
                gate_b(0, j, G_B + j)
            dve.wait_ge(S["za_in1"], 16)
            with dve.Fori(1, KD // 2) as i:
                for j in range(2):
                    gate_b(i, j, 2 * i + (G_B + j))
            split_lo(2 * KD, z_all)
            dve.wait_ge(S["x2_in"], 32)

            def residual(q, c, acc):
                dve.wait_ge(S["out_pe"], q * NCH + (c + 1))
                x = x2[:, c, bass.ds(q * QN, QN)]
                dve.tensor_tensor(x, bank(acc)[:, 0:QN], x, ALU.add).then_inc(S["x2_dve"], 1)
            for c in range(NCH):
                residual(0, c, c if c < 8 else 4 + c % 2)
            with dve.Fori(1, QS - 1) as q:
                for c in range(NCH):
                    residual(q, c, 4 + c % 2)
            dve.wait_ge(S["r_in"], 32)
            dve.wait_ge(S["w_lo_s"], G_OUT + 2 * QS)
            for n in range(NCH):
                residual(QS - 1, n, 4 + n % 2)
                dve.wait_ge(S["r_std"], n + 1)
                dve.reciprocal(rstd2[:, n:n + 1], std2[:, n:n + 1]).then_inc(S["r_rec"], 1)
                dve.wait_ge(S["r_rec"], n + 1)
                if n > 1:
                    dve.wait_ge(S["r_t"], n - 1)
                    dve.wait_ge(S[f"h_out{n % 2}"], 16 * (n // 2))
                dve.scalar_tensor_tensor(out=h2[:, n % 2].rearrange("p k t -> p (k t)"), in0=x2[:, n, :],
                                         scalar=rstd2[:, n:n + 1], in1=g2b[:], op0=ALU.mult,
                                         op1=ALU.mult).then_inc(S["r_h"], 1)

            def rstep(i_, n):
                i_.then_inc(S["r_dve"], 1)
                dve.wait_ge(S["r_dve"], n)
            dve.wait_ge(S["rt_pe0"], NCH)
            logit = bank(6, NCH * E).rearrange("p (c e) -> p c e", e=E)
            rstep(dve.tensor_reduce(lmx, logit, AX_X, ALU.max), 1)
            rstep(dve.tensor_tensor(lg[:], logit, lmx.unsqueeze(2).to_broadcast([P, NCH, E]), ALU.subtract), 2)
            dve.wait_ge(S["r_exp"], 1)
            rstep(dve.tensor_reduce(lsum, aff[:], AX_X, ALU.add), 3)
            rstep(dve.reciprocal(lrec, lsum), 4)
            rstep(dve.tensor_tensor(aff[:], aff[:], lrec.unsqueeze(2).to_broadcast([P, NCH, E]), ALU.mult), 5)

            dve.wait_ge(S["a_T"], 1)
            count = [0]

            def kstep(i_):
                count[0] += 1
                i_.then_inc(S["tk"], 1)
                dve.wait_ge(S["tk"], count[0])
            for grp, (t0, tn, cap) in enumerate(((0, TP, CAP_P), (TP, TS, CAP_S))):
                work = affT[:, t0:t0 + tn]
                for r in range(cap // 8):
                    v, x = topv[:, grp, 8 * r:8 * r + 8], topi[:, grp, 8 * r:8 * r + 8]
                    kstep(dve.max(v, work))
                    kstep(dve.max_index(x, v, work))
                    kstep(dve.match_replace(work, v, work, -1.0))
            kstep(dve.tensor_copy(topv[:, 1, CAP_S:P].rearrange("e (g c) -> e g c", c=CAP_S),
                                  topv[:, 1, 0:CAP_S].unsqueeze(1).to_broadcast([E, GRP - 1, CAP_S])))
            kstep(dve.tensor_copy(topi[:, 1, CAP_S:P].rearrange("e (g c) -> e g c", c=CAP_S),
                                  topi[:, 1, 0:CAP_S].unsqueeze(1).to_broadcast([E, GRP - 1, CAP_S])))
            kstep(dve.tensor_copy(topf[:], topi[:]))
            dve.wait_ge(S["rt_pe"], 4)
            for n in range(2):
                dve.tensor_copy(gates[:, n], bank(3)[:, n * E:(n + 1) * E]).then_inc(S["rows_s"], 1)
                dve.tensor_copy(rows[:, n], bank(3)[:, (n + 2) * E:(n + 3) * E]).then_inc(S["rows_s"], 1)
            dve.tensor_scalar(rows[:, 2], bank(3)[:, 3 * E:4 * E], float(TP), None, ALU.add).then_inc(S["rows_s"], 1)
            dve.wait_ge(S["rows_s"], 5)
            dve.wait_ge(S["y_out"], 32)

            def frame(e):
                is0, is1, is_last = (isinstance(e, int) and e == v for v in (0, 1, E))
                more = not (isinstance(e, int) and e >= E - 1)
                for n, (kind, ee, kk, q, slot) in enumerate(pieces(e)):
                    l = n + (8 if is_last else 0)
                    if is_last and n == 0:
                        out(e - 2)
                        hidden(e - 1)
                    dve.wait_ge(S["e_hi"], q + 1)
                    pt = part(l, is0) if not is_last else q % 3
                    dve.tensor_tensor(elo[:, pt], raw[:, slot], f32(ehi[:, pt]), ALU.subtract).then_inc(S["e_lo"], 1)
                    if l == 1 and not (is0 or is1):
                        out(e - 2)
                    if l == 2 and not is0:
                        hidden(e - 1)
                    if l == (7 if is0 else 9) and not is_last:
                        gated(e)
                    if more and l == (7 if is0 else 10):
                        rows_lo(e + 1)
                if is_last:
                    out(e - 1)

            def gated(e):
                dve.wait_ge(S["e_pe"], 8 if isinstance(e, int) and e == 0 else 12 * e + 4)
                dve.wait_ge(S["silu_p"], e + 1)
                dve.wait_ge(S["silu_s"], e + 1)
                dve.tensor_tensor(hid[:], bank(2, D), hid[:], ALU.mult).then_inc(S["mul_p"], 1)
                dve.tensor_tensor(hid_s[:], bank(7, GN), hid_s[:], ALU.mult).then_inc(S["mul_s"], 1)

            def rows_lo(e):
                dve.wait_ge(S["xh_act"], e + 1)
                dve.tensor_tensor(xT_lo[:], bank(0, D).rearrange("p (k t) -> p k t", k=KD), f32(xT_hi[:]),
                                  ALU.subtract).then_inc(S["xl_dve"], 1)
                dve.wait_ge(S["txs_pe"], e + 1)
                dve.tensor_copy(xT_s[:], bank(7, GN).rearrange("p (k t) -> p k t", k=KD)).then_inc(S["xs_dve"], 1)

            def hidden(e):
                dve.wait_ge(S["hh_act"], e + 1)
                dve.tensor_tensor(hT_lo[:], bank(2, D).rearrange("p (k t) -> p k t", k=KD), f32(hT_hi[:]),
                                  ALU.subtract).then_inc(S["hl_dve"], 1)
                dve.wait_ge(S["ths_pe"], e + 1)
                dve.tensor_copy(hT_s[:], bank(7, GN)).then_inc(S["hs_dve"], 1)

            def out(e):
                dve.wait_ge(S["e_pe"], 12 * E if isinstance(e, int) and e == E - 1 else 12 * e + 20)
                if not (isinstance(e, int) and e == 0):
                    dve.wait_ge(S["scat"], 32 * e)
                for g in range(GRP):
                    r = slice(CAP_S * g, CAP_S * (g + 1))
                    last = dve.tensor_scalar(ob_s[:, g * GN:(g + 1) * GN], bank(6, GN)[r], gates[r, 1, bass.ds(e, 1)],
                                             None, ALU.mult)
                last.then_inc(S["ob_dve"], 1)

            rows_lo(0)
            run_frames(dve, frame)


_INS = ['x_prompt', 'x_sample', 'norm1_g', 'w_in', 'v_norm_g', 'w_spatial', 'b_spatial', 'w_a_out',
        'q_norm_g', 'w_uq', 'kv_norm_g', 'w_ukv', 'q_head_g', 'k_head_g', 'w_b_out', 'w_out',
        'norm2_g', 'w_router', 'w_gate', 'w_up', 'w_down']


def rope_table():
    import numpy as np
    half = ROPE // 2
    freq = (np.float32(10000.0) ** (-np.arange(half, dtype=np.float32) / np.float32(half))).astype(np.float32)
    pos = np.concatenate([np.arange(TP), np.arange(TS)]).astype(np.float32)
    ang = (freq[:, None] * pos[None, :]).astype(np.float32).astype(np.float64)
    c, s = np.cos(ang), np.sin(ang)
    return np.ascontiguousarray(np.concatenate([c, c, -s, s]).astype(np.float32))


def kernel(**inputs):
    import numpy as np
    import concourse.bacc as bacc
    from concourse.bass_utils import run_bass_kernel_spmd

    nc = bacc.Bacc("TRN2", target_bir_lowering=False, num_devices=1)
    arrays, args = {}, []
    for name in _INS:
        a = np.ascontiguousarray(inputs[name])
        a = a.reshape(a.shape[1:])
        arrays[f"in_{name}"] = a
    arrays["rope_cs"] = rope_table()
    for name, a in arrays.items():
        args.append(nc.dram_tensor(name, a.shape, mybir.dt.from_np(a.dtype), kind="ExternalInput").ap())
    args.append(nc.dram_tensor("y_p", (TP, D), F32, kind="ExternalOutput").ap())
    args.append(nc.dram_tensor("y_s", (TS, D), F32, kind="ExternalOutput").ap())
    build(nc, *args)
    r = run_bass_kernel_spmd(nc, [arrays], core_ids=[0])
    return (r.results[0]["y_p"].reshape(1, TP, D), r.results[0]["y_s"].reshape(1, TS, D))
```

```python
from contextlib import ExitStack

import concourse.bass as bass
from concourse import mybir

F32 = mybir.dt.float32
F32R = mybir.dt.float32r
U32 = mybir.dt.uint32
ALU = mybir.AluOpType
ACT = mybir.ActivationFunctionType
AX_X = mybir.AxisListType.X

P = 128
D = 1024
KD = D // P
TP, TS = 1024, 256
T = TP + TS
NCH = T // P
NCH_P = TP // P
BLOCKS = [(0, 512), (512, 512), (1024, 256)]
BANK = 512
H = 8
NOPE, ROPE = 128, 64
HEAD = NOPE + ROPE
QR, KVR = 256, 128
OFF_CQ = 2 * D
OFF_KR = OFF_CQ + QR + KVR
OFF_GA = OFF_KR + ROPE
EPS = 1e-6
SCALE = float(HEAD) ** -0.5
E = 16
CAP_P, CAP_S = 2 * TP // E, 2 * TS // E
GRP = P // CAP_S
GN = D // GRP
HALF = TP // 2
L_A, L_B, L_S = 0, 32, 64
LISTS = L_S + E
QN = 2 * P
QS = D // QN

G_C, G_V, G_U, G_GATE, G_A, G_B, G_OUT = 0, 4, 12, 20, 36, 44, 52


def build(nc, x_p, x_s, norm1_g, w_in, v_norm_g, w_spatial, b_spatial, w_a_out, q_norm_g, w_uq,
          kv_norm_g, w_ukv, q_head_g, k_head_g, w_b_out, w_out, norm2_g, w_router, w_gate, w_up,
          w_down, rope_cs, y_p, y_s):
    ctx = ExitStack()
    with ctx:
        def sem(name):
            return ctx.enter_context(nc.semaphore(name))

        def sb(stack, name, shape, dt=F32):
            return stack.enter_context(nc.sbuf_tensor(name, shape, dt))

        def f32(ap):
            return ap.bitcast(F32)

        v_d = nc.dram_tensor("v_d", [KD, P, T], F32).ap()
        u_d = nc.dram_tensor("u_d", [KD, P, T], F32).ap()
        g_d = nc.dram_tensor("g_d", [2 * KD, P, T], F32).ap()
        y_d = nc.dram_tensor("ya_d", [KD, P, T], F32).ap()
        za_d = nc.dram_tensor("za_d", [KD, P, T], F32).ap()
        o_d = nc.dram_tensor("o_d", [H, P, T], F32).ap()
        h_d = nc.dram_tensor("h_d", [T, D], F32).ap()

        PS = ctx.enter_context(nc.psum_tensor("PS", [P, 8 * BANK], F32))

        def bank(b, n=BANK, w=1):
            return PS[:, b * BANK:b * BANK + n * w]

        def lin_set(j, b):
            o = 3 * BANK * j + BLOCKS[b][0]
            return PS[:, o:o + BLOCKS[b][1]]

        def lin_all(j):
            return PS[:, 3 * BANK * j:3 * BANK * j + T]

        ident = sb(ctx, "ident", [P, P])
        ones = sb(ctx, "ones", [P, P])
        flip = sb(ctx, "flip", [P, P])
        small = sb(ctx, "small", [P, 256])
        g1c = small[:, 0:8]
        gqn = small[:, 8:10]
        gkvn = small[:, 10:11]
        gq = small[:, 11:12]
        gqr = small[:, 12:13]
        gk = small[:, 13:14]
        gkr = small[:, 14:15]
        ssq1 = small[:, 16:26]
        rstd1 = small[:, 36:46]
        std1 = small[:, 46:56]
        ssq2 = small[:, 56:66]
        rstd2 = small[:, 76:86]
        std2 = small[:, 86:96]
        rq_v = small[:, 96:106]
        rq_s = small[:, 106:116]
        rq_r = small[:, 116:126]
        rq = small[:, 126:136]
        mx = small[:, 136:146]
        nmx = small[:, 146:156]
        psumr = small[:, 156:166]
        prec = small[:, 166:176]
        lmx = small[:, 176:186]
        lsum = small[:, 186:196]
        lrec = small[:, 196:206]
        vg = small[:, 206:207]
        epsc = small[:, 209:210]
        rk_v = small[:, 210:220]
        rk_s = small[:, 220:230]
        kr_sum = small[:, 241:251]
        rk_r = small[:, 230:240]
        spare = small[:, 240:241]


        w_raw = sb(ctx, "w_raw", [P, 2, KD, P])
        w_hi = sb(ctx, "w_hi", [P, 2, KD, P], F32R)
        w_lo = sb(ctx, "w_lo", [P, 2, KD, P], F32R)
        stg = sb(ctx, "stg", [P, 2, T])
        gt = sb(ctx, "gt", [P, 2, T])

        region_a = 2 * KD * T * 4
        with ExitStack() as s:
            act_hi = sb(s, "act_hi", [P, KD, T], F32R)
            act_lo = sb(s, "act_lo", [P, KD, T], F32R)
            with ExitStack() as s2:
                x_in = sb(s2, "x_in", [P, NCH, D])
                xn = sb(s2, "xn", [P, 2, D])
                htmp = sb(s2, "htmp", [P, 2, KD, P])
            with ExitStack() as s2:
                tab_q = sb(s2, "tab_q", [P, T])
                cq_hi = sb(s2, "cq_hi", [P, 2, T], F32R)
                cq_lo = sb(s2, "cq_lo", [P, 2, T], F32R)
                ckv = sb(s2, "ckv", [P, T])
                krf = sb(s2, "krf", [P, T])
                sq_kr = sb(s2, "sq_kr", [P, T])
                ckv_hi = sb(s2, "ckv_hi", [P, T], F32R)
                ckv_lo = sb(s2, "ckv_lo", [P, T], F32R)
                with ExitStack() as s3:
                    rs_v = sb(s3, "rs_v", [P, T])
                    with ExitStack() as s4:
                        acc_v = sb(s4, "acc_v", [P, T])
                        ct = sb(s4, "ct", [P, 3, T])
                    with ExitStack() as s4:
                        vt = sb(s4, "vt", [P, T])
                        vtok = sb(s4, "vtok", [P, T])
                        yt = sb(s4, "yt", [P, T])
                        ws = sb(s4, "ws", [P, P])
                        wsT = sb(s4, "wsT", [P, P])
                        bb = sb(s4, "bb", [P, P])
                with ExitStack() as s3:
                    aq_raw = sb(s3, "aq_raw", [P, 2, 256])
                    aq_hi = sb(s3, "aq_hi", [P, 2, 256], F32R)
                    aq_lo = sb(s3, "aq_lo", [P, 2, 256], F32R)
                    akv_raw = sb(s3, "akv_raw", [P, 256])
                    ak_hi = sb(s3, "ak_hi", [P, P], F32R)
                    ak_lo = sb(s3, "ak_lo", [P, P], F32R)
                    kf = sb(s3, "kf", [P, T])
                    diag = sb(s3, "diag", [P, T])
                    prob = sb(s3, "prob", [P, 2, TP])
                    ostg = sb(s3, "ostg", [P, 2, BANK])
            with ExitStack() as s2:
                o_all = sb(s2, "o_all", [P, KD, T])
                z_all = sb(s2, "z_all", [P, KD, T])
            with ExitStack() as s2:
                with ExitStack() as s3:
                    x2 = sb(s3, "x2", [P, NCH, D])
                with ExitStack() as s3:
                    xs_p = sb(s3, "xs_p", [P, D])
                    xs_s = sb(s3, "xs_s", [CAP_S, D])
                    xT_hi = sb(s3, "xT_hi", [P, KD, P], F32R)
                    xT_lo = sb(s3, "xT_lo", [P, KD, P], F32R)
                    hT_hi = sb(s3, "hT_hi", [P, KD, P], F32R)
                    hT_lo = sb(s3, "hT_lo", [P, KD, P], F32R)
                    hid = sb(s3, "hid", [P, D])
                    ob_p = sb(s3, "ob_p", [P, D])
                    ob_s = sb(s3, "ob_s", [CAP_S, D])
                    xT_s = sb(s3, "xT_s", [P, KD, CAP_S])
                    hid_s = sb(s3, "hid_s", [P, GN])
                    hT_s = sb(s3, "hT_s", [P, GN])
                    ixg_p = sb(s3, "ixg_p", [P, 1], U32)
                    ixg_s = sb(s3, "ixg_s", [CAP_S, 1], U32)
                    ixs_p = sb(s3, "ixs_p", [P, 1], U32)
                    ixs_s = sb(s3, "ixs_s", [CAP_S, 1], U32)
                sb(s2, "x2_room", [P, NCH, D])
                g2b = sb(s2, "g2b", [P, D])
                wr = sb(s2, "wr", [P, KD, E])
                lg = sb(s2, "lg", [P, NCH, E])
                aff = sb(s2, "aff", [P, NCH, E])
                lists = sb(s2, "lists", [P, HALF // P, LISTS])
                work = sb(s2, "work", [LISTS, HALF])
                topv = sb(s2, "topv", [LISTS, P])
                topi = sb(s2, "topi", [LISTS, P], U32)
                topf = sb(s2, "topf", [LISTS, P])
                chosen = sb(s2, "chosen", [P, 2, LISTS])
                pick = sb(s2, "pick", [P, 3, E])
                gates = sb(s2, "gates", [P, 2, E])
                rows = sb(s2, "rows", [P, 3, E], U32)
                w2_hi = sb(s2, "w2_hi", [P, 2, KD, P], F32R)
                w2_lo = sb(s2, "w2_lo", [P, 2, KD, P], F32R)
        with ExitStack() as s:
            q_hi = sb(s, "q_hi", [P, T], F32R)
            q_lo = sb(s, "q_lo", [P, T], F32R)
            qr2 = sb(s, "qr2", [P, T], F32R)
            k_hi = sb(s, "k_hi", [P, T], F32R)
            k_lo = sb(s, "k_lo", [P, T], F32R)
            kr2 = sb(s, "kr2", [P, T], F32R)
            krl = sb(s, "krl", [P, T], F32R)
            v_hi = sb(s, "v_hi", [P, T], F32R)
            v_lo = sb(s, "v_lo", [P, T], F32R)
            pt_hi = sb(s, "pt_hi", [P, NCH_P, BANK], F32R)
            pt_lo = sb(s, "pt_lo", [P, NCH_P, BANK], F32R)
        with ExitStack() as s:
            raw = sb(s, "raw", [P, 4, 2, D])
            ehi = sb(s, "ehi", [P, 3, 2, D], F32R)
            elo = sb(s, "elo", [P, 3, 2, D], F32R)
        h2, h2T = w_raw[:, :, :, :], gt[:, :, 0:D]
        tab_k, sq_v = gt[:, 0, :], gt[:, 1, :]
        ut = gt[:, 0, :]
        sq_q, sq_qr, sq_k = stg[:, 0, :], gt[:, 0, :], gt[:, 1, :]
        rt1, rt2 = stg[0:ROPE, 1, :], prob[:, :, :].rearrange("p a n -> p (a n)")[0:ROPE, 0:T]
        rt3 = diag[0:ROPE, :]

        names = []
        names += """consts params g1_in tab_in n1_ssq n1_std n1_rec n1_xn n1_tr n1_h n1_hi n1_lo_even
            n1_lo_odd""".split()
        names += """w_in0 w_in1 w_rounded w_split tile_pe evac stored0 stored1""".split()
        names += """v_sq v_acc latent_dve latent_act sum_pe rms_act""".split()
        names += """sp_vin sp_wsin sp_uin sp_bin sp_vn sp_t sp_tok sp_m sp_act sp_y sp_stored""".split()
        names += """ld_in0 ld_in1 part_hi part_lo gt_in0 gt_in1 o_back o_back_last za_in0 za_in1 z_sum""".split()
        names += """aw_in aw_hi aw_lo ap_pe ap_act ap_dve kr_pe krl_pool""".split()
        names += """scores_pe max_dve bias_dve exp_act recip_dve prob_act prob_dve probT_pe pt_hi_act
            pt_lo_dve values_pe values_act o_st0 o_st1""".split()
        names += """x2_in out_pe x2_dve""".split()
        names += """r_in logits_pe r_ssq r_std r_rec h_dve hT_pe hT_act r_exp r_dve y_out h_out0 h_out1
            aff_pe affT_act topk_dve chosen_pe rows_dve""".split()
        names += """e_in0 e_in1 e_in2 e_in3 e_hi e_lo e_pe""".split()
        names += """ix_g ix_s gathered tx_pe txs_pe xh_act xl_dve xs_dve silu_p silu_s mul_p mul_s th_pe
            ths_pe hh_act hl_dve hs_dve ob_act ob_dve scattered""".split()
        names += """passed_pool passed_pe""".split()
        S = {n: sem(n) for n in names}
        credit = {n: 2 for n in """sp_t sp_y sp_m sp_act sp_tok sp_vn aw_lo aw_hi ap_pe ap_act ap_dve
            scores_pe max_dve bias_dve exp_act recip_dve prob_act prob_dve probT_pe pt_hi_act
            pt_lo_dve values_pe values_act part_lo z_sum""".split()}
        credit.update(o_st0=32, o_st1=32, sp_stored=32)

        def at(name, n):
            return n + credit.get(name, 0)

        w_in_s = [S["w_in0"], S["w_in1"]]
        stored = [S["stored0"], S["stored1"]]
        x_in_s = [sem(f"x_loaded{n}") for n in range(5)]
        ld_in = [S["ld_in0"], S["ld_in1"]]
        gt_in = [S["gt_in0"], S["gt_in1"]]

        def mm3(pe, out, lh, ll, rh, rl, first, last):
            pe.matmul(out, lh, rh, start=first, stop=False)
            pe.matmul(out, lh, rl, start=False, stop=False)
            return pe.matmul(out, ll, rh, start=False, stop=last)

        w_in_v = w_in.rearrange("(k p) n -> p k n", p=P)
        x_view = [x_p.rearrange("(c p) d -> p c d", p=P), x_s.rearrange("(c p) d -> p c d", p=P)]

        def w_tile(kind, m):
            if kind in "vug":
                first = {"v": D, "u": 0, "g": OFF_GA}[kind]
                return w_in_v[:, :, bass.ds(m * P + first, P)]
            w = {"a": w_a_out, "b": w_b_out, "o": w_out}[kind]
            return w.rearrange("(k p) n -> p k n", p=P)[:, :, bass.ds(m * P, P)]

        def pieces(e):
            first, last = isinstance(e, int) and e == 0, isinstance(e, int) and e == E
            q0 = 0 if first else 12 * e - 4
            out = []
            if not last:
                out += [("g", e, l, l) for l in range(4)] + [("u", e, l, l + 4) for l in range(4)]
            if not first:
                out += [("d", e - 1, l, (l if last else l + 8)) for l in range(4)]
            return [(kind, ee, kk, q0 + l, l % 4) for kind, ee, kk, l in out]

        def part(l, first):
            return l % 3 if first else (l + 2) % 3

        def loads_of(e, n):
            if isinstance(e, int):
                return 16 * ((0 if e == 0 else 12 * e - 4) + n + 4 >> 2)
            return 48 * e + (16 * (n // 4))

        def run_frames(eng, frame):
            frame(0)
            frame(1)
            with eng.Fori(2, E - 1) as e:
                frame(e)
            frame(E - 1)
            frame(E)

        def numbered(steps):
            out, n = {}, 0
            for step in steps.split():
                name, _, width = step.partition(":")
                n += int(width or 1)
                out[name] = n
            return out, n
        PE_STEP, PE_STEPS = numbered("k:3 q:3 sum_k v:3 scale_k:3 qr0 qr1 qr2 sum_q")
        ACT_STEP, ACT_STEPS = numbered(
            "sqrt_table sq_k kf sq_q q_hi rk_s v_hi sq_qr0 k_hi sq_qr1 kr2_up sq_qr2 kr2_down qr2_up rq_s exp_table")
        DVE_STEP, DVE_STEPS = numbered("rk_v q_lo rk_r diag v_lo kf rt3 rt_0:2 k_lo rt_1:2 rt_2:2 rt1 qr2_down rq_sum rq_v rq_r rq")

        def s_bank(c):
            return 3 if c == NCH - 1 else 2 * (c % 2)

        def t_bank(c):
            return 5 if c == NCH - 1 else 4

        TOPK_STEPS = 3 * CAP_P // 8 - 1 + 3
        ROWS_STEPS = 11

        block = ctx.enter_context(nc.Block())

        @block.sync
        def _(sp):
            def load_w(g, j, view):
                sp.wait_ge(S["w_split"], g - 1)
                sp.dma_start(w_raw[:, j], view).then_inc(w_in_s[j], 16)

            col = lambda a: a.rearrange("(p o) -> p o", o=1)
            for n in range(5):
                src = x_view[0][:, 2 * n:2 * n + 2] if n < 4 else x_view[1][:, 0:2]
                sp.dma_start(x_in[:, 2 * n:2 * n + 2], src).then_inc(x_in_s[n], 16)
                if n == 0:
                    sp.dma_start(g1c, norm1_g.rearrange("(k p) -> p k", p=P),
                                 allow_slow_non_contiguous=True).then_inc(S["g1_in"], 16)
                if n in (1, 2):
                    j = n - 1
                    sp.dma_start(w_raw[:, j], w_in_v[:, :, OFF_CQ + j * P:OFF_CQ + (j + 1) * P]).then_inc(w_in_s[j], 16)
            for dst, src in ((gqn, q_norm_g.rearrange("(k p) -> p k", p=P)), (gkvn, col(kv_norm_g)),
                             (gq, col(q_head_g)[0:NOPE]), (gqr[0:64], col(q_head_g)[NOPE:HEAD]),
                             (gqr[64:96], col(q_head_g)[NOPE + 32:HEAD]),
                             (gqr[96:128], col(q_head_g)[NOPE:NOPE + 32]),
                             (gk, col(k_head_g)[0:NOPE]), (gkr[0:64], col(k_head_g)[NOPE:HEAD]),
                             (gkr[64:96], col(k_head_g)[NOPE + 32:HEAD]),
                             (gkr[96:128], col(k_head_g)[NOPE:NOPE + 32]), (tab_k, rope_cs)):
                sp.dma_start(dst, src, allow_slow_non_contiguous=True).then_inc(S["params"], 16)

            sp.wait_ge(S["w_split"], 1)
            sp.dma_start(w_raw[:, 0], w_in_v[:, :, OFF_CQ + 2 * P:OFF_CQ + 3 * P]).then_inc(w_in_s[0], 16)
            sp.wait_ge(S["w_split"], 2)
            for a, b, c in ((0, 64, 0), (64, 96, 32), (96, 128, 0)):
                sp.dma_start(w_raw[:, 1, :, a:b], w_in_v[:, :, OFF_KR + c:OFF_KR + c + b - a])\
                    .then_inc(w_in_s[1], 16)
            sp.wait_ge(S["n1_lo_even"], NCH // 2)
            sp.wait_ge(S["n1_lo_odd"], NCH // 2)
            sp.dma_start(tab_q[:], rope_cs).then_inc(S["tab_in"], 16)

            for kind, g0 in (("v", G_V), ("u", G_U)):
                with sp.Fori(0, KD // 2) as i:
                    for j in range(2):
                        load_w(g0 + 2 * i + j, j, w_tile(kind, 2 * i + j))

            def gates_and_group(i, weights):
                if weights:
                    load_w(G_GATE + 2 * i, 0, w_tile("g", 2 * i))
                sp.wait_ge(S["sp_t"], at("sp_t", 3 * i))
                sp.dma_start(vt[:], v_d[i]).then_inc(S["sp_vin"], 16)
                sp.dma_start(ws[:], w_spatial[i]).then_inc(S["sp_wsin"], 16)
                if weights:
                    load_w(G_GATE + 2 * i + 1, 1, w_tile("g", 2 * i + 1))
                sp.wait_ge(S["sp_y"], at("sp_y", 3 * i))
                sp.dma_start(ut, u_d[i]).then_inc(S["sp_uin"], 16)
                sp.dma_start(bb[:], b_spatial[bass.ds(i, 1), :].to_broadcast([P, P])).then_inc(S["sp_bin"], 16)
                sp.dma_start(vg, v_norm_g.rearrange("(k p o) -> k p o", p=P, o=1)[i]).then_inc(S["sp_bin"], 16)

            for j in range(2):
                load_w(G_GATE + j, j, w_tile("g", j))
            for j in range(2):
                sp.wait_ge(stored[j], 16 * KD)
            sp.wait_ge(S["latent_dve"], 21)
            gates_and_group(0, False)
            with sp.Fori(1, KD) as i:
                gates_and_group(i, True)

            for j in range(2):
                load_w(G_A + j, j, w_tile("a", j))
            for j in range(2):
                sp.wait_ge(S["sp_stored"], at("sp_stored", 16 * (KD - 1)))
                sp.wait_ge(stored[j], 16 * 2 * KD)
                sp.dma_start(stg[:, j, :], y_d[j]).then_inc(ld_in[j], 16)
            sp.wait_ge(S["sp_stored"], at("sp_stored", 16 * KD))
            with sp.Fori(1, KD // 2) as i:
                for j in range(2):
                    sp.wait_ge(S["part_lo"], at("part_lo", 2 * i + (j - 1)))
                    sp.dma_start(stg[:, j, :], y_d[2 * i + j]).then_inc(ld_in[j], 16)
            for j in range(2):
                sp.dma_start(gt[:, j, :], g_d[j]).then_inc(gt_in[j], 16)
            with sp.Fori(1, KD // 2) as i:
                for j in range(2):
                    load_w(G_A + 2 * i + j, j, w_tile("a", 2 * i + j))
                    sp.wait_ge(S["evac"], 3 * (G_A - 1) + 3 * (2 * i + j))
                    sp.dma_start(gt[:, j, :], g_d[2 * i + j]).then_inc(gt_in[j], 16)

            uq = w_uq.rearrange("(k p) n -> p k n", p=P)
            sp.wait_ge(S["evac"], 3 * G_A)
            with sp.Fori(0, H) as h:
                sp.wait_ge(S["ap_pe"], at("ap_pe", PE_STEPS * h))
                sp.dma_start(aq_raw[:, :, 0:HEAD], uq[:, :, bass.ds(h * HEAD, HEAD)]).then_inc(S["aw_in"], 16)
                sp.dma_start(aq_raw[:, :, 192:224], uq[:, :, bass.ds(h * HEAD + (NOPE + 32), 32)]).then_inc(S["aw_in"], 16)
                sp.dma_start(aq_raw[:, :, 224:256], uq[:, :, bass.ds(h * HEAD + NOPE, 32)]).then_inc(S["aw_in"], 16)
                sp.dma_start(akv_raw[:], w_ukv[:, bass.ds(h * 256, 256)]).then_inc(S["aw_in"], 16)

            for j in range(2):
                load_w(G_B + j, j, w_tile("b", j))
            sp.wait_ge(S["ap_pe"], at("ap_pe", PE_STEPS * H))
            sp.wait_ge(S["ap_dve"], at("ap_dve", DVE_STEPS * H))
            sp.wait_ge(S["ap_act"], at("ap_act", ACT_STEPS * H))
            sp.wait_ge(S["o_st0"], at("o_st0", 32 * (H - 1)))
            sp.wait_ge(S["o_st1"], at("o_st1", 16 * (H - 1)))
            sp.dma_start(o_all[:, 0:H - 1], o_d[0:H - 1].rearrange("h p t -> p h t")).then_inc(S["o_back"], 16)
            for j in range(2):
                sp.dma_start(gt[:, j, :], g_d[KD + j]).then_inc(gt_in[j], 16)
            sp.wait_ge(S["o_st0"], at("o_st0", 32 * H))
            sp.wait_ge(S["o_st1"], at("o_st1", 16 * H))
            sp.dma_start(o_all[:, H - 1], o_d[H - 1]).then_inc(S["o_back_last"], 16)
            for j in range(2):
                sp.wait_ge(stored[j], 16 * 20)
            sp.wait_ge(S["pt_lo_dve"], at("pt_lo_dve", NCH * H))
            for n, (k0, k1) in enumerate(((0, 2), (2, KD))):
                sp.dma_start(z_all[:, k0:k1], za_d[k0:k1].rearrange("k p t -> p k t")).then_inc(S[f"za_in{n}"], 16)
            with sp.Fori(1, KD // 2) as i:
                for j in range(2):
                    load_w(G_B + 2 * i + j, j, w_tile("b", 2 * i + j))
                    sp.wait_ge(S["z_sum"], at("z_sum", 2 * i + (j - 1)))
                    sp.dma_start(gt[:, j, :], g_d[2 * i + (KD + j)]).then_inc(gt_in[j], 16)

            sp.wait_ge(S["part_lo"], at("part_lo", 2 * KD))
            sp.dma_start(x2[:, 0:NCH_P], x_view[0]).then_inc(S["x2_in"], 16)
            sp.dma_start(x2[:, NCH_P:NCH], x_view[1]).then_inc(S["x2_in"], 16)
            with sp.Fori(0, KD // 2) as i:
                for j in range(2):
                    load_w(G_OUT + 2 * i + j, j, w_tile("o", 2 * i + j))
            sp.wait_ge(S["part_lo"], at("part_lo", 3 * KD))
            sp.dma_start(g2b[:], norm2_g.rearrange("(o d) -> o d", o=1).to_broadcast([P, D])).then_inc(S["r_in"], 16)
            sp.dma_start(wr[:], w_router.rearrange("(k p) e -> p k e", p=P)).then_inc(S["r_in"], 16)
            for n in range(NCH):
                sp.wait_ge(S["h_dve"], n + 1)
                sp.dma_start(h_d[n * P:(n + 1) * P], h2[:, n % 2].rearrange("p k t -> p (k t)"))\
                    .then_inc(S[f"h_out{n % 2}"], 16)
            sp.wait_ge(S["x2_dve"], QS * NCH)
            sp.dma_start(y_p.rearrange("(c p) d -> p c d", p=P), x2[:, 0:NCH_P]).then_inc(S["y_out"], 16)
            sp.dma_start(y_s.rearrange("(c p) d -> p c d", p=P), x2[:, NCH_P:NCH]).then_inc(S["y_out"], 16)

            sp.wait_ge(S["out_pe"], QS * NCH)
            mats = {"g": w_gate, "u": w_up, "d": w_down}

            def load_piece(kind, e, kk, q, slot):
                if not isinstance(q, int) or q >= 4:
                    sp.wait_ge(S["e_pe"], q - 3)
                sp.dma_start(raw[:, slot], mats[kind][e].rearrange("(k p) n -> p k n", p=P)[:, 2 * kk:2 * kk + 2])\
                    .then_inc(S[f"e_in{slot}"], 16)

            def frame(e):
                for kind, ee, kk, q, slot in pieces(e):
                    load_piece(kind, ee, kk, q, slot)
            run_frames(sp, frame)
            sp.wait_ge(S["scattered"], 32 * E)

        @block.gpsimd
        def _(pool):
            def settled():
                pool.sem_inc(S["passed_pool"], 1)

            for n, c in credit.items():
                pool.sem_inc(S[n], c)
            pool.memset(ones[:], 1.0).then_inc(S["consts"], 1)
            pool.memset(ident[:], 1.0).then_inc(S["consts"], 1)
            pool.memset(epsc, EPS).then_inc(S["consts"], 1)
            pool.wait_ge(S["consts"], 3)
            pool.affine_select(out=ident[:], in_=ident[:], compare_op=ALU.is_equal, fill=0.0, base=0,
                               pattern=[[-1, P]], channel_multiplier=1).then_inc(S["consts"], 1)
            pool.affine_select(out=flip[:], in_=ones[:], compare_op=ALU.is_equal, fill=0.0, base=1 - P,
                               pattern=[[1, P]], channel_multiplier=1).then_inc(S["consts"], 1)

            def split(g, j, loads):
                pool.wait_ge(w_in_s[j], 16 * loads)
                if not isinstance(g, int) or g > 1:
                    pool.wait_ge(S["tile_pe"], 5 if isinstance(g, int) and g == 2 else 3 * (g - 1))
                settled()
                pool.tensor_scalar(w_hi[:, j], w_raw[:, j], 1.0, 0.0, ALU.mult, ALU.add).then_inc(S["w_rounded"], 1)
                pool.wait_ge(S["w_rounded"], g + 1)
                pool.tensor_tensor(w_lo[:, j], w_raw[:, j], f32(w_hi[:, j]), ALU.subtract).then_inc(S["w_split"], 1)

            for n in range(0, NCH, 2):
                pool.wait_ge(S["n1_hi"], n + 1)
                pool.tensor_tensor(act_lo[:, :, n * P:(n + 1) * P], htmp[:, 0], f32(act_hi[:, :, n * P:(n + 1) * P]),
                                   ALU.subtract).then_inc(S["n1_lo_even"], 1)
                if n in (2, 4):
                    split(n // 2 - 1, n // 2 - 1, 1)
            split(2, 0, 2)
            split(3, 1, 4)

            def split_loop(g0):
                with pool.Fori(0, KD // 2) as i:
                    for j in range(2):
                        split(g0 + 2 * i + j, j, i + (g0 // 2 + 1 + 2 * j))

            split_loop(G_V)
            split_loop(G_U)
            with pool.Fori(0, KD) as i:
                split(G_GATE + 2 * i, 0, i + (G_GATE // 2 + 1))
                split(G_GATE + 2 * i + 1, 1, i + (G_GATE // 2 + 3))
            split_loop(G_A)

            def head_weights(h):
                pool.wait_ge(S["aw_in"], 64 * h + 64)
                settled()
                pool.tensor_scalar(ak_hi[:], akv_raw[:, 0:P], 1.0, 0.0, ALU.mult, ALU.add).then_inc(S["aw_hi"], 1)
                pool.tensor_scalar(aq_hi[:], aq_raw[:], 1.0, 0.0, ALU.mult, ALU.add).then_inc(S["aw_hi"], 1)
                pool.wait_ge(S["aw_hi"], at("aw_hi", 2 * h + 2))
                pool.tensor_tensor(ak_lo[:], akv_raw[:, 0:P], f32(ak_hi[:]), ALU.subtract).then_inc(S["aw_lo"], 1)
                pool.tensor_tensor(aq_lo[:], aq_raw[:], f32(aq_hi[:]), ALU.subtract).then_inc(S["aw_lo"], 1)

            def head(h, more):
                pool.wait_ge(S["ap_act"], at("ap_act", ACT_STEPS * h + ACT_STEP["kr2_up"]))
                settled()
                pool.tensor_tensor(krl[0:ROPE], rt3, f32(kr2[0:ROPE]), ALU.subtract).then_inc(S["krl_pool"], 1)
                if more:
                    head_weights(h + 1)

            head_weights(0)
            with pool.Fori(0, H - 1) as h:
                head(h, True)
            head(H - 1, False)
            split_loop(G_B)

            for q in range(QS):
                wh, wl = (w_hi, w_lo) if q % 2 == 0 else (w2_hi, w2_lo)
                if q == 1:
                    pool.wait_ge(S["part_lo"], at("part_lo", 3 * KD))
                elif q > 1:
                    pool.wait_ge(S["out_pe"], (q - 1) * NCH)
                for j in range(2):
                    g = G_OUT + 2 * q + j
                    pool.wait_ge(w_in_s[j], 16 * (g // 2 + 1 + 2 * j))
                    if q == 0:
                        pool.wait_ge(S["tile_pe"], 3 * (g - 1))
                    settled()
                    pool.tensor_scalar(wh[:, j], w_raw[:, j], 1.0, 0.0, ALU.mult, ALU.add).then_inc(S["w_rounded"], 1)
                    pool.wait_ge(S["w_rounded"], g + 1)
                    pool.tensor_tensor(wl[:, j], w_raw[:, j], f32(wh[:, j]), ALU.subtract).then_inc(S["w_split"], 1)
            def gather(e):
                if not (isinstance(e, int) and e == 0):
                    pool.wait_ge(S["tx_pe"], e)
                    pool.wait_ge(S["txs_pe"], e)
                settled()
                for dst, k, n in ((ixg_p, 0, P), (ixg_s, 2, CAP_S)):
                    pool.tensor_copy(dst[:], rows[0:n, k, bass.ds(e, 1)]).then_inc(S["ix_g"], 1)
                pool.wait_ge(S["ix_g"], 2 * e + 2)
                settled()
                pool.indirect_dma_start(xs_p[:], None, h_d, bass.IndirectOffsetOnAxis(ap=ixg_p[:, 0:1], axis=0)).then_inc(S["gathered"], 16)
                pool.indirect_dma_start(xs_s[:], None, h_d, bass.IndirectOffsetOnAxis(ap=ixg_s[:, 0:1], axis=0)).then_inc(S["gathered"], 16)
                pool.wait_ge(S["gathered"], 32 * e + 32)

            def scatter(e):
                settled()
                for dst, k, n in ((ixs_p, 0, P), (ixs_s, 1, CAP_S)):
                    pool.tensor_copy(dst[:], rows[0:n, k, bass.ds(e, 1)]).then_inc(S["ix_s"], 1)
                pool.wait_ge(S["ix_s"], 2 * e + 2)
                pool.wait_ge(S["ob_act"], e + 1)
                pool.wait_ge(S["ob_dve"], e + 1)
                settled()
                pool.indirect_dma_start(y_p, bass.IndirectOffsetOnAxis(ap=ixs_p[:, 0:1], axis=0), ob_p[:], None,
                                        compute_op=ALU.add).then_inc(S["scattered"], 16)
                pool.indirect_dma_start(y_s, bass.IndirectOffsetOnAxis(ap=ixs_s[:, 0:1], axis=0), ob_s[:], None,
                                        compute_op=ALU.add).then_inc(S["scattered"], 16)
                pool.wait_ge(S["scattered"], 32 * e + 32)

            pool.wait_ge(S["rows_dve"], ROWS_STEPS)
            pool.wait_ge(S["h_out0"], 16 * NCH // 2)
            pool.wait_ge(S["h_out1"], 16 * NCH // 2)
            pool.wait_ge(S["y_out"], 32)
            gather(0)

            def frame(e):
                first, last = isinstance(e, int) and e == 0, isinstance(e, int) and e >= E - 1
                if not (first or (isinstance(e, int) and e == 1)):
                    scatter(e - 2)
                if not last:
                    gather(e + 1)
            run_frames(pool, frame)
            scatter(E - 1)

        @block.tensor
        def _(pe):
            pe.wait_ge(S["consts"], 5)
            def lin(g, j, between=None):
                pe.wait_ge(S["w_split"], g + 1)
                pe.wait_ge(S["evac"], 5 if isinstance(g, int) and g == 2 else 3 * (g - 1))
                for b, (t0, tn) in enumerate(BLOCKS):
                    for k in range(KD):
                        last = mm3(pe, lin_set(j, b), w_hi[:, j, k], w_lo[:, j, k],
                                   act_hi[:, k, t0:t0 + tn], act_lo[:, k, t0:t0 + tn], k == 0, k == KD - 1)
                    last.then_inc(S["tile_pe"], 1)
                    if between:
                        between(b)

            def lin_loop(g0):
                with pe.Fori(0, KD // 2) as i:
                    for j in range(2):
                        lin(g0 + 2 * i + j, j)

            def n1_turn(n):
                pe.wait_ge(S["n1_xn"], n + 1)
                if n > 0:
                    pe.wait_ge(S["n1_h"], n)
                for k in range(KD):
                    last = pe.transpose(bank(6, D)[:, k * P:(k + 1) * P], xn[:, n % 2, k * P:(k + 1) * P], ident[:])
                last.then_inc(S["n1_tr"], 1)

            def first_tiles(g, b):
                t0, tn = BLOCKS[b]
                pe.wait_ge(S["w_split"], g + 1)
                pe.wait_ge(S["n1_lo_even"], (t0 + tn) // (2 * P))
                pe.wait_ge(S["n1_lo_odd"], (t0 + tn) // (2 * P))
                for k in range(KD):
                    last = mm3(pe, lin_set(g, b), w_hi[:, g, k], w_lo[:, g, k], act_hi[:, k, t0:t0 + tn],
                               act_lo[:, k, t0:t0 + tn], k == 0, k == KD - 1)
                last.then_inc(S["tile_pe"], 1)

            for n in range(7):
                n1_turn(n)
            first_tiles(0, 0)
            n1_turn(7)
            n1_turn(8)
            first_tiles(1, 0)
            n1_turn(9)
            for b in (1, 2):
                first_tiles(0, b)
                first_tiles(1, b)
            for g in (2, 3):
                lin(g, g % 2)
            lin_loop(G_V)

            for n, (src, need, sem_) in enumerate(((rs_v, 4, "latent_dve"), (krf, 5, "latent_dve"), (acc_v, KD, "v_acc"))):
                pe.wait_ge(S[sem_], need)
                for b, (t0, tn) in enumerate(BLOCKS):
                    q = 3 * n + b
                    if q > 1:
                        pe.wait_ge(S["rms_act"], q - 1)
                    pe.matmul(bank(6 + q % 2, tn), ones[:], src[:, t0:t0 + tn], start=True,
                              stop=True).then_inc(S["sum_pe"], 1)
            lin_loop(G_U)

            pe.wait_ge(S["rms_act"], 9)
            with pe.Fori(0, KD) as i:
                def gating(j, b):
                    t0, tn = BLOCKS[b]
                    if j == 0:
                        pe.wait_ge(S["sp_vn"], at("sp_vn", i + 1))
                        if b == 0:
                            pe.wait_ge(S["sp_act"], at("sp_act", 3 * i - 1))
                        elif b == 1:
                            pe.wait_ge(S["sp_act"], at("sp_act", 3 * i))
                        else:
                            pe.wait_ge(S["sp_tok"], at("sp_tok", 4 * i + 1))
                        o = bank(6 + b % 2)
                        for c in range(tn // P):
                            last = pe.transpose(o[:, c * P:(c + 1) * P], vt[:, t0 + c * P:t0 + (c + 1) * P], ident[:])
                        if b == 2:
                            pe.wait_ge(S["sp_wsin"], 16 * i + 16)
                            last = pe.transpose(o[:, 2 * P:3 * P], ws[:], ident[:])
                        last.then_inc(S["sp_t"], 1)
                    else:
                        if b == 0:
                            pe.wait_ge(S["sp_tok"], at("sp_tok", 4 * i + 4))
                        else:
                            pe.wait_ge(S["sp_act"], at("sp_act", 3 * i + (b - 1)))
                        o = bank(7 - b % 2)
                        for c in range(tn // P):
                            last = pe.matmul(o[:, c * P:(c + 1) * P], vtok[:, t0 + c * P:t0 + (c + 1) * P],
                                             wsT[:], start=True, stop=True)
                        last.then_inc(S["sp_m"], 1)
                lin(G_GATE + 2 * i, 0, lambda b: gating(0, b))
                lin(G_GATE + 2 * i + 1, 1, lambda b: gating(1, b))

            def lin_split(g0, n0):
                for j in range(2):
                    pe.wait_ge(S["w_split"], g0 + j + 1)
                    pe.wait_ge(S["evac"], 3 * (g0 + j - 1))
                for k in range(KD):
                    pe.wait_ge(S["part_lo"], at("part_lo", n0 + k + 1))
                    for j in range(2):
                        for b, (t0, tn) in enumerate(BLOCKS):
                            last = mm3(pe, lin_set(j, b), w_hi[:, j, k], w_lo[:, j, k],
                                       act_hi[:, k, t0:t0 + tn], act_lo[:, k, t0:t0 + tn], k == 0, k == KD - 1)
                            if k == KD - 1:
                                last.then_inc(S["tile_pe"], 1)
                with pe.Fori(1, KD // 2) as i:
                    for j in range(2):
                        lin(g0 + 2 * i + j, j)

            lin_split(G_A, 0)

            pe.wait_ge(S["evac"], 3 * G_B)
            pe.wait_ge(S["latent_dve"], 22)

            def project_k(h):
                pe.wait_ge(S["aw_lo"], at("aw_lo", 2 * h + 1))
                for b, (t0, tn) in enumerate(BLOCKS):
                    mm3(pe, lin_set(0, b), ak_hi[:], ak_lo[:], ckv_hi[:, t0:t0 + tn],
                        ckv_lo[:, t0:t0 + tn], True, True).then_inc(S["ap_pe"], 1)

            def column_sums(out, src):
                for c in range(NCH):
                    last = pe.matmul(out[:, c:c + 1], src[:, c * P:(c + 1) * P], ones[0:src.shape[0], 0:1],
                                     start=True, stop=True)
                return last

            def head(h, more):
                def dve(name):
                    pe.wait_ge(S["ap_dve"], at("ap_dve", DVE_STEPS * h + DVE_STEP[name]))

                def acts(name):
                    pe.wait_ge(S["ap_act"], at("ap_act", ACT_STEPS * h + ACT_STEP[name]))

                def project_q(half, j):
                    for b, (t0, tn) in enumerate(BLOCKS):
                        for k in range(2):
                            w = slice(half * P, half * P + P)
                            last = mm3(pe, lin_set(j, b), aq_hi[:, k, w], aq_lo[:, k, w],
                                       cq_hi[:, k, t0:t0 + tn], cq_lo[:, k, t0:t0 + tn], k == 0, k == 1)
                        last.then_inc(S["ap_pe"], 1)

                pe.wait_ge(S["aw_lo"], at("aw_lo", 2 * h + 2))
                pe.wait_ge(S["pt_lo_dve"], at("pt_lo_dve", NCH * h))
                project_q(0, 1)
                acts("sq_k")
                pe.wait_ge(S["values_act"], at("values_act", 3 * h))
                pe.wait_ge(S["latent_dve"], 23)
                column_sums(bank(6), sq_k).then_inc(S["ap_pe"], 1)
                acts("kf")
                for b, (t0, tn) in enumerate(BLOCKS):
                    for c in range(t0, t0 + tn, P):
                        last = pe.matmul(lin_all(0)[:, c:c + P], ckv[:, c:c + P], akv_raw[:, P:2 * P],
                                         start=True, stop=True)
                    last.then_inc(S["ap_pe"], 1)
                dve("diag")
                for b, (t0, tn) in enumerate(BLOCKS):
                    pe.matmul(lin_set(1, b), ones[:], diag[:, t0:t0 + tn], start=True,
                              stop=True).then_inc(S["ap_pe"], 1)
                dve("v_lo")
                project_q(1, 0)
                column_sums(bank(7), sq_q)
                acts("sq_qr2")
                column_sums(bank(7)[:, NCH:2 * NCH], sq_qr[0:ROPE]).then_inc(S["ap_pe"], 1)
                acts("k_hi")
                dve("rt_2")

                def keys(c):
                    return (0, TP) if c < NCH_P else (TP, TS)

                def scores(c):
                    k0, kn = keys(c)
                    pe.wait_ge(S["exp_act"], at("exp_act", NCH * h + (c - 1)))
                    q = slice(c * P, (c + 1) * P)
                    halves = []
                    for o in range(0, kn, BANK):
                        n = min(BANK, kn - o)
                        halves.append((bank(s_bank(c) + o // BANK, n), slice(k0 + o, k0 + o + n)))
                    for out, k in halves:
                        pe.matmul(out, q_hi[:, q], k_hi[:, k], start=True, stop=False)
                        pe.matmul(out, q_hi[:, q], k_lo[:, k], start=False, stop=False)
                        pe.matmul(out, q_lo[:, q], k_hi[:, k], start=False, stop=False)
                    if c == 0:
                        acts("qr2_up")
                        dve("qr2_down")
                        pe.wait_ge(S["krl_pool"], h + 1)
                    for out, k in halves:
                        pe.matmul(out, qr2[:, q], kr2[:, k], start=False, stop=False)
                        last = pe.matmul(out, qr2[:, q], krl[:, k], start=False, stop=True)
                    last.then_inc(S["scores_pe"], 1)

                def turn(c):
                    kn = keys(c)[1]
                    pr = "prob_dve" if c % 2 else "prob_act"
                    pe.wait_ge(S[pr], at(pr, NCH // 2 * h + (c // 2 + 1)))
                    pe.wait_ge(S["pt_lo_dve"], at("pt_lo_dve", NCH * h + min(c, NCH - 2)))
                    for k in range(kn // P):
                        last = pe.transpose(bank(t_bank(c), kn)[:, k * P:(k + 1) * P],
                                            prob[:, c % 2, k * P:(k + 1) * P], ident[:])
                    last.then_inc(S["probT_pe"], 1)

                def values(b):
                    t0, tn = BLOCKS[b]
                    k0, kn = keys(t0 // P)
                    pe.wait_ge(S["pt_lo_dve"], at("pt_lo_dve", NCH * h + (t0 + tn) // P))
                    pe.wait_ge(S["values_act"], at("values_act", 3 * h + max(b - 1, 0)))
                    for k in range(kn // P):
                        v = slice(k0 + k * P, k0 + (k + 1) * P)
                        last = mm3(pe, bank(6 + b % 2, tn), v_hi[:, v], v_lo[:, v], pt_hi[:, k, 0:tn],
                                   pt_lo[:, k, 0:tn], k == 0, k == kn // P - 1)
                    last.then_inc(S["values_pe"], 1)

                for c in range(NCH):
                    scores(c)
                    if c == 6:
                        values(0)
                    if c > 1:
                        turn(c - 2)
                if more:
                    pe.wait_ge(S["exp_act"], at("exp_act", NCH * h + (NCH - 1)))
                    project_k(h + 1)
                values(1)
                turn(NCH - 2)
                turn(NCH - 1)
                values(2)

            project_k(0)
            column_sums(bank(7), sq_kr[0:ROPE]).then_inc(S["kr_pe"], 1)
            with pe.Fori(0, H - 1) as h:
                head(h, True)
            head(H - 1, False)

            lin_split(G_B, KD)

            def out_product(q, c, k, acc):
                wh, wl = (w_hi, w_lo) if q % 2 == 0 else (w2_hi, w2_lo)
                t = slice(c * P, (c + 1) * P)
                last = mm3(pe, bank(acc)[:, 0:QN], act_hi[:, k, t], act_lo[:, k, t], wh[:, :, k], wl[:, :, k],
                           k == 0, k == KD - 1)
                if k == KD - 1:
                    last.then_inc(S["out_pe"], 1)

            def out_chunk(q, c):
                pe.wait_ge(S["x2_dve"], q * NCH + c - 1)
                for k in range(KD):
                    out_product(q, c, k, 4 + c % 2)

            pe.wait_ge(S["w_split"], G_OUT + 2)
            pe.wait_ge(S["evac"], 3 * G_OUT)
            for k in range(KD):
                pe.wait_ge(S["part_lo"], at("part_lo", 2 * KD + k + 1))
                for c in range(8):
                    out_product(0, c, k, c)
            out_chunk(0, 8)
            out_chunk(0, 9)
            for q in range(1, QS - 1):
                pe.wait_ge(S["w_split"], G_OUT + 2 * q + 2)
                for c in range(NCH):
                    out_chunk(q, c)
            pe.wait_ge(S["w_split"], G_OUT + 2 * QS)
            pe.wait_ge(S["r_in"], 32)

            def channels(n):
                pe.wait_ge(S["h_dve"], n + 1)
                if n > 1:
                    pe.wait_ge(S["hT_act"], n - 1)
                for k in range(KD):
                    last = pe.transpose(bank(2 * (n % 2), D)[:, k * P:(k + 1) * P], h2[:, n % 2, k], ident[:])
                last.then_inc(S["hT_pe"], 1)

            def logits(n):
                pe.wait_ge(S["hT_act"], n + 1)
                for k in range(KD):
                    last = pe.matmul(bank(6)[:, n * E:(n + 1) * E], h2T[:, n % 2, k * P:(k + 1) * P], wr[:, k],
                                     start=(k == 0), stop=(k == KD - 1))
                last.then_inc(S["logits_pe"], 1)

            for c in range(NCH + 2):
                if c < NCH:
                    out_chunk(QS - 1, c)
                if 0 < c <= NCH:
                    channels(c - 1)
                if c > 1:
                    logits(c - 2)
            pe.wait_ge(S["r_dve"], 8)
            for c in range(HALF // P):
                last = pe.transpose(PS[0:LISTS, c * P:(c + 1) * P], lists[:, c, :], ident[:])
            last.then_inc(S["aff_pe"], 1)
            pe.wait_ge(S["topk_dve"], TOPK_STEPS)
            for n, src in enumerate((topv, topf)):
                pe.transpose(bank(3)[:, n * LISTS:(n + 1) * LISTS], src[:], ident[0:LISTS, 0:LISTS])\
                    .then_inc(S["chosen_pe"], 1)
            pe.wait_ge(S["rows_dve"], 1)
            for n in range(2):
                pe.matmul(bank(2)[:, n * E:(n + 1) * E], flip[:], chosen[:, n, L_B:L_B + E], start=True,
                          stop=True).then_inc(S["chosen_pe"], 1)

            def turn_x(e):
                pe.wait_ge(S["gathered"], 32 * e + 32)
                for k in range(KD):
                    last = pe.transpose(bank(0, D)[:, k * P:(k + 1) * P], xs_p[:, k * P:(k + 1) * P], ident[:])
                last.then_inc(S["tx_pe"], 1)

            def turn_xs(e):
                pe.sem_inc(S["passed_pe"], 1)
                for k in range(KD):
                    last = pe.transpose(bank(7)[:, k * CAP_S:(k + 1) * CAP_S], xs_s[:, k * P:(k + 1) * P],
                                        ident[0:CAP_S, 0:CAP_S])
                last.then_inc(S["txs_pe"], 1)

            def product(b0, hi, lo, bs, few, slot, pt, kk, guard_s):
                for kin in range(2):
                    k = 2 * kk + kin
                    for rhs, lhs, st, sp_ in ((ehi, hi, k == 0, False), (elo, hi, False, False), (ehi, lo, False, k == KD - 1)):
                        for half in range(2):
                            pe.matmul(bank(b0 + half), lhs[:, k], rhs[:, pt, kin, half * BANK:(half + 1) * BANK],
                                      start=st, stop=sp_)
                guard_s()
                for kin in range(2):
                    k = 2 * kk + kin
                    for g in range(GRP):
                        last = pe.matmul(bank(bs)[CAP_S * g:CAP_S * (g + 1), 0:GN], few(k),
                                         raw[:, slot, kin, g * GN:(g + 1) * GN], start=(k == 0), stop=(k == KD - 1))
                last.then_inc(S["e_pe"], 1)

            pe.wait_ge(S["rows_dve"], ROWS_STEPS)
            turn_x(0)
            turn_xs(0)

            def frame(e):
                is0, is1, is_last = (isinstance(e, int) and e == v for v in (0, 1, E))
                for n, (kind, ee, kk, q, slot) in enumerate(pieces(e)):
                    l = n + (8 if is_last else 0)
                    if is_last and n == 0:
                        turn_h(E - 1)
                        pe.wait_ge(S["hl_dve"], E)
                        pe.wait_ge(S["hs_dve"], E)
                    if l == 0:
                        pe.wait_ge(S["xl_dve"], e + 1)
                        pe.wait_ge(S["xs_dve"], e + 1)
                    if l == 4 and not is0:
                        pe.wait_ge(S["hl_dve"], e)
                        pe.wait_ge(S["hs_dve"], e)
                    if l == 8 and not is1:
                        pe.wait_ge(S["ob_act"], e - 1)
                        if is_last:
                            pe.wait_ge(S["ob_dve"], e - 1)
                    pe.wait_ge(S["e_lo"], q + 1)

                    def guard_s():
                        if l == 0 and not (is0 or is1):
                            pe.wait_ge(S["ob_dve"], e - 1)
                        if l == 8 and not is_last:
                            pe.wait_ge(S["silu_s"], e + 1)
                    if kind == "d":
                        product(4, hT_hi, hT_lo, 6, lambda k: hT_s[:, k % 2 * P + k // 2 * CAP_S:k % 2 * P + k // 2 * CAP_S + CAP_S],
                                slot, part(n if is_last else l, False) if not is_last else q % 3, kk, guard_s)
                    else:
                        product(0 if kind == "g" else 2, xT_hi, xT_lo, 6 if kind == "g" else 7,
                                lambda k: xT_s[:, k], slot, part(l, is0), kk, guard_s)
                    if l == 0 and not is0:
                        turn_h(e - 1)
                    more = not (isinstance(e, int) and e >= E - 1)
                    if more and l == (7 if is0 else 8):
                        pe.wait_ge(S["silu_p"], e + 1)
                        turn_x(e + 1)
                    if more and l == (7 if is0 else 9):
                        pe.wait_ge(S["mul_s"], e + 1)
                        turn_xs(e + 1)

            def turn_h(e):
                pe.wait_ge(S["mul_p"], e + 1)
                for k in range(KD):
                    last = pe.transpose(bank(2, D)[:, k * P:(k + 1) * P], hid[:, k * P:(k + 1) * P], ident[:])
                last.then_inc(S["th_pe"], 1)
                pe.wait_ge(S["mul_s"], e + 1)
                if not (isinstance(e, int) and e >= E - 1):
                    pe.wait_ge(S["xs_dve"], e + 2)
                for k in range(2):
                    last = pe.transpose(bank(7)[:, k * P:(k + 1) * P], hid_s[:, k * P:(k + 1) * P], ident[:])
                last.then_inc(S["ths_pe"], 1)

            run_frames(pe, frame)

        @block.scalar
        def _(act):
            for n in range(NCH + 2):
                if n < NCH:
                    if n % 2 == 0:
                        act.wait_ge(x_in_s[n // 2], 16)
                    if n > 1:
                        act.wait_ge(S["n1_ssq"], n - 1)
                    act.activation(stg[:, n % 2, 0:D], x_in[:, n], ACT.Square, accum_out=ssq1[:, n:n + 1]).then_inc(S["n1_ssq"], 1)
                    act.wait_ge(S["n1_ssq"], n + 1)
                    if n == 0:
                        act.wait_ge(S["consts"], 3)
                    act.activation(std1[:, n:n + 1], ssq1[:, n:n + 1], ACT.Sqrt, bias=epsc,
                                   scale=1.0 / D).then_inc(S["n1_std"], 1)
                if n > 1:
                    act.wait_ge(S["n1_h"], n - 1)
                    act.activation(act_hi[:, :, (n - 2) * P:(n - 1) * P], htmp[:, n % 2], ACT.Copy).then_inc(S["n1_hi"], 1)

            dst = [ct[:, 0, :], ct[:, 1, :], ckv[:], ct[:, 2, :]]
            order = [(g, b) for b in range(3) for g in range(2)] + [(g, b) for g in (2, 3) for b in range(3)]
            for n, (g, b) in enumerate(order):
                t0, tn = BLOCKS[b]
                act.wait_ge(S["tile_pe"], n + 1)
                if g == 2 and b == 0:
                    act.wait_ge(S["n1_lo_even"], NCH // 2)
                    act.wait_ge(S["n1_lo_odd"], NCH // 2)
                act.activation(dst[g][:, t0:t0 + tn], lin_set(g % 2, b), ACT.Copy).then_inc(S["evac"], 1)

            def evac(g, j, func, out, uses, guard=None):
                for b, (t0, tn) in enumerate(BLOCKS):
                    act.wait_ge(S["tile_pe"], 3 * g + (b + 1))
                    if b == 0:
                        if uses is not None:
                            act.wait_ge(stored[j], 16 * uses)
                        if guard is not None:
                            guard()
                    act.activation(stg[:, j, t0:t0 + tn], lin_set(j, b), func).then_inc(S["evac"], 1)
                act.wait_ge(S["evac"], 3 * g + 3)
                act.dma_start(out, stg[:, j, :]).then_inc(stored[j], 16)

            for j in range(2):
                evac(G_V + j, j, ACT.Gelu, v_d[j], None)
            with act.Fori(1, KD // 2) as i:
                for j in range(2):
                    evac(2 * i + (G_V + j), j, ACT.Gelu, v_d[2 * i + j], i,
                         lambda: act.wait_ge(S["v_acc"], 2 * i + (j - 1)))

            rs = [rs_v, krf, acc_v]
            for n in range(3):
                for b, (t0, tn) in enumerate(BLOCKS):
                    q = 3 * n + b
                    act.wait_ge(S["sum_pe"], q + 1)
                    act.activation(rs[n][:, t0:t0 + tn], bank(6 + q % 2, tn), ACT.Sqrt, bias=epsc,
                                   scale=1.0 / (QR, KVR, D)[n]).then_inc(S["rms_act"], 1)
            for m in range(2):
                act.wait_ge(S["latent_dve"], 9 + m)
                act.activation(cq_hi[:, m], ct[:, m, :], ACT.Copy, scale=gqn[:, m:m + 1]).then_inc(S["latent_act"], 1)
            act.wait_ge(S["latent_dve"], 13)
            act.activation(ckv_hi[:], ckv[:], ACT.Copy).then_inc(S["latent_act"], 1)

            with act.Fori(0, KD // 2) as i:
                for j in range(2):
                    evac(2 * i + (G_U + j), j, ACT.Gelu, u_d[2 * i + j], i + 4)

            with act.Fori(0, KD) as i:
                def gated(j):
                    g = 2 * i + (G_GATE + j)
                    for b, (t0, tn) in enumerate(BLOCKS):
                        act.wait_ge(S["tile_pe"], 3 * g + (b + 1))
                        if b == 0:
                            act.wait_ge(stored[j], 16 * i + 16 * KD)
                        act.activation(stg[:, j, t0:t0 + tn], lin_set(j, b), ACT.Sigmoid).then_inc(S["evac"], 1)
                        if j == 0:
                            act.wait_ge(S["sp_t"], at("sp_t", 3 * i + (b + 1)))
                            if b == 0:
                                act.wait_ge(S["sp_m"], at("sp_m", 3 * i))
                            act.activation(vtok[:, t0:t0 + tn], bank(6 + b % 2, tn), ACT.Copy).then_inc(S["sp_tok"], 1)
                            if b == 2:
                                act.activation(wsT[:], bank(6)[:, 2 * P:3 * P], ACT.Copy).then_inc(S["sp_tok"], 1)
                    act.wait_ge(S["evac"], 3 * g + 3)
                    act.dma_start(g_d[2 * i + j], stg[:, j, :]).then_inc(stored[j], 16)
                gated(0)
                gated(1)
                act.wait_ge(S["sp_y"], at("sp_y", 3 * i + 3))
                act.dma_start(y_d[i], yt[:]).then_inc(S["sp_stored"], 16)

            act.wait_ge(S["tile_pe"], 3 * G_A)
            with act.Fori(0, KD // 2) as i:
                for j in range(2):
                    act.wait_ge(ld_in[j], 16 * i + 16)
                    act.activation(act_hi[:, 2 * i + j, :], stg[:, j, :], ACT.Copy).then_inc(S["part_hi"], 1)
            with act.Fori(0, KD // 2) as i:
                for j in range(2):
                    act.wait_ge(S["evac"], 6 * i + (3 * G_A + 3 * j + 3))
                    act.dma_start(za_d[2 * i + j], stg[:, j, :]).then_inc(stored[j], 16)

            for j in range(2):
                act.wait_ge(stored[j], 16 * 20)
            with act.Fori(0, H) as h:
                def own(name):
                    act.wait_ge(S["ap_act"], at("ap_act", ACT_STEPS * h + ACT_STEP[name]))

                def dve(name):
                    act.wait_ge(S["ap_dve"], at("ap_dve", DVE_STEPS * h + DVE_STEP[name]))

                def products(name):
                    act.wait_ge(S["ap_pe"], at("ap_pe", PE_STEPS * h + PE_STEP[name]))

                def done(i_):
                    i_.then_inc(S["ap_act"], 1)

                def sq_rotary(b):
                    t0, tn = BLOCKS[b]
                    products(f"qr{b}")
                    done(act.activation(sq_qr[0:ROPE, t0:t0 + tn], lin_set(0, b)[0:ROPE], ACT.Square))

                done(act.activation(spare, epsc, ACT.Sqrt))
                products("k")
                done(act.activation(sq_k, lin_all(0), ACT.Square))
                done(act.activation(kf[:], lin_all(0), ACT.Copy, scale=gk))
                products("q")
                done(act.activation(sq_q, lin_all(1), ACT.Square))
                done(act.activation(q_hi[:], lin_all(1), ACT.Copy, scale=gq))
                dve("rk_v")
                done(act.activation(rk_s, rk_v, ACT.Sqrt, bias=epsc, scale=1.0 / HEAD))
                products("v")
                done(act.activation(v_hi[:], lin_all(0), ACT.Copy))
                sq_rotary(0)
                dve("kf")
                done(act.activation(k_hi[:], kf[:], ACT.Copy))
                sq_rotary(1)
                dve("rt3")
                done(act.activation(kr2[0:ROPE], rt3, ACT.Copy))
                sq_rotary(2)
                done(act.activation(kr2[ROPE:P], rt3, ACT.Copy))
                dve("rt1")
                done(act.activation(qr2[0:ROPE], rt1, ACT.Copy))
                dve("rq_v")
                done(act.activation(rq_s, rq_v, ACT.Sqrt, bias=epsc, scale=1.0 / HEAD))
                own("rq_s")
                done(act.activation(spare, epsc, ACT.Exp))

                def keys(c):
                    return TP if c < NCH_P else TS

                def expo(c):
                    n = keys(c)
                    act.wait_ge(S["bias_dve"], at("bias_dve", NCH * h + (c + 1)))
                    act.wait_ge(S["probT_pe"], at("probT_pe", NCH * h + (c - 1)))
                    act.activation(prob[:, c % 2, 0:n], bank(s_bank(c), n), ACT.Exp, bias=nmx[:, c:c + 1],
                                   scale=rq[:, c:c + 1], accum_out=psumr[:, c:c + 1]).then_inc(S["exp_act"], 1)

                def norm(c):
                    n = keys(c)
                    act.wait_ge(S["recip_dve"], at("recip_dve", NCH * h + (c + 1)))
                    act.activation(prob[:, c % 2, 0:n], prob[:, c % 2, 0:n], ACT.Copy,
                                   scale=prec[:, c:c + 1]).then_inc(S["prob_act"], 1)

                def high(c):
                    n = keys(c) // P
                    o = (c % NCH_P) % 4 * P
                    act.wait_ge(S["probT_pe"], at("probT_pe", NCH * h + (c + 1)))
                    if c in (0, 4, 8):
                        act.wait_ge(S["values_pe"], at("values_pe", 3 * h + c // 4))
                    act.activation(pt_hi[:, 0:n, o:o + P], bank(t_bank(c), n * P), ACT.Copy).then_inc(S["pt_hi_act"], 1)

                def out(b):
                    t0, tn = BLOCKS[b]
                    slot = b % 2
                    st = S[f"o_st{slot}"]
                    act.wait_ge(S["values_pe"], at("values_pe", 3 * h + (b + 1)))
                    act.wait_ge(st, 32 + (16 * h if slot else 32 * h + (16 if b else 0)))
                    act.activation(ostg[:, slot, 0:tn], bank(6 + slot, tn), ACT.Copy).then_inc(S["values_act"], 1)
                    act.wait_ge(S["values_act"], at("values_act", 3 * h + (b + 1)))
                    act.dma_start(o_d[h][:, t0:t0 + tn], ostg[:, slot, 0:tn]).then_inc(st, 16)

                for c in range(NCH + 2):
                    if c > 1:
                        high(c - 2)
                    if c < NCH:
                        expo(c)
                        if c % 2 == 0:
                            norm(c)
                    if c in (7, 11):
                        out(c // 4 - 1)
                out(2)

            act.wait_ge(S["values_pe"], at("values_pe", 3 * H))
            act.wait_ge(S["o_back"], 16)
            with act.Fori(0, H - 1) as h:
                act.activation(act_hi[:, h, :], o_all[:, h, :], ACT.Copy).then_inc(S["part_hi"], 1)
            act.wait_ge(S["o_back_last"], 16)
            act.activation(act_hi[:, H - 1, :], o_all[:, H - 1, :], ACT.Copy).then_inc(S["part_hi"], 1)
            act.wait_ge(S["tile_pe"], 3 * G_OUT)
            with act.Fori(0, KD) as k:
                act.wait_ge(S["z_sum"], at("z_sum", k + 1))
                act.activation(act_hi[:, k, :], z_all[:, k, :], ACT.Copy).then_inc(S["part_hi"], 1)
            for n in range(NCH + 1):
                if n < NCH:
                    act.wait_ge(S["x2_dve"], (QS - 1) * NCH + n + 1)
                    if n > 1:
                        act.wait_ge(S["r_ssq"], n - 1)
                    act.activation(stg[:, n % 2, 0:D], x2[:, n, :], ACT.Square, accum_out=ssq2[:, n:n + 1]).then_inc(S["r_ssq"], 1)
                    act.wait_ge(S["r_ssq"], n + 1)
                    act.activation(std2[:, n:n + 1], ssq2[:, n:n + 1], ACT.Sqrt, bias=epsc,
                                   scale=1.0 / D).then_inc(S["r_std"], 1)
                if n > 0:
                    act.wait_ge(S["hT_pe"], n)
                    if n > 2:
                        act.wait_ge(S["logits_pe"], n - 2)
                    m = (n - 1) % 2
                    act.activation(h2T[:, m], bank(2 * m, D), ACT.Copy).then_inc(S["hT_act"], 1)
            act.wait_ge(S["r_dve"], 2)
            act.activation(aff[:], lg[:], ACT.Exp).then_inc(S["r_exp"], 1)
            act.wait_ge(S["aff_pe"], 1)
            act.activation(work[:], PS[0:LISTS, 0:HALF], ACT.Copy).then_inc(S["affT_act"], 1)

            def frame(e):
                is0, is1, is_last = (isinstance(e, int) and e == v for v in (0, 1, E))
                more = not (isinstance(e, int) and e >= E - 1)
                for n, (kind, ee, kk, q, slot) in enumerate(pieces(e)):
                    l = n + (8 if is_last else 0)
                    if is_last and n == 0:
                        out(e - 2)
                        hidden(e - 1)
                    act.wait_ge(S[f"e_in{slot}"], loads_of(e, n))
                    if not isinstance(q, int) or q >= 3:
                        act.wait_ge(S["e_pe"], q - 2)
                    pt = part(l, is0) if not is_last else q % 3
                    act.activation(ehi[:, pt], raw[:, slot], ACT.Copy).then_inc(S["e_hi"], 1)
                    if is0 and n == 2:
                        act.wait_ge(S["y_out"], 32)
                        rows_hi(0)
                    if l == 1 and not (is0 or is1):
                        out(e - 2)
                    if l == 2 and not is0:
                        hidden(e - 1)
                    if l == 5:
                        act.wait_ge(S["e_pe"], q - 1)
                        if not is0:
                            act.wait_ge(S["ths_pe"], e)
                        act.activation(hid[:], bank(0, D), ACT.Silu).then_inc(S["silu_p"], 1)
                        act.activation(hid_s[:], bank(6, GN), ACT.Silu).then_inc(S["silu_s"], 1)
                    if more and l == (7 if is0 else 10):
                        rows_hi(e + 1)
                if is_last:
                    out(e - 1)

            def rows_hi(e):
                act.wait_ge(S["tx_pe"], e + 1)
                act.activation(xT_hi[:], bank(0, D), ACT.Copy).then_inc(S["xh_act"], 1)

            def hidden(e):
                act.wait_ge(S["th_pe"], e + 1)
                act.activation(hT_hi[:], bank(2, D), ACT.Copy).then_inc(S["hh_act"], 1)

            def out(e):
                act.wait_ge(S["e_pe"], 12 * E if isinstance(e, int) and e == E - 1 else 12 * e + 20)
                if not (isinstance(e, int) and e == 0):
                    act.wait_ge(S["scattered"], 32 * e)
                act.activation(ob_p[:], bank(4, D), ACT.Copy, scale=gates[:, 0, bass.ds(e, 1)]).then_inc(S["ob_act"], 1)

            run_frames(act, frame)

        @block.vector
        def _(dve):
            for n in range(NCH + 2):
                if n < NCH:
                    dve.wait_ge(S["n1_std"], n + 1)
                    dve.reciprocal(rstd1[:, n:n + 1], std1[:, n:n + 1]).then_inc(S["n1_rec"], 1)
                    dve.wait_ge(S["n1_rec"], n + 1)
                    if n > 1:
                        dve.wait_ge(S["n1_tr"], n - 1)
                    dve.tensor_scalar(xn[:, n % 2], x_in[:, n, :], rstd1[:, n:n + 1], None, ALU.mult).then_inc(S["n1_xn"], 1)
                if n >= 2 and n % 2:
                    m = n - 2
                    dve.wait_ge(S["n1_hi"], m + 1)
                    dve.tensor_tensor(act_lo[:, :, m * P:(m + 1) * P], htmp[:, 1], f32(act_hi[:, :, m * P:(m + 1) * P]),
                                      ALU.subtract).then_inc(S["n1_lo_odd"], 1)
                if 1 <= n <= NCH:
                    m = n - 1
                    dve.wait_ge(S["n1_tr"], m + 1)
                    if m == 0:
                        dve.wait_ge(S["g1_in"], 16)
                    if m > 1:
                        dve.wait_ge(S["n1_lo_odd" if m % 2 else "n1_lo_even"], m // 2)
                    dve.tensor_tensor(htmp[:, m % 2], bank(6, D).rearrange("p (k t) -> p k t", k=KD),
                                      g1c.unsqueeze(2).to_broadcast([P, KD, P]), ALU.mult).then_inc(S["n1_h"], 1)
            dve.wait_ge(S["params"], 16 * 11)

            def step(i_, n):
                i_.then_inc(S["latent_dve"], 1)
                dve.wait_ge(S["latent_dve"], n)
            step(dve.tensor_scalar(tab_k, tab_k, gkr, None, ALU.mult), 1)
            dve.wait_ge(S["evac"], 3 * 2)
            step(dve.tensor_tensor(rs_v[:], ct[:, 0, :], ct[:, 0, :], ALU.mult), 2)
            step(dve.tensor_tensor(acc_v[:], ct[:, 1, :], ct[:, 1, :], ALU.mult), 3)
            step(dve.tensor_tensor(rs_v[:], rs_v[:], acc_v[:], ALU.add), 4)
            dve.wait_ge(S["evac"], 3 * 3)
            step(dve.tensor_tensor(krf[:], ckv[:], ckv[:], ALU.mult), 5)
            dve.wait_ge(S["evac"], 3 * 4)
            step(dve.tensor_tensor(sq_kr[0:ROPE], ct[0:ROPE, 2, :], ct[0:ROPE, 2, :], ALU.mult), 6)
            step(dve.memset(acc_v[:], 0.0), 7)
            with dve.Fori(0, KD // 2) as i:
                for j in range(2):
                    dve.wait_ge(S["evac"], 6 * i + (3 * (G_V + j) + 3))
                    dve.tensor_tensor(sq_v, stg[:, j, :], stg[:, j, :], ALU.mult).then_inc(S["v_sq"], 1)
                    dve.wait_ge(S["v_sq"], 2 * i + (j + 1))
                    dve.tensor_tensor(acc_v[:], acc_v[:], sq_v, ALU.add).then_inc(S["v_acc"], 1)
                    dve.wait_ge(S["v_acc"], 2 * i + (j + 1))
            dve.wait_ge(S["rms_act"], 3)
            step(dve.reciprocal(rs_v[:], rs_v[:]), 8)
            for m in range(2):
                step(dve.tensor_tensor(ct[:, m, :], ct[:, m, :], rs_v[:], ALU.mult), 9 + m)
            dve.wait_ge(S["rms_act"], 6)
            step(dve.reciprocal(krf[:], krf[:]), 11)
            step(dve.tensor_tensor(ckv[:], ckv[:], krf[:], ALU.mult), 12)
            step(dve.tensor_scalar(ckv[:], ckv[:], gkvn, None, ALU.mult), 13)
            step(dve.tensor_tensor(krf[0:ROPE], ct[0:ROPE, 2, :], tab_k[0:ROPE], ALU.mult), 14)
            step(dve.tensor_tensor(ct[0:ROPE, 2, :], ct[ROPE:P, 2, :], tab_k[ROPE:P], ALU.mult), 15)
            step(dve.tensor_tensor(krf[0:ROPE], krf[0:ROPE], ct[0:ROPE, 2, :], ALU.add), 16)
            for m in range(2):
                dve.wait_ge(S["latent_act"], m + 1)
                step(dve.scalar_tensor_tensor(out=cq_lo[:, m], in0=ct[:, m, :], scalar=gqn[:, m:m + 1],
                                              in1=f32(cq_hi[:, m]), op0=ALU.mult, op1=ALU.subtract), 17 + m)
            dve.wait_ge(S["latent_act"], 3)
            step(dve.tensor_tensor(ckv_lo[:], ckv[:], f32(ckv_hi[:]), ALU.subtract), 19)
            dve.wait_ge(S["tab_in"], 16)
            dve.wait_ge(S["rms_act"], 9)
            step(dve.tensor_scalar(tab_q[:], tab_q[:], gqr, None, ALU.mult), 20)
            step(dve.reciprocal(rs_v[:], acc_v[:]), 21)

            with dve.Fori(0, KD) as i:
                dve.wait_ge(S["sp_vin"], 16 * i + 16)
                dve.tensor_tensor(vt[:], vt[:], rs_v[:], ALU.mult).then_inc(S["sp_vn"], 1)
                dve.wait_ge(S["sp_bin"], 32 * i + 32)
                dve.wait_ge(S["sp_uin"], 16 * i + 16)
                dve.wait_ge(S["sp_stored"], at("sp_stored", 16 * i))
                for b, (t0, tn) in enumerate(BLOCKS):
                    dve.wait_ge(S["sp_m"], at("sp_m", 3 * i + (b + 1)))
                    dve.scalar_tensor_tensor(
                        out=yt[:, t0:t0 + tn].rearrange("p (c q) -> p c q", q=P),
                        in0=bank(7 - b % 2, tn).rearrange("p (c q) -> p c q", q=P), scalar=vg,
                        in1=bb[:].unsqueeze(1).to_broadcast([P, tn // P, P]), op0=ALU.mult,
                        op1=ALU.add).then_inc(S["sp_act"], 1)
                    dve.wait_ge(S["sp_act"], at("sp_act", 3 * i + (b + 1)))
                    dve.tensor_tensor(yt[:, t0:t0 + tn], yt[:, t0:t0 + tn], ut[:, t0:t0 + tn],
                                      ALU.mult).then_inc(S["sp_y"], 1)

            with dve.Fori(0, KD // 2) as i:
                for j in range(2):
                    dve.wait_ge(S["part_hi"], 2 * i + (j + 1))
                    dve.tensor_tensor(act_lo[:, 2 * i + j, :], stg[:, j, :], f32(act_hi[:, 2 * i + j, :]),
                                      ALU.subtract).then_inc(S["part_lo"], 1)
            dve.wait_ge(S["part_lo"], at("part_lo", KD))

            def split_lo(n0, src):
                with dve.Fori(0, KD) as k:
                    dve.wait_ge(S["part_hi"], k + (n0 + 1))
                    dve.tensor_tensor(act_lo[:, k, :], src[:, k, :], f32(act_hi[:, k, :]),
                                      ALU.subtract).then_inc(S["part_lo"], 1)

            def gate_a(i, j, g, uses):
                dve.wait_ge(gt_in[j], 16 * i + 16)
                if uses is not None:
                    dve.wait_ge(stored[j], uses)
                for b, (t0, tn) in enumerate(BLOCKS):
                    dve.wait_ge(S["tile_pe"], 3 * g + (b + 1))
                    dve.tensor_tensor(stg[:, j, t0:t0 + tn], lin_set(j, b), gt[:, j, t0:t0 + tn],
                                      ALU.mult).then_inc(S["evac"], 1)
            with dve.Fori(0, KD // 2) as i:
                for j in range(2):
                    gate_a(i, j, 2 * i + (G_A + j), 16 * i + 16 * 2 * KD)

            dve.wait_ge(S["tile_pe"], 3 * G_B)
            dve.memset(f32(krl[ROPE:P]), 0.0).then_inc(S["latent_dve"], 1)
            dve.wait_ge(S["kr_pe"], 1)
            dve.tensor_copy(kr_sum, bank(7, NCH)).then_inc(S["latent_dve"], 1)
            dve.wait_ge(S["latent_dve"], 23)
            with dve.Fori(0, H) as h:
                def own(name):
                    dve.wait_ge(S["ap_dve"], at("ap_dve", DVE_STEPS * h + DVE_STEP[name]))

                def acts(name):
                    dve.wait_ge(S["ap_act"], at("ap_act", ACT_STEPS * h + ACT_STEP[name]))

                def products(name):
                    dve.wait_ge(S["ap_pe"], at("ap_pe", PE_STEPS * h + PE_STEP[name]))

                def done(i_):
                    i_.then_inc(S["ap_dve"], 1)

                def turned(b):
                    t0, tn = BLOCKS[b]
                    t = slice(t0, t0 + tn)
                    acts(f"sq_qr{b}")
                    done(dve.tensor_tensor(rt1[:, t], lin_set(0, b)[0:ROPE], tab_q[0:ROPE, t], ALU.mult))
                    done(dve.tensor_tensor(rt2[:, t], lin_set(0, b)[ROPE:P], tab_q[ROPE:P, t], ALU.mult))

                products("sum_k")
                done(dve.tensor_tensor(rk_v, kr_sum, bank(6, NCH), ALU.add))
                acts("q_hi")
                done(dve.scalar_tensor_tensor(out=q_lo[:], in0=lin_all(1), scalar=gq, in1=f32(q_hi[:]),
                                              op0=ALU.mult, op1=ALU.subtract))
                acts("rk_s")
                done(dve.reciprocal(rk_r, rk_s))
                own("rk_r")
                done(dve.tensor_tensor(diag[:].rearrange("p (c t) -> p c t", t=P),
                                       ident[:].unsqueeze(1).to_broadcast([P, NCH, P]),
                                       rk_r.unsqueeze(2).to_broadcast([P, NCH, P]), ALU.mult))
                acts("v_hi")
                done(dve.tensor_tensor(v_lo[:], lin_all(0), f32(v_hi[:]), ALU.subtract))
                products("scale_k")
                done(dve.tensor_tensor(kf[:], kf[:], lin_all(1), ALU.mult))
                done(dve.tensor_tensor(rt3, krf[0:ROPE], lin_all(1)[0:ROPE], ALU.mult))
                turned(0)
                acts("k_hi")
                done(dve.tensor_tensor(k_lo[:], kf[:], f32(k_hi[:]), ALU.subtract))
                turned(1)
                turned(2)
                own("rt_2")
                done(dve.tensor_tensor(rt1, rt1, rt2, ALU.add))
                acts("qr2_up")
                done(dve.tensor_tensor(qr2[ROPE:P], rt1, f32(qr2[0:ROPE]), ALU.subtract))
                products("sum_q")
                done(dve.tensor_copy(rq_r, bank(7, NCH)))
                own("rq_sum")
                done(dve.tensor_tensor(rq_v, rq_r, bank(7)[:, NCH:2 * NCH], ALU.add))
                acts("rq_s")
                done(dve.reciprocal(rq_r, rq_s))
                own("rq_r")
                done(dve.tensor_scalar(rq, rq_r, SCALE, None, ALU.mult))
                own("rq")

                def keys(c):
                    return TP if c < NCH_P else TS

                def top(c):
                    n = keys(c)
                    dve.wait_ge(S["scores_pe"], at("scores_pe", NCH * h + (c + 1)))
                    dve.tensor_reduce(mx[:, c:c + 1], bank(s_bank(c), n), AX_X, ALU.max).then_inc(S["max_dve"], 1)
                    dve.wait_ge(S["max_dve"], at("max_dve", NCH * h + (c + 1)))
                    dve.tensor_scalar(nmx[:, c:c + 1], mx[:, c:c + 1], rq[:, c:c + 1], -1.0, ALU.mult,
                                      ALU.mult).then_inc(S["bias_dve"], 1)

                def inverse(c):
                    dve.wait_ge(S["exp_act"], at("exp_act", NCH * h + (c + 1)))
                    dve.reciprocal(prec[:, c:c + 1], psumr[:, c:c + 1]).then_inc(S["recip_dve"], 1)

                def norm(c):
                    n = keys(c)
                    dve.wait_ge(S["recip_dve"], at("recip_dve", NCH * h + (c + 1)))
                    dve.tensor_scalar(prob[:, c % 2, 0:n], prob[:, c % 2, 0:n], prec[:, c:c + 1], None,
                                      ALU.mult).then_inc(S["prob_dve"], 1)

                def low(c):
                    n = keys(c) // P
                    o = (c % NCH_P) % 4 * P
                    dve.wait_ge(S["pt_hi_act"], at("pt_hi_act", NCH * h + (c + 1)))
                    dve.tensor_tensor(pt_lo[:, 0:n, o:o + P], bank(t_bank(c), n * P).rearrange("p (k q) -> p k q", q=P),
                                      f32(pt_hi[:, 0:n, o:o + P]), ALU.subtract).then_inc(S["pt_lo_dve"], 1)

                for c in range(NCH + 2):
                    if c < NCH:
                        top(c)
                    if c > 1:
                        low(c - 2)
                    if c < NCH:
                        inverse(c)
                        if c % 2:
                            norm(c)

            split_lo(KD, o_all)
            def gate_b(i, j, g):
                dve.wait_ge(gt_in[j], 16 * i + (16 * KD // 2 + 16))
                for b, (t0, tn) in enumerate(BLOCKS):
                    dve.wait_ge(S["tile_pe"], 3 * g + (b + 1))
                    dve.tensor_tensor(gt[:, j, t0:t0 + tn], lin_set(j, b), gt[:, j, t0:t0 + tn],
                                      ALU.mult).then_inc(S["evac"], 1)
                dve.wait_ge(S["evac"], 3 * g + 3)
                z = z_all[:, 2 * i + j, :]
                dve.tensor_tensor(z, z, gt[:, j, :], ALU.add).then_inc(S["z_sum"], 1)
            dve.wait_ge(S["za_in0"], 16)
            for j in range(2):
                gate_b(0, j, G_B + j)
            dve.wait_ge(S["za_in1"], 16)
            with dve.Fori(1, KD // 2) as i:
                for j in range(2):
                    gate_b(i, j, 2 * i + (G_B + j))
            split_lo(2 * KD, z_all)
            dve.wait_ge(S["x2_in"], 32)

            def residual(q, c, acc):
                dve.wait_ge(S["out_pe"], q * NCH + (c + 1))
                x = x2[:, c, bass.ds(q * QN, QN)]
                dve.tensor_tensor(x, bank(acc)[:, 0:QN], x, ALU.add).then_inc(S["x2_dve"], 1)
            for c in range(NCH):
                residual(0, c, c if c < 8 else 4 + c % 2)
            with dve.Fori(1, QS - 1) as q:
                for c in range(NCH):
                    residual(q, c, 4 + c % 2)
            dve.wait_ge(S["r_in"], 32)
            dve.wait_ge(S["w_split"], G_OUT + 2 * QS)
            for n in range(NCH):
                residual(QS - 1, n, 4 + n % 2)
                dve.wait_ge(S["r_std"], n + 1)
                dve.reciprocal(rstd2[:, n:n + 1], std2[:, n:n + 1]).then_inc(S["r_rec"], 1)
                dve.wait_ge(S["r_rec"], n + 1)
                if n > 1:
                    dve.wait_ge(S["hT_pe"], n - 1)
                    dve.wait_ge(S[f"h_out{n % 2}"], 16 * (n // 2))
                dve.scalar_tensor_tensor(out=h2[:, n % 2].rearrange("p k t -> p (k t)"), in0=x2[:, n, :],
                                         scalar=rstd2[:, n:n + 1], in1=g2b[:], op0=ALU.mult,
                                         op1=ALU.mult).then_inc(S["h_dve"], 1)

            def rstep(i_, n):
                i_.then_inc(S["r_dve"], 1)
                dve.wait_ge(S["r_dve"], n)
            dve.wait_ge(S["logits_pe"], NCH)
            logit = bank(6, NCH * E).rearrange("p (c e) -> p c e", e=E)
            rstep(dve.tensor_reduce(lmx, logit, AX_X, ALU.max), 1)
            rstep(dve.tensor_tensor(lg[:], logit, lmx.unsqueeze(2).to_broadcast([P, NCH, E]), ALU.subtract), 2)
            dve.wait_ge(S["r_exp"], 1)
            rstep(dve.tensor_reduce(lsum, aff[:], AX_X, ALU.add), 3)
            rstep(dve.reciprocal(lrec, lsum), 4)
            rstep(dve.memset(lists[:], -1.0), 5)
            for n, (first, chunks, c0) in enumerate(((L_A, HALF // P, 0), (L_B, HALF // P, HALF // P), (L_S, TS // P, NCH_P))):
                c1 = c0 + chunks
                rstep(dve.tensor_tensor(lists[:, 0:chunks, first:first + E], aff[:, c0:c1],
                                        lrec[:, c0:c1].unsqueeze(2).to_broadcast([P, chunks, E]), ALU.mult), 6 + n)

            dve.wait_ge(S["affT_act"], 1)
            count = [0]

            def kstep(i_):
                count[0] += 1
                i_.then_inc(S["topk_dve"], 1)
                dve.wait_ge(S["topk_dve"], count[0])
            for r in range(CAP_P // 8):
                v, x = topv[:, 8 * r:8 * r + 8], topi[:, 8 * r:8 * r + 8]
                kstep(dve.max(v, work[:]))
                kstep(dve.max_index(x, v, work[:]))
                if r < CAP_P // 8 - 1:
                    kstep(dve.match_replace(work[:], v, work[:], -1.0))
            for top in (topv[L_S:LISTS], topi[L_S:LISTS]):
                kstep(dve.tensor_copy(top[:, CAP_S:P].rearrange("e (g c) -> e g c", c=CAP_S),
                                      top[:, 0:CAP_S].unsqueeze(1).to_broadcast([E, GRP - 1, CAP_S])))
            kstep(dve.tensor_copy(topf[:], topi[:]))

            def chosen_step(i_, n):
                i_.then_inc(S["rows_dve"], 1)
                dve.wait_ge(S["rows_dve"], n)
            dve.wait_ge(S["chosen_pe"], 2)
            chosen_step(dve.tensor_copy(chosen[:], bank(3, 2 * LISTS).rearrange("p (v l) -> p v l", l=LISTS)), 1)
            dve.wait_ge(S["chosen_pe"], 4)
            va, ia = chosen[:, 0, L_A:L_A + E], chosen[:, 1, L_A:L_A + E]
            vb, ib = bank(2, E), bank(2)[:, E:2 * E]
            chosen_step(dve.tensor_tensor(gates[:, 0], va, vb, ALU.max), 2)
            chosen_step(dve.tensor_tensor(pick[:, 0], va, vb, ALU.is_ge), 3)
            chosen_step(dve.tensor_scalar(pick[:, 1], ib, float(HALF), None, ALU.add), 4)
            chosen_step(dve.tensor_tensor(pick[:, 2], ia, pick[:, 1], ALU.subtract), 5)
            chosen_step(dve.tensor_tensor(pick[:, 2], pick[:, 2], pick[:, 0], ALU.mult), 6)
            chosen_step(dve.tensor_tensor(pick[:, 1], pick[:, 1], pick[:, 2], ALU.add), 7)
            chosen_step(dve.tensor_copy(rows[:, 0], pick[:, 1]), 8)
            chosen_step(dve.tensor_copy(gates[:, 1], chosen[:, 0, L_S:LISTS]), 9)
            chosen_step(dve.tensor_copy(rows[:, 1], chosen[:, 1, L_S:LISTS]), 10)
            chosen_step(dve.tensor_scalar(rows[:, 2], chosen[:, 1, L_S:LISTS], float(TP), None, ALU.add), ROWS_STEPS)
            dve.wait_ge(S["y_out"], 32)

            def frame(e):
                is0, is1, is_last = (isinstance(e, int) and e == v for v in (0, 1, E))
                more = not (isinstance(e, int) and e >= E - 1)
                for n, (kind, ee, kk, q, slot) in enumerate(pieces(e)):
                    l = n + (8 if is_last else 0)
                    if is_last and n == 0:
                        out(e - 2)
                        hidden(e - 1)
                    dve.wait_ge(S["e_hi"], q + 1)
                    pt = part(l, is0) if not is_last else q % 3
                    dve.tensor_tensor(elo[:, pt], raw[:, slot], f32(ehi[:, pt]), ALU.subtract).then_inc(S["e_lo"], 1)
                    if is0 and n == 2:
                        rows_lo(0)
                    if l == 1 and not (is0 or is1):
                        out(e - 2)
                    if l == 2 and not is0:
                        hidden(e - 1)
                    if l == (7 if is0 else 9) and not is_last:
                        gated(e)
                    if more and l == (7 if is0 else 10):
                        rows_lo(e + 1)
                if is_last:
                    out(e - 1)

            def gated(e):
                dve.wait_ge(S["e_pe"], 8 if isinstance(e, int) and e == 0 else 12 * e + 4)
                dve.wait_ge(S["silu_p"], e + 1)
                dve.wait_ge(S["silu_s"], e + 1)
                dve.tensor_tensor(hid[:], bank(2, D), hid[:], ALU.mult).then_inc(S["mul_p"], 1)
                dve.tensor_tensor(hid_s[:], bank(7, GN), hid_s[:], ALU.mult).then_inc(S["mul_s"], 1)

            def rows_lo(e):
                dve.wait_ge(S["xh_act"], e + 1)
                dve.tensor_tensor(xT_lo[:], bank(0, D).rearrange("p (k t) -> p k t", k=KD), f32(xT_hi[:]),
                                  ALU.subtract).then_inc(S["xl_dve"], 1)
                dve.wait_ge(S["txs_pe"], e + 1)
                dve.tensor_copy(xT_s[:], bank(7, GN).rearrange("p (k t) -> p k t", k=KD)).then_inc(S["xs_dve"], 1)

            def hidden(e):
                dve.wait_ge(S["hh_act"], e + 1)
                dve.tensor_tensor(hT_lo[:], bank(2, D).rearrange("p (k t) -> p k t", k=KD), f32(hT_hi[:]),
                                  ALU.subtract).then_inc(S["hl_dve"], 1)
                dve.wait_ge(S["ths_pe"], e + 1)
                dve.tensor_copy(hT_s[:], bank(7, GN)).then_inc(S["hs_dve"], 1)

            def out(e):
                dve.wait_ge(S["e_pe"], 12 * E if isinstance(e, int) and e == E - 1 else 12 * e + 20)
                if not (isinstance(e, int) and e == 0):
                    dve.wait_ge(S["scattered"], 32 * e)
                for g in range(GRP):
                    r = slice(CAP_S * g, CAP_S * (g + 1))
                    last = dve.tensor_scalar(ob_s[:, g * GN:(g + 1) * GN], bank(6, GN)[r], gates[r, 1, bass.ds(e, 1)],
                                             None, ALU.mult)
                last.then_inc(S["ob_dve"], 1)

            run_frames(dve, frame)


_INS = ['x_prompt', 'x_sample', 'norm1_g', 'w_in', 'v_norm_g', 'w_spatial', 'b_spatial', 'w_a_out',
        'q_norm_g', 'w_uq', 'kv_norm_g', 'w_ukv', 'q_head_g', 'k_head_g', 'w_b_out', 'w_out',
        'norm2_g', 'w_router', 'w_gate', 'w_up', 'w_down']


def rope_table():
    import numpy as np
    half = ROPE // 2
    freq = (np.float32(10000.0) ** (-np.arange(half, dtype=np.float32) / np.float32(half))).astype(np.float32)
    pos = np.concatenate([np.arange(TP), np.arange(TS)]).astype(np.float32)
    ang = (freq[:, None] * pos[None, :]).astype(np.float32).astype(np.float64)
    c, s = np.cos(ang), np.sin(ang)
    return np.ascontiguousarray(np.concatenate([c, c, -s, s]).astype(np.float32))


def kernel(**inputs):
    import numpy as np
    import concourse.bacc as bacc
    from concourse.bass_utils import run_bass_kernel_spmd

    nc = bacc.Bacc("TRN2", target_bir_lowering=False, num_devices=1)
    arrays, args = {}, []
    for name in _INS:
        a = np.ascontiguousarray(inputs[name])
        a = a.reshape(a.shape[1:])
        arrays[f"in_{name}"] = a
    arrays["rope_cs"] = rope_table()
    for name, a in arrays.items():
        args.append(nc.dram_tensor(name, a.shape, mybir.dt.from_np(a.dtype), kind="ExternalInput").ap())
    args.append(nc.dram_tensor("y_p", (TP, D), F32, kind="ExternalOutput").ap())
    args.append(nc.dram_tensor("y_s", (TS, D), F32, kind="ExternalOutput").ap())
    build(nc, *args)
    r = run_bass_kernel_spmd(nc, [arrays], core_ids=[0])
    return (r.results[0]["y_p"].reshape(1, TP, D), r.results[0]["y_s"].reshape(1, TS, D))
```
